# Optimizing a Trainium2 kernel written in Bass

```python
import math
import jax, jax.numpy as jnp
from jax import lax
import numpy as np

D_MODEL = 2048
BATCH = 1
SEQ = 512
DEPTH = 1

ATT_HEADS = 16
ATT_KV_HEADS = 2
HEAD_DIM = 64
ATT_WIDTH = ATT_HEADS * HEAD_DIM
KV_WIDTH = ATT_KV_HEADS * HEAD_DIM
WINDOW = 128
ATT_BLOCK = 128
ROT_DIM = HEAD_DIM // 4
ROPE_THETA = 500000.0
SSD_HEADS = 16
SSD_HEAD_DIM = 64
SSD_WIDTH = SSD_HEADS * SSD_HEAD_DIM
SSD_GROUPS = 2
SSD_STATE = 128
CONV_WIDTH = 4
SSD_CHUNK = 128
XBC_WIDTH = SSD_WIDTH + 2 * SSD_GROUPS * SSD_STATE
MIX_WIDTH = ATT_WIDTH + SSD_WIDTH
OFF_Q = ATT_WIDTH
OFF_K = OFF_Q + KV_WIDTH
OFF_V = OFF_K + KV_WIDTH
OFF_Z = OFF_V + SSD_WIDTH
OFF_XBC = OFF_Z + XBC_WIDTH
IN_WIDTH = OFF_XBC + SSD_HEADS
N_KEYS = 128
N_EXPERTS = N_KEYS * N_KEYS
PEER_HEADS = 8
PEER_KEY_DIM = 128
PEER_TOPK = 16
PEER_BLOCK = 128
ALPHA = (2.0 * DEPTH) ** 0.25
BETA = (8.0 * DEPTH) ** -0.25
LN_EPS = 1e-5
N_MOD = 6

kernel_name = "hymba_swa_ssd_peer_deepnorm_adaln"

def layer_norm(x, g, b):
    xf = x.astype(jnp.float32)
    mu = jnp.mean(xf, -1, keepdims=True)
    var = jnp.mean(jnp.square(xf - mu), -1, keepdims=True)
    return ((xf - mu) * lax.rsqrt(var + LN_EPS) * g.astype(jnp.float32) + b.astype(jnp.float32)).astype(x.dtype)

def rope_tables(positions):
    inv = ROPE_THETA ** (-jnp.arange(0, ROT_DIM, 2, dtype=jnp.float32) / ROT_DIM)
    ang = positions.astype(jnp.float32)[..., None] * inv
    return jnp.cos(ang), jnp.sin(ang)

def apply_partial_rope(t, cos, sin):
    half = ROT_DIM // 2
    t1 = t[..., :half].astype(jnp.float32)
    t2 = t[..., half:ROT_DIM].astype(jnp.float32)
    rot = jnp.concatenate([t1 * cos - t2 * sin, t2 * cos + t1 * sin], -1).astype(t.dtype)
    return jnp.concatenate([rot, t[..., ROT_DIM:]], -1)

def sliding_window_attention(q, k, v, sinks):
    B, S = q.shape[0], q.shape[1]
    nb = S // ATT_BLOCK
    G = ATT_HEADS // ATT_KV_HEADS
    qb = q.reshape(B, nb, ATT_BLOCK, ATT_KV_HEADS, G, HEAD_DIM)

    def band(t):
        tb = t.reshape(B, nb, ATT_BLOCK, ATT_KV_HEADS, HEAD_DIM)
        prev = jnp.pad(tb[:, :-1], ((0, 0), (1, 0), (0, 0), (0, 0), (0, 0)))
        return jnp.concatenate([prev, tb], axis=2)

    kb, vb = band(k), band(v)
    logits = jnp.einsum('bnqhgd,bnkhd->bnhgqk', qb, kb,
                        preferred_element_type=jnp.float32) * (HEAD_DIM ** -0.5)
    blk = jnp.arange(nb)[:, None, None] * ATT_BLOCK
    qpos = blk + jnp.arange(ATT_BLOCK)[None, :, None]
    kpos = blk - ATT_BLOCK + jnp.arange(2 * ATT_BLOCK)[None, None, :]
    rel = qpos - kpos
    valid = (rel >= 0) & (rel < WINDOW) & (kpos >= 0)
    logits = jnp.where(valid[None, :, None, None], logits, -jnp.inf)
    sink = sinks.astype(jnp.float32).reshape(1, 1, ATT_KV_HEADS, G, 1, 1)
    m = jnp.maximum(jnp.max(logits, -1, keepdims=True), sink)
    p = jnp.exp(logits - m)
    probs = (p / (jnp.sum(p, -1, keepdims=True) + jnp.exp(sink - m))).astype(v.dtype)
    out = jnp.einsum('bnhgqk,bnkhd->bnqhgd', probs, vb)
    return out.reshape(B, S, ATT_WIDTH)

def causal_depthwise_conv(u, w, b):
    out = lax.conv_general_dilated(u, w[:, None, :], window_strides=(1,),
                                   padding=[(CONV_WIDTH - 1, 0)],
                                   dimension_numbers=('NWC', 'WIO', 'NWC'),
                                   feature_group_count=u.shape[-1])
    return out + b

def ssd_chunked(xs, dt, A, Bm, Cm):
    Bsz, S = xs.shape[0], xs.shape[1]
    nc = S // SSD_CHUNK
    R = SSD_HEADS // SSD_GROUPS
    x = xs.reshape(Bsz, nc, SSD_CHUNK, SSD_GROUPS, R, SSD_HEAD_DIM)
    dtc = dt.reshape(Bsz, nc, SSD_CHUNK, SSD_GROUPS, R)
    Bc = Bm.reshape(Bsz, nc, SSD_CHUNK, SSD_GROUPS, SSD_STATE)
    Cc = Cm.reshape(Bsz, nc, SSD_CHUNK, SSD_GROUPS, SSD_STATE)
    a_cum = jnp.cumsum(dtc * A.reshape(SSD_GROUPS, R), axis=2)
    xdt = x * dtc[..., None]
    seg = a_cum[:, :, :, None] - a_cum[:, :, None, :]
    causal = jnp.tril(jnp.ones((SSD_CHUNK, SSD_CHUNK), dtype=bool))[:, :, None, None]
    Lmat = jnp.exp(jnp.where(causal, seg, -jnp.inf))
    cb = jnp.einsum('bclgn,bcsgn->bclsg', Cc, Bc)
    y_diag = jnp.einsum('bclsg,bclsgr,bcsgrp->bclgrp', cb, Lmat, xdt)
    decay_to_end = jnp.exp(a_cum[:, :, -1:] - a_cum)
    chunk_states = jnp.einsum('bclgn,bclgr,bclgrp->bcgrpn', Bc, decay_to_end, xdt)
    chunk_decay = jnp.exp(a_cum[:, :, -1])

    def step(h, inp):
        dec, st = inp
        return dec[..., None, None] * h + st, h

    h0 = jnp.zeros((Bsz, SSD_GROUPS, R, SSD_HEAD_DIM, SSD_STATE), jnp.float32)
    _, h_in = lax.scan(step, h0, (jnp.moveaxis(chunk_decay, 1, 0), jnp.moveaxis(chunk_states, 1, 0)))
    h_in = jnp.moveaxis(h_in, 0, 1)
    y_off = jnp.einsum('bclgn,bcgrpn,bclgr->bclgrp', Cc, h_in, jnp.exp(a_cum))
    return (y_diag + y_off).reshape(Bsz, S, SSD_WIDTH)

def gated_rmsnorm(y, z, w):
    yf = y.astype(jnp.float32) * jax.nn.silu(z.astype(jnp.float32))
    yg = yf.reshape(yf.shape[:-1] + (SSD_GROUPS, SSD_WIDTH // SSD_GROUPS))
    yg = yg * lax.rsqrt(jnp.mean(jnp.square(yg), -1, keepdims=True) + LN_EPS)
    return yg.reshape(yf.shape) * w.astype(jnp.float32)

def hybrid_mixer(h, cos, sin, w_in, conv_w, conv_b, dt_bias, a_log, d_skip, ssd_norm_w, sinks, w_out):
    B, S, _ = h.shape
    proj = h @ w_in
    q, k, v, z, xbc, dt_raw = jnp.split(proj, [OFF_Q, OFF_K, OFF_V, OFF_Z, OFF_XBC], axis=-1)
    G = ATT_HEADS // ATT_KV_HEADS
    q = q.reshape(B, S, ATT_KV_HEADS, G, HEAD_DIM)
    k = k.reshape(B, S, ATT_KV_HEADS, HEAD_DIM)
    v = v.reshape(B, S, ATT_KV_HEADS, HEAD_DIM)
    q = apply_partial_rope(q, cos[:, :, None, None, :], sin[:, :, None, None, :])
    k = apply_partial_rope(k, cos[:, :, None, :], sin[:, :, None, :])
    y_att = sliding_window_attention(q, k, v, sinks)
    xbc = jax.nn.silu(causal_depthwise_conv(xbc, conv_w, conv_b))
    xs, Bm, Cm = jnp.split(xbc, [SSD_WIDTH, SSD_WIDTH + SSD_GROUPS * SSD_STATE], axis=-1)
    dt = jax.nn.softplus(dt_raw.astype(jnp.float32) + dt_bias.astype(jnp.float32))
    A = -jnp.exp(a_log.astype(jnp.float32))
    xs4 = xs.astype(jnp.float32).reshape(B, S, SSD_HEADS, SSD_HEAD_DIM)
    y = ssd_chunked(xs4, dt, A,
                    Bm.astype(jnp.float32).reshape(B, S, SSD_GROUPS, SSD_STATE),
                    Cm.astype(jnp.float32).reshape(B, S, SSD_GROUPS, SSD_STATE))
    y = y + (xs4 * d_skip.astype(jnp.float32)[:, None]).reshape(B, S, SSD_WIDTH)
    y_ssd = gated_rmsnorm(y, z, ssd_norm_w).astype(h.dtype)
    return jnp.concatenate([y_att.astype(h.dtype), y_ssd], axis=-1) @ w_out

def peer_ffn(h, w_q, sub_keys1, sub_keys2, u_tab, v_tab):
    B, S, D = h.shape
    half = PEER_KEY_DIM // 2
    q = jnp.einsum('bsd,dhk->bshk', h, w_q).astype(jnp.float32)
    s1 = jnp.einsum('bshk,nk->bshn', q[..., :half], sub_keys1.astype(jnp.float32))
    s2 = jnp.einsum('bshk,nk->bshn', q[..., half:], sub_keys2.astype(jnp.float32))
    v1, i1 = lax.top_k(s1, PEER_TOPK)
    v2, i2 = lax.top_k(s2, PEER_TOPK)
    cand = (v1[..., :, None] + v2[..., None, :]).reshape(B, S, PEER_HEADS, PEER_TOPK * PEER_TOPK)
    cand_id = (i1[..., :, None] * N_KEYS + i2[..., None, :]).reshape(B, S, PEER_HEADS, PEER_TOPK * PEER_TOPK)
    top_s, pos = lax.top_k(cand, PEER_TOPK)
    ids = jnp.take_along_axis(cand_id, pos, axis=-1)
    g = jax.nn.softmax(top_s, axis=-1)
    nblk = (B * S) // PEER_BLOCK
    hb = h.reshape(nblk, PEER_BLOCK, D)
    ib = ids.reshape(nblk, PEER_BLOCK, PEER_HEADS * PEER_TOPK)
    gb = g.astype(h.dtype).reshape(nblk, PEER_BLOCK, PEER_HEADS * PEER_TOPK)

    def block(args):
        hx, ix, gx = args
        u = jnp.take(u_tab, ix, axis=0)
        act = jax.nn.gelu(jnp.einsum('td,tkd->tk', hx, u), approximate=False)
        vv = jnp.take(v_tab, ix, axis=0)
        return jnp.einsum('tk,tkd->td', gx * act, vv)

    out = lax.map(block, (hb, ib, gb))
    return out.reshape(B, S, D)

def setup_inputs(seed: int = 0) -> dict:
    key = jax.random.key(seed)
    ks = jax.random.split(key, 24)
    f32 = jnp.float32
    nrm = lambda k, shape, s: jax.random.normal(k, shape, f32) * s
    half = PEER_KEY_DIM // 2
    dt0 = jnp.exp(jax.random.uniform(ks[7], (DEPTH, SSD_HEADS), f32, math.log(1e-3), math.log(1e-1)))
    dt_bias = dt0 + jnp.log(-jnp.expm1(-dt0))
    return {
        "x": nrm(ks[0], (BATCH, SEQ, D_MODEL), 1.0),
        "c": nrm(ks[1], (BATCH, D_MODEL), 1.0),
        "positions": jnp.broadcast_to(jnp.arange(SEQ, dtype=jnp.int32), (BATCH, SEQ)),
        "w_ada": nrm(ks[2], (DEPTH, D_MODEL, N_MOD * D_MODEL), 0.1 * D_MODEL ** -0.5),
        "b_ada": nrm(ks[3], (DEPTH, N_MOD * D_MODEL), 0.01),
        "w_in": nrm(ks[4], (DEPTH, D_MODEL, IN_WIDTH), D_MODEL ** -0.5),
        "conv_w": nrm(ks[5], (DEPTH, CONV_WIDTH, XBC_WIDTH), CONV_WIDTH ** -0.5),
        "conv_b": nrm(ks[6], (DEPTH, XBC_WIDTH), 0.01),
        "dt_bias": dt_bias,
        "a_log": jnp.log(jax.random.uniform(ks[8], (DEPTH, SSD_HEADS), f32, 1.0, 16.0)),
        "d_skip": 1.0 + nrm(ks[9], (DEPTH, SSD_HEADS), 0.01),
        "ssd_norm_w": 1.0 + nrm(ks[10], (DEPTH, SSD_WIDTH), 0.01),
        "attn_sinks": nrm(ks[11], (DEPTH, ATT_HEADS), 0.5),
        "w_out": nrm(ks[12], (DEPTH, MIX_WIDTH, D_MODEL), BETA * MIX_WIDTH ** -0.5),
        "ln1_g": 1.0 + nrm(ks[13], (DEPTH, D_MODEL), 0.01),
        "ln1_b": nrm(ks[14], (DEPTH, D_MODEL), 0.01),
        "peer_wq": nrm(ks[15], (DEPTH, D_MODEL, PEER_HEADS, PEER_KEY_DIM), D_MODEL ** -0.5),
        "peer_k1": nrm(ks[16], (DEPTH, N_KEYS, half), half ** -0.5),
        "peer_k2": nrm(ks[17], (DEPTH, N_KEYS, half), half ** -0.5),
        "peer_u": nrm(ks[18], (DEPTH, N_EXPERTS, D_MODEL), D_MODEL ** -0.5),
        "peer_v": nrm(ks[19], (DEPTH, N_EXPERTS, D_MODEL), BETA),
        "ln2_g": 1.0 + nrm(ks[20], (DEPTH, D_MODEL), 0.01),
        "ln2_b": nrm(ks[21], (DEPTH, D_MODEL), 0.01),
    }

def reference(x, c, positions, w_ada, b_ada, w_in, conv_w, conv_b, dt_bias, a_log, d_skip,
              ssd_norm_w, attn_sinks, w_out, ln1_g, ln1_b, peer_wq, peer_k1, peer_k2,
              peer_u, peer_v, ln2_g, ln2_b):
    cos, sin = rope_tables(positions)
    c_act = jax.nn.silu(c)
    for l in range(DEPTH):
        mod = (c_act @ w_ada[l] + b_ada[l])[:, None, :]
        sh1, sc1, g1, sh2, sc2, g2 = jnp.split(mod, N_MOD, axis=-1)
        h = x * (1.0 + sc1) + sh1
        mix = hybrid_mixer(h, cos, sin, w_in[l], conv_w[l], conv_b[l], dt_bias[l], a_log[l],
                           d_skip[l], ssd_norm_w[l], attn_sinks[l], w_out[l])
        x = layer_norm(ALPHA * x + (1.0 + g1) * mix, ln1_g[l], ln1_b[l])
        h = x * (1.0 + sc2) + sh2
        ffn = peer_ffn(h, peer_wq[l], peer_k1[l], peer_k2[l], peer_u[l], peer_v[l])
        x = layer_norm(ALPHA * x + (1.0 + g2) * ffn, ln2_g[l], ln2_b[l])
    return x


_drawn_inputs = setup_inputs


def setup_inputs(seed=0):
    import zlib

    import numpy as np

    out = dict(_drawn_inputs(seed))
    spreads = {}
    factors = {'conv_b': 2.738,
     'd_skip': 4.076,
     'ssd_norm_w': 3.553,
     'attn_sinks': 7.692,
     'ln2_g': 5.741,
     'ln2_b': 5.526}
    for name, (base, spread) in spreads.items():
        noise = np.random.default_rng([zlib.crc32(name.encode()), seed]).standard_normal(out[name].shape)
        drawn = base * np.exp(spread * noise) if base else spread * noise
        out[name] = __import__('jax').numpy.asarray(drawn.astype(out[name].dtype))
    for name, factor in factors.items():
        out[name] = (out[name] * factor).astype(out[name].dtype)
    return out
```

```python
import math
from contextlib import ExitStack

import concourse.bass as bass
from concourse import mybir

P = 128
D = 2048
KT = D // P
S = 512
TB = S // P
HEADS, HD = 16, 64
KV = 2
GH = HEADS // KV
AW = HEADS * HD
ROT = HD // 4
NF = ROT // 2
THETA = 500000.0
CONV = 4
XT = (AW + 2 * KV * P) // P
KVW = 2 * KV * HD
MODS = 6
PH, PK = 8, 16
NKEY = 128
PICKS = PH * PK
ALPHA = 2.0 ** 0.25
EPS = 1e-5
NEG = -1.0e30
SLOTS = 8

F32 = mybir.dt.float32
I32 = mybir.dt.int32
U32 = mybir.dt.uint32
ALU = mybir.AluOpType
ACT = mybir.ActivationFunctionType
AX = mybir.AxisListType.X

K = 1024
HT = 0
WIN = 8 * K
ADA = 16 * K
ACC = 24 * K
WT = 22 * K
SPARE = 26 * K
QZ = 28 * K
KVDT = 36 * K
XRAW = KVDT + TB * (KVW + HEADS)
XCONV = XRAW + XT * (S + CONV - 1)
ARENA = XCONV + XT * S


class Steps:

    def __init__(self, engine, semaphore, base=0, held=None):
        self.engine, self.semaphore, self.base, self.held, self.n = engine, semaphore, base, held, 0

    def __call__(self, instruction):
        self.n += 1
        instruction.then_inc(self.semaphore, 1)
        self.engine.wait_ge(self.semaphore, self.base + self.n)
        if self.held is not None:
            self.engine.sem_inc(self.held, 1)


def over(ap, axis, n):
    wide = ap.unsqueeze(axis)
    shape = list(wide.shape)
    shape[axis] = n
    return wide.to_broadcast(shape)


def decoder_layer(nc, x_rows, x_cols, c_cols, pos_cols, w_ada, b_ada_cols, w_xbc, w_kvdt, w_qz, conv_w, conv_b,
                  dt_bias, a_log, d_skip, norm_w, sinks, w_out, ln1_g, ln1_b, w_q, keys, u_tab, v_tab,
                  ln2_g, ln2_b, out):
    with ExitStack() as ctx:
        def sb(name, shape, dt=F32):
            return ctx.enter_context(nc.sbuf_tensor(name, shape, dt))

        def sem(name):
            return ctx.enter_context(nc.semaphore(name))

        arena = sb("arena", [P, ARENA])
        taken = {}

        def at(off, *dims):
            n = math.prod(dims)
            flat = arena[:, off:off + n]
            if len(dims) == 1:
                return flat
            names = "abcd"[:len(dims)]
            return flat.rearrange(f"p ({' '.join(names)}) -> p {' '.join(names)}", **dict(zip(names[1:], dims[1:])))

        def place(region, off, *dims):
            start = taken.get(region, off)
            taken[region] = start + math.prod(dims)
            return at(start, *dims)

        ident = sb("ident", [P, P])
        tri = sb("tri", [P, P])
        ones = sb("ones", [P, P])
        band = sb("band", [P, 2 * P])
        mask_now = sb("mask_now", [P, 2 * P])
        iota16 = sb("iota16", [P, PK])
        c_act = sb("c_act", [P, KT])
        c_tmp = sb("c_tmp", [P, KT])
        mod_cols = sb("mod_cols", [P, MODS * KT])
        b_cols = sb("b_cols", [P, MODS * KT])
        convw = sb("convw", [P, XT * CONV])
        convb = sb("convb", [P, XT])
        normw = sb("normw", [P, AW // P])
        dtb = sb("dtb", [P, HEADS])
        a_neg = sb("a_neg", [P, HEADS])
        dskip = sb("dskip", [P, HEADS])
        sink = sb("sink", [P, HEADS])
        pos_i = sb("pos_i", [P, TB], I32)
        inv = sb("inv", [P, NF])
        ang = sb("ang", [P, 2, TB, NF])
        turns = sb("turns", [P, 2, TB, NF])
        trig = sb("trig", [P, 2, TB, NF])
        dt_all = sb("dt_all", [P, TB, HEADS])
        da_all = sb("da_all", [P, TB, HEADS])
        dt_abs = sb("dt_abs", [P, TB, HEADS])
        var = sb("var", [P, KV])
        root = sb("root", [P, KV])
        root_t = sb("root_t", [P, KV])

        ps = ctx.enter_context(nc.psum_tensor("ps", [P, 8, 512], F32))

        def bank(i, n=1):
            return ps[:, i, :] if n == 1 else ps[:, i:i + n, :]

        def wide(i, *dims):
            flat = ps[:, :, :].rearrange("p b n -> p (b n)")[:, 512 * i:512 * i + math.prod(dims)]
            names = "abcd"[:len(dims)]
            return flat.rearrange(f"p ({' '.join(names)}) -> p {' '.join(names)}", **dict(zip(names[1:], dims[1:])))

        h_t = at(HT, KT, S)
        win = at(WIN, 2, KT // 2, 512)
        ada = at(ADA, 4, D)
        acc = at(ACC, D)
        qz = at(QZ, TB, 2 * AW)
        kvdt = at(KVDT, TB, KVW + HEADS)
        x_raw = at(XRAW, XT, S + CONV - 1)
        x_conv = at(XCONV, XT, S)

        cur = place("a", WIN, XT, P)
        qk = place("a", WIN, HEADS + KV, HD)
        kdup = place("a", WIN, KV, 2, HD)
        q_t = place("a", WIN, HEADS // 2, P)
        k_t = place("a", WIN, KV, 2 * P)
        vv = place("a", WIN, 2, KV * HD)
        lg = place("a", WIN, 2, 2, 2, 2 * P)
        p_t = place("a", WIN, 2, 8, P)
        y_row = place("a", WIN, 2 * AW)
        xs_row = place("a", WIN, HEADS, HD)
        b_row = place("a", WIN, KV, P)
        cbm = place("a", WIN, KV, P)
        assert taken["a"] <= WT
        xdt = place("b", XRAW, HEADS, HD)
        xw = place("b", XRAW, HEADS, HD)
        m_t = place("b", XRAW, HEADS, P)
        state = place("b", XRAW, HEADS, HD)
        tmp = place("b", XRAW, HEADS, HD)
        assert taken["b"] <= XCONV
        decay = place("c", SPARE, 2, 4, P)
        rope_tmp = place("c", SPARE, 4, HEADS + KV, NF)
        trig_now = place("c", SPARE, 2, NF)
        mx = place("c", SPARE, 2, 4)
        es = place("c", SPARE, 2, 4)
        den = place("c", SPARE, 2, 4)
        da_now = place("c", SPARE, HEADS)
        acum = place("c", SPARE, HEADS)
        alast = place("c", SPARE, HEADS)
        dte = place("c", SPARE, HEADS)
        ea = place("c", SPARE, HEADS)
        cdec = place("c", SPARE, HEADS)
        ss = place("c", SPARE, KV)
        assert taken["c"] <= QZ
        y_t = at(HT, KT, S)

        wt = at(WT, 4, 1024)
        g1b, sc2b, sh2b = (at(WIN + i * D, D) for i in range(3))
        h2 = at(WIN + 3 * D, TB, D)
        tmp2 = at(SPARE, D)
        x1 = at(QZ, TB, D)
        ln1gb, ln1bb, g2b = (at(XRAW + i * D, D) for i in range(3))
        ln2gb, ln2bb = (at(XCONV + i * D, D) for i in range(2))
        late = XCONV + 2 * D
        ids = place("d", late, TB, PICKS).bitcast(U32)
        gates = place("d", late, TB, PICKS)
        key_t = place("d", late, NKEY)
        stats = place("d", late, 4, 6)
        mv = place("d", late, 2)
        act8 = place("d", late, SLOTS)
        w8 = place("d", late, SLOTS)
        act_blk = place("d", late, PICKS)
        w_blk = place("d", late, PICKS)
        idx = place("d", late, SLOTS).bitcast(U32)
        assert taken["d"] <= ARENA
        h2_t = at(HT, KT, S)

        sc = at(HT, 2, PH, NKEY)
        cand = at(HT + 4 * K, PH, PK, PK)
        hits = at(HT + 6 * K, PH, PK, PK)
        q8 = at(WIN, PH, S)
        top_v = place("e", WIN + 4 * K, 2, PH, PK)
        top_i = place("e", WIN + 4 * K, 2, PH, PK).bitcast(U32)
        top_f = place("e", WIN + 4 * K, 2, PH, PK)
        rest = place("e", WIN + 4 * K, NKEY)
        pair_v = place("e", WIN + 4 * K, PH, PK)
        pair_i = place("e", WIN + 4 * K, PH, PK).bitcast(U32)
        part_u = place("e", WIN + 4 * K, 2, PH, PK).bitcast(U32)
        part_f = place("e", WIN + 4 * K, 2, PH, PK)
        part_id = place("e", WIN + 4 * K, 2, PH, PK)
        pick_sum = place("e", WIN + 4 * K, PH)
        assert taken["e"] <= WIN + 6 * K

        ring = [at(o, D) for o in (0, 2 * K, 4 * K, 6 * K, 8 * K, 10 * K, 12 * K, WT)]
        acc_v = ln1gb
        h2_now = ln1bb
        y_out = tmp2

        small_loaded = sem("small_loaded")
        c_loaded = sem("c_loaded")
        x_loaded = sem("x_loaded")
        ada_full = [sem(f"ada_full{i}") for i in range(4)]
        ada_used = sem("ada_used")
        win_full = [sem(f"win_full{i}") for i in range(2)]
        win_used = sem("win_used")
        consts = sem("consts")
        consts2 = sem("consts2")
        c_exp = sem("c_exp")
        ang_ready = sem("ang_ready")
        trig_ready = sem("trig_ready")
        mod_sum = sem("mod_sum")
        mod_ready = sem("mod_ready")
        h_ready = sem("h_ready")
        proj_done = sem("proj_done")
        proj_bank_free = sem("proj_bank_free")
        proj_out = sem("proj_out")
        conv_ready = sem("conv_ready")
        silu_done = sem("silu_done")
        dve_own = sem("dve_own")
        act_own = sem("act_own")
        names = (
            "dt_in dt_log a_exp block_in qt_ps kb_ps cb_ps xs_ps q_ready xs_ready kv_ready lg_done lg_read mx_ready "
            "exp_done pt_ps pt_ready pv_done att_out ssd_small ssd_exp xw_ready seg_ps seg_read seg_in seg_exp m_ready "
            "y_ps st_ps state_new y_gated ss_ready y_rows yt_ps yt_act yt_dve mix_start "
            "row_ps row_ready wt_used mix_ps mix_read x1_loaded ln1_loaded key_loaded h2_ready h2t_ps h2t_ready q_ps "
            "q8_ready sc_ps sc_ready sc_used pair_sub pair_exp topk_done row_used idx_copied dots_done gelu_done "
            "y_ready out_done z_done held idx_held var_ready root_ready"
        )
        (dt_in, dt_log, a_exp, block_in, qt_ps, kb_ps, cb_ps, xs_ps, q_ready, xs_ready, kv_ready, lg_done, lg_read, mx_ready,
         exp_done, pt_ps, pt_ready, pv_done, att_out, ssd_small, ssd_exp, xw_ready, seg_ps, seg_read, seg_in, seg_exp, m_ready,
         y_ps, st_ps, state_new, y_gated, ss_ready, y_rows, yt_ps, yt_act, yt_dve, mix_start,
         row_ps, row_ready, wt_used, mix_ps, mix_read, x1_loaded, ln1_loaded, key_loaded, h2_ready, h2t_ps, h2t_ready, q_ps,
         q8_ready, sc_ps, sc_ready, sc_used, pair_sub, pair_exp, topk_done, row_used, idx_copied, dots_done, gelu_done,
         y_ready, out_done, z_done, held, idx_held, var_ready, root_ready) = map(sem, names.split())
        wt_full = [sem(f"wt_full{i}") for i in range(4)]
        ring_full = [sem(f"ring_full{i}") for i in range(SLOTS)]

        block = ctx.enter_context(nc.Block())

        @block.sync
        def _(sp):
            sp.dma_start(c_tmp[:, :], c_cols[:, :]).then_inc(c_loaded, 16)
            for to, what in ((b_cols, b_ada_cols), (convw, conv_w), (convb, conv_b), (normw, norm_w), (pos_i, pos_cols)):
                sp.dma_start(to[:, :], what[:, :]).then_inc(small_loaded, 16)
            for to, what in ((dtb, dt_bias), (a_neg, a_log), (dskip, d_skip), (sink, sinks)):
                sp.dma_start(to[:, :], what[0:1, :].to_broadcast([P, HEADS])).then_inc(small_loaded, 16)

            def ada_tiles(m):
                for k in range(KT):
                    if not (isinstance(m, int) and k < 4):
                        sp.wait_ge(ada_used, m * KT + k - 3)
                    sp.dma_start(ada[:, k % 4, :], w_ada[k * P:(k + 1) * P, bass.ts(m, D)]).then_inc(ada_full[k % 4], 16)

            ada_tiles(0)
            sp.dma_start(h_t, x_cols[:, :, :]).then_inc(x_loaded, 16)
            with sp.Fori(1, MODS) as m:
                ada_tiles(m)

            def weights(n, slot, what, wait):
                if wait is not None:
                    sp.wait_ge(wt_used, wait)
                sp.dma_start(wt[:, slot, :], what).then_inc(wt_full[slot], 16)

            sp.wait_ge(mod_ready, MODS)
            for slot in range(4):
                weights(0, slot, w_out[slot, :, :], None)
            sp.wait_ge(yt_dve, TB)
            sp.wait_ge(yt_act, TB)
            sp.dma_start(x1, x_rows.rearrange("(b p) d -> p b d", p=P)).then_inc(x1_loaded, 16)
            for to, what in ((ln1gb, ln1_g), (ln1bb, ln1_b), (ln2gb, ln2_g), (ln2bb, ln2_b)):
                sp.dma_start(to, what[0:1, :].to_broadcast([P, D])).then_inc(ln1_loaded, 16)
            sp.dma_start(key_t, keys[:, :]).then_inc(key_loaded, 16)
            with sp.Fori(1, 8) as i:
                for slot in range(4):
                    weights(i, slot, w_out[bass.ds(i * 4 + slot, 1), :, :].rearrange("a p n -> (a p) n"), i * 4 + (slot - 3))
            with sp.Fori(0, 4) as i:
                for slot in range(4):
                    weights(i, slot, w_q[bass.ds(i * 4 + slot, 1), :, :].rearrange("a p n -> (a p) n"), i * 4 + (slot + 29))
            with sp.Fori(0, TB) as m:
                sp.wait_ge(y_ready, m + 1)
                sp.dma_start(out[bass.ts(m, P), :], y_out).then_inc(out_done, 16)
            sp.wait_ge(out_done, 16 * TB)

        @block.gpsimd
        def _(pool):
            def win_half(half, what, cols, slices):
                if slices is not None:
                    pool.wait_ge(*((proj_done, slices * 4) if half else (win_used, slices)))
                pool.dma_start(win[:, half, :, 0:cols], what).then_inc(win_full[half], 16)

            for half in range(2):
                win_half(half, w_xbc[0, :, half * 8:half * 8 + 8, :], 512, None)
            nc.gpsimd.memset(ones[:, :], 1.0).then_inc(consts, 1)
            nc.gpsimd.memset(ident[:, :], 0.0).then_inc(consts, 1)
            nc.gpsimd.memset(band[:, :], 0.0).then_inc(consts, 1)
            nc.gpsimd.memset(x_raw[:, :, 0:CONV - 1], 0.0).then_inc(consts, 1)
            for f in range(NF):
                nc.gpsimd.memset(inv[:, f:f + 1], float(THETA ** (-2.0 * f / ROT))).then_inc(consts, 1)
            nc.gpsimd.iota(iota16[:, :], pattern=[[1, PK]], base=0, channel_multiplier=0,
                           allow_small_or_imprecise_dtypes=True).then_inc(consts, 1)
            pool.wait_ge(consts, 13)
            nc.gpsimd.affine_select(out=tri[:, :], in_=ones[:, :], compare_op=ALU.is_ge, fill=0.0, base=0,
                                    pattern=[[1, P]], channel_multiplier=-1).then_inc(consts2, 1)
            nc.gpsimd.affine_select(out=ident[:, :], in_=ident[:, :], compare_op=ALU.not_equal, fill=1.0, base=0,
                                    pattern=[[-1, P]], channel_multiplier=1).then_inc(consts2, 1)
            nc.gpsimd.affine_select(out=band[:, :], in_=band[:, :], compare_op=ALU.is_gt, fill=NEG, base=0,
                                    pattern=[[1, 2 * P]], channel_multiplier=-1).then_inc(consts2, 1)
            pool.wait_ge(consts2, 3)
            nc.gpsimd.affine_select(out=band[:, :], in_=band[:, :], compare_op=ALU.is_ge, fill=NEG, base=P,
                                    pattern=[[-1, 2 * P]], channel_multiplier=1).then_inc(consts2, 1)
            pool.wait_ge(consts2, 4)
            nc.gpsimd.memset(mask_now[:, 0:P], NEG).then_inc(consts2, 1)
            nc.gpsimd.tensor_copy(mask_now[:, P:2 * P], band[:, P:2 * P]).then_inc(consts2, 1)

            with pool.Fori(1, 3) as n:
                for half in range(2):
                    win_half(half, w_xbc[bass.ds(n, 1), :, half * 8:half * 8 + 8, :].rearrange("a p k n -> (a p) k n"),
                             512, n)
            for half in range(2):
                win_half(half, w_kvdt[:, half * 8:half * 8 + 8, :], KVW + HEADS, 3)
            with pool.Fori(0, 4) as n:
                for half in range(2):
                    win_half(half, w_qz[bass.ds(n, 1), :, half * 8:half * 8 + 8, :].rearrange("a p k n -> (a p) k n"),
                             512, n + 4)

            pool.wait_ge(topk_done, TB)
            with pool.Fori(0, TB) as m:
                for t, table in enumerate((u_tab, v_tab)):
                    with pool.Fori(0, PICKS // SLOTS) as i:
                        for slot in range(SLOTS):
                            count = m * (2 * PICKS) + i * SLOTS + (t * PICKS + slot + 1)
                            pool.wait_ge(row_used, count)
                            nc.gpsimd.tensor_copy(idx[:, slot:slot + 1], ids[:, bass.ds(m, 1), bass.ds(i * SLOTS + slot, 1)]
                                                  .rearrange("p a b -> p (a b)")).then_inc(idx_copied, 1)
                            pool.wait_ge(idx_copied, count)
                            pool.sem_inc(idx_held, 1)
                            nc.gpsimd.indirect_dma_start(
                                out=ring[slot], out_offset=None, in_=table[:, :],
                                in_offset=bass.IndirectOffsetOnAxis(ap=idx[:, slot:slot + 1], axis=0),
                            ).then_inc(ring_full[slot], 16)

        @block.scalar
        def _(act):
            own = Steps(act, act_own)
            act.wait_ge(c_loaded, 16)
            nc.scalar.activation(c_act[:, :], c_tmp[:, :], ACT.Exp, scale=-1.0).then_inc(c_exp, 1)
            act.wait_ge(ang_ready, 1)
            nc.scalar.activation(trig[:, :, :, :].rearrange("p a b c -> p (a b c)"),
                                 ang[:, :, :, :].rearrange("p a b c -> p (a b c)"), ACT.Sin).then_inc(trig_ready, 1)
            act.sem_inc(proj_bank_free, 4)
            with act.Fori(0, 3) as n:
                for m in range(4):
                    act.wait_ge(proj_done, n * 4 + (m + 1))
                    nc.scalar.activation(x_raw[:, bass.ds(n * 4 + m, 1), CONV - 1:].rearrange("p a s -> p (a s)"), bank(m), ACT.Copy)\
                        .then_inc(proj_bank_free, 1)
            for m in range(4):
                act.wait_ge(proj_done, 12 + m + 1)
                nc.scalar.activation(kvdt[:, m, :], ps[:, m, 0:KVW + HEADS], ACT.Copy).then_inc(proj_bank_free, 1)
            for n in range(3):
                act.wait_ge(conv_ready, n + 1)
                part = x_conv[:, 4 * n:4 * n + 4, :]
                nc.scalar.activation(part, part, ACT.Silu).then_inc(silu_done, 1)
            with act.Fori(0, 4) as n:
                for m in range(4):
                    act.wait_ge(proj_done, n * 4 + (16 + m + 1))
                    nc.scalar.activation(qz[:, m, bass.ts(n, 512)], bank(m), ACT.Copy).then_inc(proj_bank_free, 1)
            act.wait_ge(proj_bank_free, 4 + 32)
            gate = qz[:, :, AW:]
            nc.scalar.activation(gate, gate, ACT.Silu).then_inc(z_done, 1)
            act.wait_ge(dt_in, 1)
            own(nc.scalar.activation(dt_abs[:, :, :], dt_abs[:, :, :], ACT.Exp, scale=-1.0))
            nc.scalar.activation(dt_abs[:, :, :], dt_abs[:, :, :], ACT.Ln, bias=1.0).then_inc(dt_log, 1)
            nc.scalar.activation(a_neg[:, :], a_neg[:, :], ACT.Exp).then_inc(a_exp, 1)

            def roots(n):
                act.wait_ge(var_ready, n + 1)
                nc.scalar.activation(root[:, :], var[:, :], ACT.Ln).then_inc(act_own, 1)
                act.wait_ge(act_own, n + 2)
                nc.scalar.activation(root[:, :], root[:, :], ACT.Exp, scale=-0.5).then_inc(root_ready, 1)

            def exps(b, u):
                act.wait_ge(mx_ready, b * 4 + (u + 1))
                nc.scalar.activation(es[:, u % 2, :], es[:, u % 2, :], ACT.Exp)
                for i in range(4):
                    row = lg[:, u % 2, i // 2, i % 2, :]
                    ins = nc.scalar.activation(row, row, ACT.Exp, bias=mx[:, u % 2, i:i + 1], accum_out=den[:, u % 2, i:i + 1])
                ins.then_inc(exp_done, 1)

            def p_turned(b, u):
                act.wait_ge(pt_ps, b * 4 + (u + 1))
                nc.scalar.activation(p_t[:, u % 2, :, :], wide(2, 8, P), ACT.Copy).then_inc(pt_ready, 1)

            with act.Fori(0, TB) as b:
                act.wait_ge(qt_ps, b + 1)
                nc.scalar.activation(q_t, wide(2, HEADS // 2, P), ACT.Copy).then_inc(q_ready, 1)
                act.wait_ge(xs_ps, b + 1)
                nc.scalar.activation(xs_row, wide(4, HEADS, HD), ACT.Copy).then_inc(xs_ready, 1)
                act.wait_ge(ssd_small, b + 1)
                nc.scalar.activation(ea, acum, ACT.Exp)
                nc.scalar.activation(cdec, alast, ACT.Exp)
                nc.scalar.activation(dte, dte, ACT.Exp).then_inc(ssd_exp, 1)
                exps(b, 0)
                exps(b, 1)
                p_turned(b, 0)
                exps(b, 2)
                p_turned(b, 1)
                exps(b, 3)
                p_turned(b, 2)
                p_turned(b, 3)
                for c in range(4):
                    act.wait_ge(seg_in, b * 4 + (c + 1))
                    nc.scalar.activation(decay[:, c % 2, :, :], decay[:, c % 2, :, :], ACT.Exp).then_inc(seg_exp, 1)
                act.wait_ge(yt_ps, b * 2 + 1)
                nc.scalar.activation(y_t[:, 0:8, bass.ts(b, P)], wide(0, 8, P), ACT.Copy).then_inc(yt_act, 1)
                act.wait_ge(y_gated, b + 1)
                for g in range(KV):
                    ins = nc.scalar.activation(decay[:, g, :, :], tmp[:, g * GH:(g + 1) * GH, :].rearrange("p a b -> p (a b)")
                                               .rearrange("p (a b) -> p a b", b=P), ACT.Square, accum_out=ss[:, g:g + 1])
                ins.then_inc(ss_ready, 1)
                roots(b)

            for i, row in enumerate((g1b, sc2b, sh2b, g2b)):
                act.wait_ge(row_ps, i + 1)
                nc.scalar.activation(row, wide(4 * (i % 2), D), ACT.Copy).then_inc(row_ready, 1)
            for m in range(TB + 1):
                if m < TB:
                    roots(TB + m)
                if m:
                    act.wait_ge(h2t_ps, m)
                    nc.scalar.activation(h2_t[:, :, (m - 1) * P:m * P], wide(4 * ((m - 1) % 2), KT, P), ACT.Copy).then_inc(h2t_ready, 1)
            for h in range(PH):
                act.wait_ge(q_ps, h + 1)
                nc.scalar.activation(q8[:, h, :], bank(h), ACT.Copy).then_inc(q8_ready, 1)
            for m in range(TB):
                act.wait_ge(sc_ps, m + 1)
                if m:
                    act.wait_ge(sc_used, m)
                nc.scalar.activation(sc, wide(4 * (m % 2), 2, PH, NKEY), ACT.Copy).then_inc(sc_ready, 1)
                act.wait_ge(pair_sub, m + 1)
                nc.scalar.activation(pair_v, pair_v, ACT.Exp).then_inc(pair_exp, 1)
            with act.Fori(0, TB) as m:
                act.wait_ge(dots_done, m + 1)
                nc.scalar.activation(act_blk, act_blk, ACT.Gelu).then_inc(gelu_done, 1)
                roots(m + 2 * TB)

        @block.vector
        def _(dve):
            own = Steps(dve, dve_own)
            dve.wait_ge(c_exp, 1)
            own(nc.vector.tensor_scalar(c_act[:, :], c_act[:, :], 1.0, None, ALU.add))
            own(nc.vector.reciprocal(c_act[:, :], c_act[:, :]))
            own(nc.vector.tensor_tensor(c_act[:, :], c_act[:, :], c_tmp[:, :], ALU.mult))

            dve.wait_ge(small_loaded, 9 * 16)
            dve.wait_ge(consts, 13)
            ang0 = ang[:, 0, :, :].rearrange("p a b -> p (a b)")
            ang1 = ang[:, 1, :, :].rearrange("p a b -> p (a b)")
            tn = turns[:, 0, :, :].rearrange("p a b -> p (a b)")
            tn1 = turns[:, 1, :, :].rearrange("p a b -> p (a b)")
            pos_f = turns[:, 1, :, 0]
            own(nc.vector.tensor_copy(pos_f, pos_i[:, :]))
            own(nc.vector.tensor_tensor(ang[:, 0, :, :], over(pos_f, 2, NF), over(inv[:, :], 1, TB), ALU.mult))
            own(nc.vector.tensor_scalar(tn, ang0, 1.0 / (2 * math.pi), None, ALU.mult))
            own(nc.vector.tensor_scalar(tn, tn, 12582912.0, None, ALU.add))
            own(nc.vector.tensor_scalar(tn, tn, -12582912.0, None, ALU.add))
            two_pi, part = 2 * math.pi, 6.28125
            part2 = round((two_pi - part) * 2 ** 19) / 2 ** 19
            for piece in (part, part2, two_pi - part - part2):
                own(nc.vector.scalar_tensor_tensor(ang0, tn, -piece, ang0, ALU.mult, ALU.add))
            own(nc.vector.tensor_scalar(ang1, ang0, math.pi / 2, None, ALU.add))
            own(nc.vector.tensor_scalar(tn1, ang1, math.pi, -two_pi, ALU.is_gt, ALU.mult))
            own(nc.vector.tensor_tensor(ang1, ang1, tn1, ALU.add))
            both = ang[:, :, :, :].rearrange("p a b c -> p (a b c)")
            nc.vector.tensor_scalar(both, both, 3.1415925, -3.1415925, ALU.min, ALU.max).then_inc(ang_ready, 1)
            for m in (1, 4):
                part = b_cols[:, m * KT:(m + 2) * KT]
                own(nc.vector.tensor_scalar(part, part, 1.0, None, ALU.add))

            def modulation(m):
                for k in range(KT):
                    dve.wait_ge(ada_full[k % 4], m * (16 * KT // 4) + 16 * (k // 4 + 1))
                    if k == 0:
                        nc.vector.tensor_scalar(acc, ada[:, 0, :], c_act[:, 0:1], None, ALU.mult).then_inc(ada_used, 1)
                    else:
                        dve.wait_ge(ada_used, m * KT + k)
                        nc.vector.scalar_tensor_tensor(acc, ada[:, k % 4, :], c_act[:, k:k + 1], acc, ALU.mult, ALU.add)\
                            .then_inc(ada_used, 1)
                dve.wait_ge(mod_sum, m + 1)
                nc.vector.tensor_tensor(mod_cols[:, bass.ts(m, KT)], ps[:, 4, 0:KT], b_cols[:, bass.ts(m, KT)], ALU.add)\
                    .then_inc(mod_ready, 1)

            with dve.Fori(0, 2) as m:
                modulation(m)
            dve.wait_ge(mod_ready, 2)
            dve.wait_ge(x_loaded, 16)
            for k in range(KT):
                nc.vector.tensor_scalar(h_t[:, k, :], h_t[:, k, :], mod_cols[:, KT + k:KT + k + 1], mod_cols[:, k:k + 1],
                                        ALU.mult, ALU.add).then_inc(h_ready, 1)

            with dve.Fori(0, 3) as n:
                modulation(n + 2)
                dve.wait_ge(proj_bank_free, n * 4 + 8)
                for m in range(4):
                    tile = n * 4 + m
                    src = x_raw[:, bass.ds(tile, 1), :].rearrange("p a s -> p (a s)")
                    dst = x_conv[:, bass.ds(tile, 1), :].rearrange("p a s -> p (a s)")
                    base = own.base + own.n + n * 15 + m * 4
                    for j in range(CONV):
                        w = convw[:, bass.ds(tile * CONV + j, 1)]
                        if j == 0:
                            ins = nc.vector.tensor_scalar(dst, src[:, 0:S], w, convb[:, bass.ds(tile, 1)], ALU.mult, ALU.add)
                        else:
                            dve.wait_ge(dve_own, base + j)
                            ins = nc.vector.scalar_tensor_tensor(dst, src[:, j:j + S], w, dst, ALU.mult, ALU.add)
                        ins.then_inc(conv_ready if m == 3 and j == 3 else dve_own, 1)
            own.n += 3 * 15
            modulation(5)


            dve.wait_ge(proj_done, 32)
            nc.vector.memset(k_t, 0.0)
            nc.vector.memset(vv, 0.0)
            nc.vector.memset(state, 0.0)
            dve.wait_ge(proj_bank_free, 20)
            own(nc.vector.tensor_tensor(dt_all[:, :, :], kvdt[:, :, KVW:], over(dtb[:, :], 1, TB), ALU.add))
            nc.vector.scalar_tensor_tensor(dt_abs[:, :, :], dt_all[:, :, :], -1.0, dt_all[:, :, :], ALU.mult, ALU.max).then_inc(dt_in, 1)
            dve.wait_ge(dt_log, 1)
            own(nc.vector.scalar_tensor_tensor(dt_all[:, :, :], dt_all[:, :, :], 0.0, dt_abs[:, :, :], ALU.max, ALU.add))
            dve.wait_ge(a_exp, 1)
            own(nc.vector.scalar_tensor_tensor(da_all[:, :, :], over(a_neg[:, :], 1, TB), -1.0, dt_all[:, :, :],
                                               ALU.mult, ALU.mult))
            dve.wait_ge(silu_done, 3)
            dve.wait_ge(z_done, 1)
            dve.wait_ge(trig_ready, 1)
            dve.wait_ge(consts2, 6)

            def logits(b, u, step):
                i = u % 2
                dve.wait_ge(lg_done, b * 4 + (u + 1))
                rows = lg[:, i, :, :, :].rearrange("p a b k -> p (a b) k")
                nc.vector.scalar_tensor_tensor(rows, wide(0, 4, 2 * P), HD ** -0.5, over(mask_now[:, :], 1, 4), ALU.mult, ALU.add)\
                    .then_inc(lg_read, 1)
                dve.wait_ge(lg_read, b * 4 + (u + 1))
                step(nc.vector.tensor_reduce(mx[:, i, :], rows, AX, ALU.max))
                s4 = sink[:, 4 * u:4 * u + 4].rearrange("p (a b) -> p b a", b=2)
                m4 = mx[:, i, :].rearrange("p (b a) -> p b a", b=2)
                e4 = es[:, i, :].rearrange("p (b a) -> p b a", b=2)
                step(nc.vector.tensor_tensor(m4, m4, s4, ALU.max))
                nc.vector.tensor_tensor(e4, s4, m4, ALU.subtract)
                nc.vector.tensor_scalar(mx[:, i, :], mx[:, i, :], -1.0, None, ALU.mult).then_inc(mx_ready, 1)

            def attended(b, u, step):
                i = u % 2
                dve.wait_ge(pv_done, b * 4 + (u + 1))
                step(nc.vector.tensor_tensor(den[:, i, :], den[:, i, :], es[:, i, :], ALU.add))
                step(nc.vector.reciprocal(den[:, i, :], den[:, i, :]))
                src = ps[:, 4 + u // 2, (u % 2) * 256:(u % 2) * 256 + 256].rearrange("p (a b d) -> p a b d", a=2, b=2)
                dst = y_row[:, u * 256:u * 256 + 256].rearrange("p (a b d) -> p a b d", a=2, b=2)
                r = over(den[:, i, :].rearrange("p (b a) -> p a b", b=2), 3, HD)
                nc.vector.tensor_tensor(dst, src, r, ALU.mult).then_inc(att_out, 1)

            def segment(b, c, step):
                dve.wait_ge(seg_ps, b * 4 + (c + 1))
                d = decay[:, c % 2, :, :]
                nc.vector.tensor_tensor(d, wide(c % 2, 4, P), over(acum[:, 4 * c:4 * c + 4], 2, P), ALU.subtract)\
                    .then_inc(seg_read, 1)
                dve.wait_ge(seg_read, b * 4 + (c + 1))
                nc.vector.tensor_scalar(d, d, 0.0, None, ALU.min).then_inc(seg_in, 1)

            def mixing(b, c):
                dve.wait_ge(seg_exp, b * 4 + (c + 1))
                nc.vector.tensor_tensor(m_t[:, 4 * c:4 * c + 4, :], decay[:, c % 2, :, :], over(cbm[:, c // 2, :], 1, 4), ALU.mult)\
                    .then_inc(m_ready, 1)

            def one_over_root(n, step):
                dve.wait_ge(root_ready, n + 1)
                step(nc.vector.tensor_tensor(root_t[:, :], root[:, :], root[:, :], ALU.mult))
                step(nc.vector.tensor_tensor(root_t[:, :], root_t[:, :], var[:, :], ALU.mult))
                step(nc.vector.tensor_scalar(root_t[:, :], root_t[:, :], -0.5, 1.5, ALU.mult, ALU.add))
                step(nc.vector.tensor_tensor(root[:, :], root[:, :], root_t[:, :], ALU.mult))

            start = own.n
            MIX_STEPS = 30
            with dve.Fori(0, TB) as b:
                step = Steps(dve, dve_own, b * MIX_STEPS + start)
                nc.vector.tensor_copy(cur, x_conv[:, :, bass.ts(b, P)])
                nc.vector.tensor_copy(qk[:, 0:HEADS, :].rearrange("p a b -> p (a b)"), qz[:, bass.ds(b, 1), 0:AW].rearrange("p a b -> p (a b)"))
                nc.vector.tensor_copy(qk[:, HEADS:, :].rearrange("p a b -> p (a b)"), kvdt[:, bass.ds(b, 1), 0:KV * HD].rearrange("p a b -> p (a b)"))
                nc.vector.tensor_copy(da_now, da_all[:, bass.ds(b, 1), :].rearrange("p a b -> p (a b)"))
                step(nc.vector.tensor_copy(trig_now, trig[:, :, bass.ds(b, 1), :].rearrange("p a b c -> p a (b c)")))
                t1, t2 = qk[:, :, 0:NF], qk[:, :, NF:ROT]
                sn, cs = over(trig_now[:, 0, :], 1, HEADS + KV), over(trig_now[:, 1, :], 1, HEADS + KV)
                for i, (t, f) in enumerate(((t1, cs), (t2, sn), (t2, cs), (t1, sn))):
                    ins = nc.vector.tensor_tensor(rope_tmp[:, i, :, :], t, f, ALU.mult)
                step(ins)
                nc.vector.tensor_tensor(t1, rope_tmp[:, 0, :, :], rope_tmp[:, 1, :, :], ALU.subtract)
                step(nc.vector.tensor_tensor(t2, rope_tmp[:, 2, :, :], rope_tmp[:, 3, :, :], ALU.add))
                nc.vector.tensor_copy(k_t[:, :, 0:P], k_t[:, :, P:2 * P])
                step(nc.vector.tensor_copy(vv[:, 0, :], vv[:, 1, :]))
                nc.vector.tensor_copy(vv[:, 1, :], kvdt[:, bass.ds(b, 1), KV * HD:KVW].rearrange("p a b -> p (a b)"))
                nc.vector.tensor_copy(kdup, over(qk[:, HEADS:, :], 2, 2)).then_inc(block_in, 1)
                dve.wait_ge(kb_ps, b + 1)
                nc.vector.tensor_copy(k_t[:, :, P:2 * P], ps[:, 6, 0:256].rearrange("p (a b) -> p a b", a=2))
                nc.vector.tensor_copy(b_row, ps[:, 6, 256:512].rearrange("p (a b) -> p a b", a=2))
                dve.wait_ge(cb_ps, b + 1)
                nc.vector.tensor_copy(acum, ps[:, 7, 0:HEADS])
                step(nc.vector.tensor_copy(alast, ps[:, 7, HEADS:2 * HEADS]))
                nc.vector.tensor_tensor(dte, alast, acum, ALU.subtract).then_inc(ssd_small, 1)
                nc.vector.tensor_tensor(cbm, ps[:, 7, 128:384].rearrange("p (a b) -> p a b", a=2), over(tri[:, :], 1, 2), ALU.mult)\
                    .then_inc(kv_ready, 1)
                logits(b, 0, step)
                logits(b, 1, step)
                attended(b, 0, step)
                logits(b, 2, step)
                attended(b, 1, step)
                logits(b, 3, step)
                attended(b, 2, step)
                nc.vector.tensor_copy(mask_now[:, 0:P], band[:, 0:P])
                dve.wait_ge(xs_ready, b + 1)
                dt_b = dt_all[:, bass.ds(b, 1), :].rearrange("p a b -> p (a b)")
                step(nc.vector.tensor_tensor(xdt, xs_row, over(dt_b, 2, HD), ALU.mult))
                dve.wait_ge(ssd_exp, b + 1)
                nc.vector.tensor_tensor(xw, xdt, over(dte, 2, HD), ALU.mult).then_inc(xw_ready, 1)
                segment(b, 0, step)
                segment(b, 1, step)
                attended(b, 3, step)
                mixing(b, 0)
                segment(b, 2, step)
                mixing(b, 1)
                segment(b, 3, step)
                mixing(b, 2)
                mixing(b, 3)
                dve.wait_ge(st_ps, b + 1)
                step(nc.vector.tensor_tensor(tmp, state, over(cdec, 2, HD), ALU.mult))
                nc.vector.tensor_tensor(state, tmp, wide(2, HEADS, HD), ALU.add).then_inc(state_new, 1)
                dve.wait_ge(state_new, b + 1)
                dve.wait_ge(y_ps, b + 1)
                nc.vector.tensor_tensor(xw, xs_row, over(dskip[:, :], 2, HD), ALU.mult)
                step(nc.vector.tensor_tensor(tmp, wide(4, HEADS, HD), over(ea, 2, HD), ALU.mult))
                step(nc.vector.tensor_tensor(tmp, tmp, wide(6, HEADS, HD), ALU.add))
                step(nc.vector.tensor_tensor(tmp, tmp, xw, ALU.add))
                z_b = qz[:, bass.ds(b, 1), AW:].rearrange("p a (h d) -> p (a h) d", d=HD)
                nc.vector.tensor_tensor(tmp, tmp, z_b, ALU.mult).then_inc(y_gated, 1)
                dve.wait_ge(ss_ready, b + 1)
                nc.vector.tensor_scalar(var[:, :], ss, 1.0 / (GH * HD), EPS, ALU.mult, ALU.add).then_inc(var_ready, 1)
                one_over_root(b, step)
                for g in range(KV):
                    ins = nc.vector.tensor_scalar(y_row[:, AW + g * 512:AW + (g + 1) * 512],
                                                  tmp[:, g * GH:(g + 1) * GH, :].rearrange("p a b -> p (a b)"), root[:, g:g + 1], None, ALU.mult)
                ins.then_inc(y_rows, 1)
                dve.wait_ge(yt_ps, b * 2 + 2)
                nc.vector.tensor_tensor(y_t[:, 8:16, bass.ts(b, P)], wide(2, 8, P), over(normw[:, :], 2, P), ALU.mult).then_inc(yt_dve, 1)
                assert step.n == MIX_STEPS, step.n
            own.n += TB * MIX_STEPS

            dve.sem_inc(mix_read, 4)
            dve.wait_ge(x1_loaded, 16)
            dve.wait_ge(row_ready, 4)
            for n in range(2):
                for m in range(TB):
                    cols = slice(n * 1024, (n + 1) * 1024)
                    dve.wait_ge(mix_ps, n * 4 + m + 1)
                    nc.vector.tensor_tensor(tmp2[:, 0:1024], wide(2 * m, 1024), g1b[:, cols], ALU.mult).then_inc(mix_read, 1)
                    dve.wait_ge(mix_read, 4 + n * 4 + m + 1)
                    own(nc.vector.scalar_tensor_tensor(x1[:, m, cols], x1[:, m, cols], ALPHA, tmp2[:, 0:1024], ALU.mult, ALU.add))

            def layer_norm(n, row, gain, step):
                for j in range(4):
                    ins = nc.vector.bn_stats(stats[:, j, :], row[:, j * 512:(j + 1) * 512])
                step(ins)
                step(nc.vector.bn_aggr(mv, stats.rearrange("p a b -> p (a b)")))
                nc.vector.tensor_scalar(var[:, 0:1], mv[:, 1:2], EPS, None, ALU.add).then_inc(var_ready, 1)
                one_over_root(n, step)
                step(nc.vector.tensor_scalar(row, row, mv[:, 0:1], root[:, 0:1], ALU.subtract, ALU.mult))
                step(nc.vector.tensor_tensor(row, row, gain, ALU.mult))

            dve.wait_ge(ln1_loaded, 4 * 16)
            start1 = own.n
            with dve.Fori(0, TB) as m:
                step = Steps(dve, dve_own, m * 10 + start1, held)
                row = x1[:, bass.ds(m, 1), :].rearrange("p a b -> p (a b)")
                h_row = h2[:, bass.ds(m, 1), :].rearrange("p a b -> p (a b)")
                layer_norm(m + TB, row, ln1gb, step)
                step(nc.vector.tensor_tensor(row, row, ln1bb, ALU.add))
                step(nc.vector.tensor_tensor(h_row, row, sc2b, ALU.mult))
                nc.vector.tensor_tensor(h_row, h_row, sh2b, ALU.add).then_inc(h2_ready, 1)
                assert step.n == 10, step.n
            own.n += TB * 10

            def best16(values, indices, source, scratch, step):
                step(nc.vector.max(values[:, 0:8], source))
                nc.vector.max_index(indices[:, 0:8], values[:, 0:8], source)
                step(nc.vector.match_replace(scratch, values[:, 0:8], source, NEG))
                step(nc.vector.max(values[:, 8:16], scratch))
                return nc.vector.max_index(indices[:, 8:16], values[:, 8:16], scratch)

            start2 = own.n
            TOP_STEPS = 88
            with dve.Fori(0, TB) as m:
                step = Steps(dve, dve_own, m * TOP_STEPS + start2, held)
                dve.wait_ge(sc_ready, m + 1)
                dve.sem_inc(held, 1)
                for side in range(2):
                    for h in range(PH):
                        ins = best16(top_v[:, side, h, :], top_i[:, side, h, :], sc[:, side, h, :], rest, step)
                step(ins)
                step(nc.vector.tensor_copy(top_f, top_i))
                step(nc.vector.tensor_tensor(cand, over(top_v[:, 0, :, :], 3, PK), over(top_v[:, 1, :, :], 2, PK), ALU.add))
                for h in range(PH):
                    flat = cand[:, h, :, :].rearrange("p a b -> p (a b)")
                    ins = best16(pair_v[:, h, :], pair_i[:, h, :], flat, flat, step)
                step(ins)
                step(nc.vector.tensor_copy(pick_sum, pair_v[:, :, 0]))
                nc.vector.tensor_tensor(pair_v, pair_v, over(pick_sum, 2, PK), ALU.subtract).then_inc(pair_sub, 1)
                nc.vector.tensor_scalar(part_u[:, 0, :, :], pair_i, 4, None, ALU.logical_shift_right)
                step(nc.vector.tensor_scalar(part_u[:, 1, :, :], pair_i, 15, None, ALU.bitwise_and))
                step(nc.vector.tensor_copy(part_f, part_u))
                for side in range(2):
                    flat = hits.rearrange("p a b c -> p (a b) c")
                    places = part_f[:, side, :, :].rearrange("p a b -> p (a b)")
                    step(nc.vector.tensor_tensor(flat, over(iota16[:, :], 1, PICKS), over(places, 2, PK), ALU.is_equal))
                    step(nc.vector.tensor_tensor(hits, hits, over(top_f[:, side, :, :], 2, PK), ALU.mult))
                    step(nc.vector.tensor_reduce(part_id[:, side, :, :].rearrange("p a b -> p (a b)"), flat, AX, ALU.add))
                step(nc.vector.scalar_tensor_tensor(part_f[:, 0, :, :], part_id[:, 0, :, :], float(NKEY), part_id[:, 1, :, :],
                                                    ALU.mult, ALU.add))
                nc.vector.tensor_copy(ids[:, bass.ds(m, 1), :].rearrange("p a (b c) -> p (a b) c", c=PK), part_f[:, 0, :, :])
                dve.wait_ge(pair_exp, m + 1)
                step(nc.vector.tensor_reduce(pick_sum, pair_v, AX, ALU.add))
                step(nc.vector.reciprocal(pick_sum, pick_sum))
                nc.vector.tensor_tensor(gates[:, bass.ds(m, 1), :].rearrange("p a (b c) -> p (a b) c", c=PK), pair_v,
                                        over(pick_sum, 2, PK), ALU.mult).then_inc(topk_done, 1)
                dve.wait_ge(topk_done, m + 1)
                dve.sem_inc(sc_used, 1)
                assert step.n == TOP_STEPS, step.n
            own.n += TB * TOP_STEPS

            dve.sem_inc(row_used, SLOTS)
            start3 = own.n
            EXP_STEPS = 12
            with dve.Fori(0, TB) as m:
                step = Steps(dve, dve_own, m * (EXP_STEPS + 32) + start3, held)
                nc.vector.memset(acc_v, 0.0)
                step(nc.vector.tensor_copy(h2_now, h2[:, bass.ds(m, 1), :].rearrange("p a b -> p (a b)")))
                with dve.Fori(0, PICKS // SLOTS) as i:
                    for slot in range(SLOTS):
                        dve.wait_ge(ring_full[slot], m * (16 * 2 * PICKS // SLOTS) + i * 16 + 16)
                        nc.vector.tensor_tensor_reduce(out=ring[slot], in0=ring[slot], in1=h2_now, scale=1.0, scalar=0.0,
                                                       op0=ALU.mult, op1=ALU.add, accum_out=act8[:, slot:slot + 1]).then_inc(row_used, 1)
                    dve.wait_ge(row_used, m * (2 * PICKS) + i * SLOTS + 2 * SLOTS)
                    nc.vector.tensor_copy(act_blk[:, bass.ds(i * SLOTS, SLOTS)], act8).then_inc(dve_own, 1)
                    dve.wait_ge(dve_own, m * (EXP_STEPS + 32) + i + (start3 + step.n + 1))
                step.n += PICKS // SLOTS
                dve.sem_inc(dots_done, 1)
                dve.wait_ge(gelu_done, m + 1)
                step(nc.vector.tensor_tensor(w_blk, act_blk, gates[:, bass.ds(m, 1), :].rearrange("p a b -> p (a b)"), ALU.mult))
                with dve.Fori(0, PICKS // SLOTS) as i:
                    nc.vector.tensor_copy(w8, w_blk[:, bass.ds(i * SLOTS, SLOTS)]).then_inc(dve_own, 1)
                    dve.wait_ge(dve_own, m * (EXP_STEPS + 32) + i + (start3 + step.n + 1))
                    for slot in range(SLOTS):
                        dve.wait_ge(ring_full[slot], m * (16 * 2 * PICKS // SLOTS) + i * 16 + (16 * PICKS // SLOTS + 16))
                        dve.wait_ge(row_used, m * (2 * PICKS) + i * SLOTS + (SLOTS + PICKS + slot))
                        nc.vector.scalar_tensor_tensor(acc_v, ring[slot], w8[:, slot:slot + 1], acc_v, ALU.mult, ALU.add)\
                            .then_inc(row_used, 1)
                    dve.wait_ge(row_used, m * (2 * PICKS) + i * SLOTS + (2 * SLOTS + PICKS))
                step.n += PICKS // SLOTS
                step(nc.vector.tensor_tensor(acc_v, acc_v, g2b, ALU.mult))
                step(nc.vector.scalar_tensor_tensor(acc_v, x1[:, bass.ds(m, 1), :].rearrange("p a b -> p (a b)"), ALPHA, acc_v,
                                                    ALU.mult, ALU.add))
                layer_norm(m + 2 * TB, acc_v, ln2gb, step)
                nc.vector.tensor_tensor(y_out, acc_v, ln2bb, ALU.add).then_inc(y_ready, 1)
                dve.wait_ge(out_done, m * 16 + 16)
                assert step.n == EXP_STEPS + 32, step.n

        @block.tensor
        def _(pe):
            def mod_sums(m):
                pe.wait_ge(ada_used, (m + 1) * KT)
                for k in range(KT):
                    ins = nc.tensor.matmul(ps[:, 4, k:k + 1], acc[:, k * P:(k + 1) * P], ones[:, 0:1], start=True, stop=True)
                ins.then_inc(mod_sum, 1)

            def slice_of(first, n, cols, channels):
                for half in range(2):
                    pe.wait_ge(win_full[half], n * 16 + 16 * (first + 1))
                    for m in range(4):
                        if half == 0:
                            pe.wait_ge(proj_bank_free, n * 4 + (4 * first + m + 1))
                        for j in range(8):
                            k = half * 8 + j
                            if channels:
                                lhs, rhs = win[:, half, j, m * P:(m + 1) * P], h_t[:, k, :]
                            else:
                                lhs, rhs = h_t[:, k, m * P:(m + 1) * P], win[:, half, j, 0:cols]
                            ins = nc.tensor.matmul(ps[:, m, 0:cols], lhs, rhs, start=k == 0, stop=k == KT - 1)
                        if half == 1:
                            ins.then_inc(proj_done, 1)
                        elif m == 3:
                            ins.then_inc(win_used, 1)

            pe.wait_ge(consts2, 6)
            for m in range(2):
                mod_sums(m)
            pe.wait_ge(h_ready, KT)
            with pe.Fori(0, 3) as n:
                slice_of(0, n, 512, True)
                mod_sums(n + 2)
            slice_of(3, 0, KVW + HEADS, False)
            with pe.Fori(0, 3) as n:
                slice_of(4, n, 512, False)
            mod_sums(5)
            slice_of(4, 3, 512, False)

            def turn(dst, src):
                return nc.tensor.transpose(dst, src, ident[:, :])

            def logits(b, u):
                if u:
                    pe.wait_ge(lg_read, b * 4 + u)
                for pair in range(2):
                    for par in range(2):
                        rows = slice(64 * par, 64 * par + 64)
                        ins = nc.tensor.matmul(ps[:, par, pair * 256:pair * 256 + 256], q_t[rows, 2 * u + pair, :],
                                               k_t[rows, u // 2, :], start=True, stop=True)
                ins.then_inc(lg_done, 1)

            def turn_p(b, u):
                pe.wait_ge(exp_done, b * 4 + (u + 1))
                if u:
                    pe.wait_ge(pt_ready, b * 4 + u)
                for j in range(8):
                    ins = turn(wide(2, 8, P)[:, j, :], lg[:, u % 2, j // 4, j // 2 % 2, (j % 2) * P:(j % 2 + 1) * P])
                ins.then_inc(pt_ps, 1)

            def values(b, u):
                pe.wait_ge(pt_ready, b * 4 + (u + 1))
                if u % 2:
                    pe.wait_ge(att_out, b * 4 + u)
                for pair in range(2):
                    for par in range(2):
                        h = 4 * u + 2 * pair + par
                        for half in range(2):
                            ins = nc.tensor.matmul(ps[:, 4 + h // GH, (h % GH) * HD:(h % GH + 1) * HD],
                                                   p_t[:, u % 2, (par * 2 + pair) * 2 + half, :],
                                                   vv[:, half, (h // GH) * HD:(h // GH + 1) * HD], start=half == 0, stop=half == 1)
                ins.then_inc(pv_done, 1)

            def segments(b, c):
                if c >= 2:
                    pe.wait_ge(seg_read, b * 4 + (c - 1))
                for i in range(4):
                    h = 4 * c + i
                    ins = nc.tensor.matmul(ps[:, c % 2, i * P:(i + 1) * P], da_now[:, h:h + 1].to_broadcast([P, P]), tri[:, :],
                                           start=True, stop=True)
                ins.then_inc(seg_ps, 1)

            def within(b, c):
                pe.wait_ge(m_ready, b * 4 + (c + 1))
                for i in range(4):
                    h = 4 * c + i
                    ins = nc.tensor.matmul(ps[:, 6 + h // GH, (h % GH) * HD:(h % GH + 1) * HD], m_t[:, h, :], xdt[:, h, :],
                                           start=True, stop=True)
                return ins

            with pe.Fori(0, TB) as b:
                pe.wait_ge(block_in, b + 1)
                for i in range(HEADS // 2):
                    ins = turn(wide(2, 8, P)[:, i, :], qk[:, 2 * i:2 * i + 2, :].rearrange("p a b -> p (a b)"))
                ins.then_inc(qt_ps, 1)
                for g in range(KV):
                    turn(ps[:, 6, g * P:(g + 1) * P], kdup[:, g, :, :].rearrange("p a b -> p (a b)"))
                for g in range(KV):
                    ins = turn(ps[:, 6, (2 + g) * P:(3 + g) * P], cur[:, 8 + g, :])
                ins.then_inc(kb_ps, 1)
                nc.tensor.matmul(ps[:, 7, 0:HEADS], tri[:, :], da_now, start=True, stop=True)
                nc.tensor.matmul(ps[:, 7, HEADS:2 * HEADS], ones[:, :], da_now, start=True, stop=True)
                for g in range(KV):
                    ins = nc.tensor.matmul(ps[:, 7, (1 + g) * P:(2 + g) * P], cur[:, 8 + g, :], cur[:, 10 + g, :], start=True, stop=True)
                ins.then_inc(cb_ps, 1)
                for i in range(8):
                    ins = turn(wide(4, 8, P)[:, i, :], cur[:, i, :])
                ins.then_inc(xs_ps, 1)
                pe.wait_ge(q_ready, b + 1)
                pe.wait_ge(kv_ready, b + 1)
                logits(b, 0)
                logits(b, 1)
                turn_p(b, 0)
                logits(b, 2)
                pe.wait_ge(xs_ready, b + 1)
                values(b, 0)
                turn_p(b, 1)
                logits(b, 3)
                values(b, 1)
                turn_p(b, 2)
                pe.wait_ge(lg_read, b * 4 + 4)
                segments(b, 0)
                segments(b, 1)
                values(b, 2)
                turn_p(b, 3)
                values(b, 3)
                within(b, 0)
                segments(b, 2)
                within(b, 1)
                segments(b, 3)
                pe.wait_ge(xw_ready, b + 1)
                pe.wait_ge(att_out, b * 4 + 4)
                for g in range(KV):
                    nc.tensor.matmul(ps[:, 4 + g, :], cur[:, 10 + g, :], state[:, g * GH:(g + 1) * GH, :].rearrange("p a b -> p (a b)"),
                                     start=True, stop=True)
                for g in range(KV):
                    ins = nc.tensor.matmul(ps[:, 2 + g, :], b_row[:, g, :], xw[:, g * GH:(g + 1) * GH, :].rearrange("p a b -> p (a b)"),
                                           start=True, stop=True)
                ins.then_inc(st_ps, 1)
                within(b, 2)
                within(b, 3).then_inc(y_ps, 1)
                pe.wait_ge(seg_read, b * 4 + 4)
                for i in range(8):
                    ins = turn(wide(0, 8, P)[:, i, :], y_row[:, i * P:(i + 1) * P])
                ins.then_inc(yt_ps, 1)
                pe.wait_ge(y_rows, b + 1)
                for i in range(8):
                    ins = turn(wide(2, 8, P)[:, i, :], y_row[:, (8 + i) * P:(9 + i) * P])
                ins.then_inc(yt_ps, 1)
                pe.wait_ge(yt_act, b + 1)

            pe.wait_ge(yt_dve, TB)
            pe.wait_ge(mod_ready, MODS)
            for i, m in enumerate((2, 4, 3, 5)):
                if i >= 2:
                    pe.wait_ge(row_ready, i - 1)
                for k in range(KT):
                    ins = nc.tensor.matmul(ps[:, 4 * (i % 2) + k // 4, (k % 4) * P:(k % 4 + 1) * P],
                                           mod_cols[:, m * KT + k:m * KT + k + 1].to_broadcast([P, P]), ident[:, :], start=True, stop=True)
                ins.then_inc(row_ps, 1)

            pe.wait_ge(row_ready, 4)
            with pe.Fori(0, 2) as n:
                for k in range(KT):
                    pe.wait_ge(wt_full[k % 4], n * 64 + 16 * (k // 4 + 1))
                    for m in range(TB):
                        if k == 0:
                            pe.wait_ge(mix_read, n * 4 + (m + 1))
                        for j in range(2):
                            ins = nc.tensor.matmul(ps[:, 2 * m + j, :], y_t[:, k, m * P:(m + 1) * P], wt[:, k % 4, j * 512:(j + 1) * 512],
                                                   start=k == 0, stop=k == KT - 1)
                        if k == KT - 1:
                            ins.then_inc(mix_ps, 1)
                        elif m == TB - 1:
                            ins.then_inc(wt_used, 1)
                pe.wait_ge(mix_ps, n * 4 + 4)
                pe.sem_inc(wt_used, 1)

            for m in range(TB):
                pe.wait_ge(h2_ready, m + 1)
                if m >= 2:
                    pe.wait_ge(h2t_ready, m - 1)
                for k in range(KT):
                    ins = turn(wide(4 * (m % 2), KT, P)[:, k, :], h2[:, m, k * P:(k + 1) * P])
                ins.then_inc(h2t_ps, 1)
            pe.wait_ge(h2t_ready, TB)
            for k in range(KT):
                pe.wait_ge(wt_full[k % 4], 128 + 16 * (k // 4 + 1))
                for h in range(PH):
                    ins = nc.tensor.matmul(bank(h), wt[:, k % 4, h * P:(h + 1) * P], h2_t[:, k, :], start=k == 0, stop=k == KT - 1)
                    if k == KT - 1:
                        ins.then_inc(q_ps, 1)
                if k < KT - 1:
                    ins.then_inc(wt_used, 1)
            pe.wait_ge(key_loaded, 16)
            pe.wait_ge(q8_ready, PH)
            for m in range(TB):
                if m >= 2:
                    pe.wait_ge(sc_ready, m - 1)
                for h in range(PH):
                    for side in range(2):
                        rows = slice(64 * side, 64 * side + 64)
                        ins = nc.tensor.matmul(wide(4 * (m % 2), 2, PH, NKEY)[:, side, h, :], q8[rows, h, m * P:(m + 1) * P],
                                               key_t[rows, :], start=True, stop=True)
                ins.then_inc(sc_ps, 1)


def kernel(**inputs):
    import numpy as np
    import concourse.bacc as bacc
    from concourse.bass_utils import run_bass_kernel_spmd as run

    a = {n: np.asarray(v) for n, v in inputs.items()}
    x = a["x"][0]
    w_in = a["w_in"][0].reshape(KT, P, -1).transpose(1, 0, 2)
    z0 = AW + KVW
    xbc0 = z0 + AW
    dt0 = xbc0 + XT * P
    laid = {
        "x_rows": x,
        "x_cols": x.T.reshape(KT, P, S).transpose(1, 0, 2),
        "c_cols": a["c"][0].reshape(KT, P).T,
        "pos_cols": a["positions"][0].reshape(TB, P).T,
        "w_ada": a["w_ada"][0],
        "b_ada_cols": a["b_ada"][0].reshape(MODS * KT, P).T,
        "w_xbc": np.stack([w_in[:, :, xbc0 + i * 512:xbc0 + (i + 1) * 512] for i in range(XT // 4)]),
        "w_kvdt": np.concatenate([w_in[:, :, AW:z0], w_in[:, :, dt0:]], axis=2),
        "w_qz": np.stack([w_in[:, :, c:c + 512] for c in (0, 512, z0, z0 + 512)]),
        "conv_w": a["conv_w"][0].reshape(CONV, XT, P).transpose(2, 1, 0).reshape(P, XT * CONV),
        "conv_b": a["conv_b"][0].reshape(XT, P).T,
        "dt_bias": a["dt_bias"],
        "a_log": a["a_log"],
        "d_skip": a["d_skip"],
        "norm_w": a["ssd_norm_w"][0].reshape(AW // P, P).T,
        "sinks": a["attn_sinks"],
        "w_out": a["w_out"][0].reshape(KT, P, 2, D // 2).transpose(2, 0, 1, 3).reshape(2 * KT, P, D // 2),
        "ln1_g": a["ln1_g"],
        "ln1_b": a["ln1_b"],
        "w_q": a["peer_wq"][0].reshape(KT, P, PH * P),
        "keys": np.concatenate([a["peer_k1"][0].T, a["peer_k2"][0].T]),
        "u_tab": a["peer_u"][0],
        "v_tab": a["peer_v"][0],
        "ln2_g": a["ln2_g"],
        "ln2_b": a["ln2_b"],
    }
    nc = bacc.Bacc("TRN2", target_bir_lowering=False, num_devices=1)
    arrays, args = {}, []
    for name, value in laid.items():
        value = np.ascontiguousarray(value)
        arrays[f"in_{name}"] = value
        args.append(nc.dram_tensor(f"in_{name}", value.shape, mybir.dt.from_np(value.dtype), kind="ExternalInput").ap())
    args.append(nc.dram_tensor("out_rows", (S, D), F32, kind="ExternalOutput").ap())
    decoder_layer(nc, *args)
    result = run(nc, [arrays], core_ids=[0])
    return result.results[0]["out_rows"].reshape(1, S, D)
```

```python
import math
from contextlib import ExitStack

import concourse.bass as bass
from concourse import mybir

P = 128
D = 2048
KT = D // P
S = 512
TB = S // P
HEADS, HD = 16, 64
KV = 2
GH = HEADS // KV
AW = HEADS * HD
ROT = HD // 4
NF = ROT // 2
THETA = 500000.0
CONV = 4
XT = (AW + 2 * KV * P) // P
KVW = 2 * KV * HD
MODS = 6
PH, PK = 8, 16
NKEY = 128
PICKS = PH * PK
ALPHA = 2.0 ** 0.25
EPS = 1e-5
NEG = -1.0e30
DB = TB - 1
DT = DB * P
GT = 4
GROUPS = NKEY // GT
UNIT = 1024
RAWS = 4
SLOTS = PICKS // GROUPS
TG = 16
OH = 8
AHEAD = 6
WIN_PAIRS = AHEAD * GT // TB // 2
WIN_UNITS = 4 * WIN_PAIRS

F32 = mybir.dt.float32
F32R = mybir.dt.float32r
I32 = mybir.dt.int32
U32 = mybir.dt.uint32
ALU = mybir.AluOpType
ACT = mybir.ActivationFunctionType
AX = mybir.AxisListType.X

K = 1024
HT = 0
WIN = 8 * K
ADA = 16 * K
ACC = 24 * K
WT = 22 * K
SPARE = 26 * K
QZ = 28 * K
KVDT = 36 * K
XRAW = KVDT + TB * (KVW + HEADS)
XCONV = XRAW + XT * (S + CONV - 1)
GM = 0
RAW = GM + 2 * GT * DT
GEL = RAW + RAWS * UNIT
OUT4 = GEL + 2 * DT
RING = OUT4 + TB * D
SPREAD = 14 * K
STAGE = QZ
PARTS = 26 * K
WP, SP_, HP = 2 * 2 * GT * DT, 2 * 2 * UNIT, 2 * KT * DT
LATE = PARTS + WP + SP_ + HP
ARENA = LATE + 2048
assert RING + 2 * D <= 20 * K and LATE >= PARTS


class Steps:

    def __init__(self, engine, semaphore, base=0, held=None):
        self.engine, self.semaphore, self.base, self.held, self.n = engine, semaphore, base, held, 0

    def __call__(self, instruction):
        self.n += 1
        instruction.then_inc(self.semaphore, 1)
        self.engine.wait_ge(self.semaphore, self.base + self.n)
        if self.held is not None:
            self.engine.sem_inc(self.held, 1)


def over(ap, axis, n):
    wide = ap.unsqueeze(axis)
    shape = list(wide.shape)
    shape[axis] = n
    return wide.to_broadcast(shape)


class Group:

    def __init__(self, kind, c, p=None):
        self.kind, self.c, self.p = kind, c, p
        u = [("u", i, half) for i in range(GT) for half in range(2)]
        v = [("v", i, half) for half in range(2) for i in range(GT)]
        self.units = {"start": [], "ahead": v, "full": u[:4] + v[:4] + u[4:] + v[4:], "last": v}[kind]
        self.second = p is None and c == 1

    def val(self, times, plus=0):
        at = times * self.c + plus
        return at if self.p is None else self.p * (2 * times) + at

    def unit(self, j):
        if self.kind == "ahead":
            return self.val(2 * GT, j - 2 * GT)
        return self.val(4 * GT, j - 2 * GT * (AHEAD + 1))

    def round(self, times, plus=0):
        at = times * (self.c // 2) + plus
        return at if self.p is None else self.p * times + at

    def tiles_at(self, j):
        if self.kind == "start":
            return [(i, due) for i in range(GT) for due in ("made", "high", "low")]
        if self.kind == "ahead":
            return [(j // 2, "made")] if j % 2 == 0 else [(j // 2, "high"), (j // 2, "low")]
        due = []
        if self.kind == "full":
            for i in range(GT):
                since = j - self.units.index(("u", i, 1))
                due += [(i, what) for what in {2: ("gelu", "made"), 3: ("high",), 4: ("low",)}.get(since, ())]
        return due

    def steps(self):
        return range(max(len(self.units), 1))


def stream(engine, group):
    group(Group("start", 0))
    group(Group("ahead", 1))
    with engine.Fori(1, AHEAD // 2) as p:
        for c in range(2):
            group(Group("ahead", c, p))
    with engine.Fori(AHEAD // 2, GROUPS // 2) as p:
        for c in range(2):
            group(Group("full", c, p))
    group(Group("last", GROUPS))


def decoder_layer(nc, x_rows, x_cols, c_cols, pos_cols, w_ada, b_ada_cols, w_xbc, w_kvdt, w_qz, conv_w, conv_b,
                  dt_bias, a_log, d_skip, norm_w, sinks, w_out, ln1_g, ln1_b, w_q, keys, u_units, u_tab, v_tab,
                  ln2_g, ln2_b, out):
    with ExitStack() as ctx:
        def sb(name, shape, dt=F32):
            return ctx.enter_context(nc.sbuf_tensor(name, shape, dt))

        def sem(name):
            return ctx.enter_context(nc.semaphore(name))

        taken = {}

        def at(off, *dims, base=None):
            n = math.prod(dims)
            flat = (arena if base is None else base)[:, off:off + n]
            if len(dims) == 1:
                return flat
            names = "abcd"[:len(dims)]
            return flat.rearrange(f"p ({' '.join(names)}) -> p {' '.join(names)}", **dict(zip(names[1:], dims[1:])))

        def place(region, off, *dims):
            start = taken.get(region, off)
            taken[region] = start + math.prod(dims)
            return at(start, *dims)

        ident = sb("ident", [P, P])
        tri = sb("tri", [P, P])
        ones = sb("ones", [P, P])
        band = sb("band", [P, 2 * P])
        mask_now = sb("mask_now", [P, 2 * P])
        iota = sb("iota", [P, NKEY])
        c_act = sb("c_act", [P, KT])
        c_tmp = sb("c_tmp", [P, KT])
        mod_cols = sb("mod_cols", [P, MODS * KT])
        b_cols = sb("b_cols", [P, MODS * KT])
        convw = sb("convw", [P, XT * CONV])
        convb = sb("convb", [P, XT])
        normw = sb("normw", [P, AW // P])
        dtb = sb("dtb", [P, HEADS])
        a_neg = sb("a_neg", [P, HEADS])
        dskip = sb("dskip", [P, HEADS])
        sink = sb("sink", [P, HEADS])
        pos_i = sb("pos_i", [P, TB], I32)
        inv = sb("inv", [P, NF])
        ang = sb("ang", [P, 2, TB, NF])
        turns = sb("turns", [P, 2, TB, NF])
        trig = sb("trig", [P, 2, TB, NF])
        dt_all = sb("dt_all", [P, TB, HEADS])
        da_all = sb("da_all", [P, TB, HEADS])
        dt_abs = sb("dt_abs", [P, TB, HEADS])
        var = sb("var", [P, KV])
        root = sb("root", [P, KV])
        root_t = sb("root_t", [P, KV])

        with nc.sbuf_tensor("arena", [P, ARENA], F32) as arena:
            pass
        below_parts = sb("below_parts", [P, PARTS])
        w_parts = sb("w_parts", [P, 2, 2, GT, DT], F32R)
        split = sb("split", [P, 2, 2, UNIT], F32R)
        h2_parts = sb("h2_parts", [P, 2, KT, DT], F32R)
        sb("above_parts", [P, ARENA - LATE])
        gates_out = nc.dram_tensor("gates_by_expert", (P, DT // TG, NKEY, TG), F32, kind="Internal").ap()
        acts_out = nc.dram_tensor("acts_ahead", (AHEAD * GT, P, DT), F32, kind="Internal").ap()
        x1_out = nc.dram_tensor("x1_rows", (P, TB, D), F32, kind="Internal").ap()

        ps = ctx.enter_context(nc.psum_tensor("ps", [P, 8, 512], F32))

        def bank(i, n=1):
            return ps[:, i, :] if n == 1 else ps[:, i:i + n, :]

        def wide(i, *dims):
            flat = ps[:, :, :].rearrange("p b n -> p (b n)")[:, 512 * i:512 * i + math.prod(dims)]
            names = "abcd"[:len(dims)]
            return flat.rearrange(f"p ({' '.join(names)}) -> p {' '.join(names)}", **dict(zip(names[1:], dims[1:])))

        h_t = at(HT, KT, S)
        win = at(WIN, 2, KT // 2, 512)
        ada = at(ADA, 4, D)
        acc = at(ACC, D)
        qz = at(QZ, TB, 2 * AW)
        kvdt = at(KVDT, TB, KVW + HEADS)
        x_raw = at(XRAW, XT, S + CONV - 1)
        x_conv = at(XCONV, XT, S)

        cur = place("a", WIN, XT, P)
        qk = place("a", WIN, HEADS + KV, HD)
        kdup = place("a", WIN, KV, 2, HD)
        q_t = place("a", WIN, HEADS // 2, P)
        k_t = place("a", WIN, KV, 2 * P)
        vv = place("a", WIN, 2, KV * HD)
        lg = place("a", WIN, 2, 2, 2, 2 * P)
        p_t = place("a", WIN, 2, 8, P)
        y_row = place("a", WIN, 2 * AW)
        xs_row = place("a", WIN, HEADS, HD)
        b_row = place("a", WIN, KV, P)
        cbm = place("a", WIN, KV, P)
        assert taken["a"] <= WT
        xdt = place("b", XRAW, HEADS, HD)
        xw = place("b", XRAW, HEADS, HD)
        m_t = place("b", XRAW, HEADS, P)
        state = place("b", XRAW, HEADS, HD)
        tmp = place("b", XRAW, HEADS, HD)
        assert taken["b"] <= XCONV
        decay = place("c", SPARE, 2, 4, P)
        rope_tmp = place("c", SPARE, 4, HEADS + KV, NF)
        trig_now = place("c", SPARE, 2, NF)
        mx = place("c", SPARE, 2, 4)
        es = place("c", SPARE, 2, 4)
        den = place("c", SPARE, 2, 4)
        da_now = place("c", SPARE, HEADS)
        acum = place("c", SPARE, HEADS)
        alast = place("c", SPARE, HEADS)
        dte = place("c", SPARE, HEADS)
        ea = place("c", SPARE, HEADS)
        cdec = place("c", SPARE, HEADS)
        ss = place("c", SPARE, KV)
        assert taken["c"] <= QZ
        y_t = at(HT, KT, S)

        wt = at(WT, 4, 1024)
        wt_q = at(WT, 4, 1024, base=below_parts)
        g1b, sc2b, sh2b = (at(WIN + i * D, D) for i in range(3))
        h2 = at(WIN + 3 * D, TB, D)
        tmp2 = at(SPARE, D)
        x1 = at(QZ, TB, D)
        ln1gb, ln1bb = (at(XRAW + i * D, D) for i in range(2))
        late = LATE
        ids = place("d", late, TB, PICKS).bitcast(U32)
        gates = place("d", late, TB, PICKS)
        key_t = place("d", late, NKEY)
        stats = place("d", late, 4, 6)
        mv = place("d", late, 2)
        act4 = place("d", late, SLOTS)
        w4 = place("d", late, SLOTS)
        idx = place("d", late, SLOTS).bitcast(U32)
        assert taken["d"] <= ARENA
        h2_t = at(HT, KT, S, base=below_parts)

        sc = at(HT, 2, PH, NKEY)
        cand = at(HT + 4 * K, PH, PK, PK)
        hits = at(HT + 6 * K, PH, PK, PK)
        q8 = at(WIN, PH, S)
        top_v = place("e", WIN + 4 * K, 2, PH, PK)
        top_i = place("e", WIN + 4 * K, 2, PH, PK).bitcast(U32)
        top_f = place("e", WIN + 4 * K, 2, PH, PK)
        rest = place("e", WIN + 4 * K, NKEY)
        pair_v = place("e", WIN + 4 * K, PH, PK)
        pair_i = place("e", WIN + 4 * K, PH, PK).bitcast(U32)
        part_u = place("e", WIN + 4 * K, 2, PH, PK).bitcast(U32)
        part_f = place("e", WIN + 4 * K, 2, PH, PK)
        part_id = place("e", WIN + 4 * K, 2, PH, PK)
        pick_sum = place("e", WIN + 4 * K, PH)
        assert taken["e"] <= WIN + 6 * K

        one_hot = at(SPREAD, 2, 2, OH, NKEY)
        pick_cols = at(SPREAD + 4 * OH * NKEY, 3, DT)
        stage = at(STAGE, 2, NKEY, TG)
        gm = at(GM, 2, DT // TG, GT * TG, base=below_parts)
        pre_gel = at(SPREAD + 4 * OH * NKEY + 3 * DT, 2, DT)
        assert SPREAD + 4 * OH * NKEY + 5 * DT <= 20 * K and STAGE + 2 * NKEY * TG <= PARTS + WP
        pre_raw = wt_q
        raw = at(RAW, RAWS, UNIT, base=below_parts)
        gel = at(GEL, 2, DT, base=below_parts)
        h2_t_dense = h2_t[:, :, 0:DT]
        out4 = at(OUT4, TB, D)
        acc_v = out4[:, DB, :]
        h2_now = h2[:, DB, :]
        ring = [at(o, D) for o in (RING, RING + D, WT, WT + D)]
        assert RING + 2 * D <= WIN + 3 * D + DB * D
        g2b = at(GM, D)
        x1_back = at(PARTS + WP + SP_, TB, D)
        ln2gb, ln2bb = (at(PARTS + WP + SP_ + (TB + i) * D, D) for i in range(2))

        small_loaded = sem("small_loaded")
        c_loaded = sem("c_loaded")
        x_loaded = sem("x_loaded")
        ada_full = [sem(f"ada_full{i}") for i in range(4)]
        ada_used = sem("ada_used")
        win_full = [sem(f"win_full{i}") for i in range(2)]
        win_used = sem("win_used")
        consts = sem("consts")
        consts2 = sem("consts2")
        c_exp = sem("c_exp")
        ang_ready = sem("ang_ready")
        trig_ready = sem("trig_ready")
        mod_sum = sem("mod_sum")
        mod_ready = sem("mod_ready")
        h_ready = sem("h_ready")
        proj_done = sem("proj_done")
        proj_bank_free = sem("proj_bank_free")
        proj_out = sem("proj_out")
        conv_ready = sem("conv_ready")
        silu_done = sem("silu_done")
        dve_own = sem("dve_own")
        act_own = sem("act_own")
        names = (
            "dt_in dt_log a_exp block_in qt_ps kb_ps cb_ps xs_ps q_ready xs_ready kv_ready lg_done lg_read mx_ready "
            "exp_done pt_ps pt_ready pv_done att_out ssd_small ssd_exp xw_ready seg_ps seg_read seg_in seg_exp m_ready "
            "y_ps st_ps state_new y_gated ss_ready y_rows yt_ps yt_act yt_dve mix_start "
            "row_ps row_ready wt_used mix_ps mix_read x1_loaded ln1_loaded key_loaded h2_ready h2t_ps h2t_ready q_ps "
            "q8_ready sc_ps sc_ready sc_used pair_sub pair_exp topk_done row_used idx_copied dots_done gelu_done "
            "x1_stored h2_high h2_split parts_read cols_ps cols_ready spread hot_gated hot_ready g_ps g_staged "
            "pre_high pre_split pre_used pre_gelu high_done unit_split unit_used tile_gelu w_made w_high w_ready v_read picks_w tail_loaded tail_row tail_row_ready "
            "y_ready out_done z_done held idx_held var_ready root_ready"
        )
        (dt_in, dt_log, a_exp, block_in, qt_ps, kb_ps, cb_ps, xs_ps, q_ready, xs_ready, kv_ready, lg_done, lg_read, mx_ready,
         exp_done, pt_ps, pt_ready, pv_done, att_out, ssd_small, ssd_exp, xw_ready, seg_ps, seg_read, seg_in, seg_exp, m_ready,
         y_ps, st_ps, state_new, y_gated, ss_ready, y_rows, yt_ps, yt_act, yt_dve, mix_start,
         row_ps, row_ready, wt_used, mix_ps, mix_read, x1_loaded, ln1_loaded, key_loaded, h2_ready, h2t_ps, h2t_ready, q_ps,
         q8_ready, sc_ps, sc_ready, sc_used, pair_sub, pair_exp, topk_done, row_used, idx_copied, dots_done, gelu_done,
         x1_stored, h2_high, h2_split, parts_read, cols_ps, cols_ready, spread, hot_gated, hot_ready, g_ps, g_staged,
         pre_high, pre_split, pre_used, pre_gelu, high_done, unit_split, unit_used, tile_gelu, w_made, w_high, w_ready, v_read, picks_w, tail_loaded, tail_row, tail_row_ready,
         y_ready, out_done, z_done, held, idx_held, var_ready, root_ready) = map(sem, names.split())
        wt_full = [sem(f"wt_full{i}") for i in range(4)]
        ring_full = [sem(f"ring_full{i}") for i in range(SLOTS)]
        g_stored = [sem(f"g_stored{i}") for i in range(2)]
        pre_full = [sem(f"pre_full{i}") for i in range(RAWS)]
        acts_stored = [sem(f"acts_stored{i}") for i in range(2)]
        gel_full = [sem(f"gel_full{i}") for i in range(2)]
        raw_full = [sem(f"raw_full{i}") for i in range(RAWS)]
        gm_full = [sem(f"gm_full{i}") for i in range(2)]

        block = ctx.enter_context(nc.Block())

        @block.sync
        def _(sp):
            sp.dma_start(c_tmp[:, :], c_cols[:, :]).then_inc(c_loaded, 16)
            for to, what in ((b_cols, b_ada_cols), (convw, conv_w), (convb, conv_b), (normw, norm_w), (pos_i, pos_cols)):
                sp.dma_start(to[:, :], what[:, :]).then_inc(small_loaded, 16)
            for to, what in ((dtb, dt_bias), (a_neg, a_log), (dskip, d_skip), (sink, sinks)):
                sp.dma_start(to[:, :], what[0:1, :].to_broadcast([P, HEADS])).then_inc(small_loaded, 16)

            def ada_tiles(m):
                for k in range(KT):
                    if not (isinstance(m, int) and k < 4):
                        sp.wait_ge(ada_used, m * KT + k - 3)
                    sp.dma_start(ada[:, k % 4, :], w_ada[k * P:(k + 1) * P, bass.ts(m, D)]).then_inc(ada_full[k % 4], 16)

            ada_tiles(0)
            sp.dma_start(h_t, x_cols[:, :, :]).then_inc(x_loaded, 16)
            with sp.Fori(1, MODS) as m:
                ada_tiles(m)

            def weights(slot, what, wait, to=wt):
                if wait is not None:
                    sp.wait_ge(wt_used, wait)
                sp.dma_start(to[:, slot, :], what).then_inc(wt_full[slot], 16)

            sp.wait_ge(mod_ready, MODS)
            for slot in range(4):
                weights(slot, w_out[slot, :, :], None)
            sp.wait_ge(yt_dve, TB)
            sp.wait_ge(yt_act, TB)
            sp.dma_start(x1, x_rows.rearrange("(b p) d -> p b d", p=P)).then_inc(x1_loaded, 16)
            for to, what in ((ln1gb, ln1_g), (ln1bb, ln1_b)):
                sp.dma_start(to, what[0:1, :].to_broadcast([P, D])).then_inc(ln1_loaded, 16)
            sp.dma_start(key_t, keys[:, :]).then_inc(key_loaded, 16)
            with sp.Fori(1, 8) as i:
                for slot in range(4):
                    weights(slot, w_out[bass.ds(i * 4 + slot, 1), :, :].rearrange("a p n -> (a p) n"), i * 4 + (slot - 3))
            with sp.Fori(0, 4) as i:
                for slot in range(4):
                    weights(slot, w_q[bass.ds(i * 4 + slot, 1), :, :].rearrange("a p n -> (a p) n"), i * 4 + (slot + 29), wt_q)
            sp.wait_ge(h2_ready, TB)
            sp.dma_start(x1_out[:, :, :], x1).then_inc(x1_stored, 16)
            sp.wait_ge(q_ps, PH)
            sp.sem_inc(pre_split, RAWS)
            for m in range(TB):
                with sp.Fori(0, WIN_PAIRS) as i:
                    for j in range(4):
                        sp.wait_ge(pre_split, i * 4 + (m * WIN_UNITS + j + 1))
                        sp.dma_start(pre_raw[:, j, :], u_units[bass.ds(i * 4 + (m * WIN_UNITS + j), 1), :, :].rearrange("a p n -> (a p) n"))\
                            .then_inc(pre_full[j], 16)
                if m:
                    for n in range((m - 1) * P // TG, m * P // TG):
                        sp.wait_ge(g_staged, 2 + (n + 1) * TG // 4)
                        sp.dma_start(gates_out[:, n, :, :], stage[:, n % 2, :, :]).then_inc(g_stored[n % 2], 16)
            for i in range(2):
                sp.wait_ge(g_stored[i], 16 * (1 + DT // TG // 2))
                sp.wait_ge(acts_stored[i], 16 * (1 + AHEAD * GT // 2))
            sp.wait_ge(x1_stored, 16)
            sp.wait_ge(topk_done, TB)
            v_tiles = v_tab.rearrange("(a b) d -> b a d", b=NKEY)

            def read_back(g, i):
                if not (g.kind == "start" and i < 2):
                    sp.wait_ge(w_ready, g.val(GT, i - 1))
                sp.dma_start(gel[:, i % 2, :], acts_out[bass.ds(g.val(GT, i), 1), :, :].rearrange("a p n -> (a p) n"))\
                    .then_inc(gel_full[i % 2], 16)

            def group(g):
                if g.kind != "last":
                    if not (g.kind == "start" or g.second):
                        sp.wait_ge(w_made, g.val(GT, -GT))
                    buf = g.c % 2
                    sp.dma_start(gm[:, buf, :, :], gates_out[:, :, bass.ds(g.val(GT), GT), :].rearrange("p a b c -> p a (b c)"))\
                        .then_inc(gm_full[buf], 16)
                if g.kind == "start":
                    for i in range(GT):
                        read_back(g, i)
                for j, (table, i, half) in enumerate(g.units):
                    if g.kind == "ahead" and j % 2 == 0:
                        read_back(g, j // 2)
                    slot = j % RAWS
                    if not (g.second and j < RAWS):
                        sp.wait_ge(unit_split, g.unit(j - RAWS + 1))
                    if table == "u":
                        what = u_units[bass.ds(g.val(2 * GT, 2 * i + half), 1), :, :]
                    else:
                        what = v_tiles[bass.ds(g.val(GT, i - GT), 1), :, half * UNIT:(half + 1) * UNIT]
                    sp.dma_start(raw[:, slot, :], what.rearrange("a p n -> (a p) n")).then_inc(raw_full[slot], 16)

            stream(sp, group)
            sp.wait_ge(unit_used, Group("last", GROUPS).unit(0))
            sp.dma_start(x1_back, x1_out[:, :, :]).then_inc(tail_loaded, 16)
            for to, what in ((ln2gb, ln2_g), (ln2bb, ln2_b)):
                sp.dma_start(to, what[0:1, :].to_broadcast([P, D])).then_inc(tail_loaded, 16)
            for m in range(TB):
                sp.wait_ge(y_ready, m + 1)
                sp.dma_start(out[m * P:(m + 1) * P, :], out4[:, m, :]).then_inc(out_done, 16)
            sp.wait_ge(out_done, 16 * TB)

        @block.gpsimd
        def _(pool):
            def win_half(half, what, cols, slices):
                if slices is not None:
                    pool.wait_ge(*((proj_done, slices * 4) if half else (win_used, slices)))
                pool.dma_start(win[:, half, :, 0:cols], what).then_inc(win_full[half], 16)

            for half in range(2):
                win_half(half, w_xbc[0, :, half * 8:half * 8 + 8, :], 512, None)
            nc.gpsimd.memset(ones[:, :], 1.0).then_inc(consts, 1)
            nc.gpsimd.memset(ident[:, :], 0.0).then_inc(consts, 1)
            nc.gpsimd.memset(band[:, :], 0.0).then_inc(consts, 1)
            nc.gpsimd.memset(x_raw[:, :, 0:CONV - 1], 0.0).then_inc(consts, 1)
            for f in range(NF):
                nc.gpsimd.memset(inv[:, f:f + 1], float(THETA ** (-2.0 * f / ROT))).then_inc(consts, 1)
            nc.gpsimd.iota(iota[:, :], pattern=[[1, NKEY]], base=0, channel_multiplier=0,
                           allow_small_or_imprecise_dtypes=True).then_inc(consts, 1)
            pool.wait_ge(consts, 13)
            nc.gpsimd.affine_select(out=tri[:, :], in_=ones[:, :], compare_op=ALU.is_ge, fill=0.0, base=0,
                                    pattern=[[1, P]], channel_multiplier=-1).then_inc(consts2, 1)
            nc.gpsimd.affine_select(out=ident[:, :], in_=ident[:, :], compare_op=ALU.not_equal, fill=1.0, base=0,
                                    pattern=[[-1, P]], channel_multiplier=1).then_inc(consts2, 1)
            nc.gpsimd.affine_select(out=band[:, :], in_=band[:, :], compare_op=ALU.is_gt, fill=NEG, base=0,
                                    pattern=[[1, 2 * P]], channel_multiplier=-1).then_inc(consts2, 1)
            pool.wait_ge(consts2, 3)
            nc.gpsimd.affine_select(out=band[:, :], in_=band[:, :], compare_op=ALU.is_ge, fill=NEG, base=P,
                                    pattern=[[-1, 2 * P]], channel_multiplier=1).then_inc(consts2, 1)
            pool.wait_ge(consts2, 4)
            nc.gpsimd.memset(mask_now[:, 0:P], NEG).then_inc(consts2, 1)
            nc.gpsimd.tensor_copy(mask_now[:, P:2 * P], band[:, P:2 * P]).then_inc(consts2, 1)

            with pool.Fori(1, 3) as n:
                for half in range(2):
                    win_half(half, w_xbc[bass.ds(n, 1), :, half * 8:half * 8 + 8, :].rearrange("a p k n -> (a p) k n"),
                             512, n)
            for half in range(2):
                win_half(half, w_kvdt[:, half * 8:half * 8 + 8, :], KVW + HEADS, 3)
            with pool.Fori(0, 4) as n:
                for half in range(2):
                    win_half(half, w_qz[bass.ds(n, 1), :, half * 8:half * 8 + 8, :].rearrange("a p k n -> (a p) k n"),
                             512, n + 4)

            for m in range(TB):
                with pool.Fori(0, WIN_PAIRS) as i:
                    for j in range(4):
                        pool.wait_ge(pre_high, i * 4 + (m * WIN_UNITS + j + 1))
                        nc.gpsimd.tensor_tensor(split[:, j % 2, 1, :], pre_raw[:, j, :], split[:, j % 2, 0, :].bitcast(F32), ALU.subtract)\
                            .then_inc(pre_split, 1)
                if m:
                    with pool.Fori((m - 1) * P // (2 * OH), m * P // (2 * OH)) as i:
                        for buf in range(2):
                            pool.wait_ge(hot_ready, i * 2 + (buf + 1))
                            pool.sem_inc(spread, 1)
                            rows = one_hot[:, buf, 1, :, :]
                            nc.gpsimd.tensor_tensor(rows, rows, over(pick_cols[:, 2, bass.ds(i * (2 * OH) + buf * OH, OH)], 2, NKEY), ALU.mult)\
                                .then_inc(hot_gated, 1)

            pool.wait_ge(topk_done, TB)
            pool.wait_ge(g_ps, DT // 4 + 2 * OH // 4)
            pool.wait_ge(pre_split, AHEAD * GT * 2 + RAWS)
            for i in range(2):
                pool.wait_ge(acts_stored[i], 16 * (1 + AHEAD * GT // 2))
            with pool.Fori(0, GROUPS) as i:
                for t, table in enumerate((u_tab, v_tab)):
                    for slot in range(SLOTS):
                        count = i * (2 * SLOTS) + (t * SLOTS + slot + 1)
                        pool.wait_ge(row_used, count)
                        pool.sem_inc(idx_held, 1)
                        nc.gpsimd.tensor_copy(idx[:, slot:slot + 1], ids[:, DB, bass.ds(i * SLOTS + slot, 1)]).then_inc(idx_copied, 1)
                        pool.wait_ge(idx_copied, count)
                        pool.sem_inc(idx_held, 1)
                        nc.gpsimd.indirect_dma_start(
                            out=ring[slot], out_offset=None, in_=table[:, :],
                            in_offset=bass.IndirectOffsetOnAxis(ap=idx[:, slot:slot + 1], axis=0),
                        ).then_inc(ring_full[slot], 16)

        @block.scalar
        def _(act):
            own = Steps(act, act_own)
            act.wait_ge(c_loaded, 16)
            nc.scalar.activation(c_act[:, :], c_tmp[:, :], ACT.Exp, scale=-1.0).then_inc(c_exp, 1)
            act.wait_ge(ang_ready, 1)
            nc.scalar.activation(trig[:, :, :, :].rearrange("p a b c -> p (a b c)"),
                                 ang[:, :, :, :].rearrange("p a b c -> p (a b c)"), ACT.Sin).then_inc(trig_ready, 1)
            act.sem_inc(proj_bank_free, 4)
            with act.Fori(0, 3) as n:
                for m in range(4):
                    act.wait_ge(proj_done, n * 4 + (m + 1))
                    nc.scalar.activation(x_raw[:, bass.ds(n * 4 + m, 1), CONV - 1:].rearrange("p a s -> p (a s)"), bank(m), ACT.Copy)\
                        .then_inc(proj_bank_free, 1)
            for m in range(4):
                act.wait_ge(proj_done, 12 + m + 1)
                nc.scalar.activation(kvdt[:, m, :], ps[:, m, 0:KVW + HEADS], ACT.Copy).then_inc(proj_bank_free, 1)
            for n in range(3):
                act.wait_ge(conv_ready, n + 1)
                part = x_conv[:, 4 * n:4 * n + 4, :]
                nc.scalar.activation(part, part, ACT.Silu).then_inc(silu_done, 1)
            with act.Fori(0, 4) as n:
                for m in range(4):
                    act.wait_ge(proj_done, n * 4 + (16 + m + 1))
                    nc.scalar.activation(qz[:, m, bass.ts(n, 512)], bank(m), ACT.Copy).then_inc(proj_bank_free, 1)
            act.wait_ge(proj_bank_free, 4 + 32)
            gate = qz[:, :, AW:]
            nc.scalar.activation(gate, gate, ACT.Silu).then_inc(z_done, 1)
            act.wait_ge(dt_in, 1)
            own(nc.scalar.activation(dt_abs[:, :, :], dt_abs[:, :, :], ACT.Exp, scale=-1.0))
            nc.scalar.activation(dt_abs[:, :, :], dt_abs[:, :, :], ACT.Ln, bias=1.0).then_inc(dt_log, 1)
            nc.scalar.activation(a_neg[:, :], a_neg[:, :], ACT.Exp).then_inc(a_exp, 1)

            def roots(n):
                act.wait_ge(var_ready, n + 1)
                nc.scalar.activation(root[:, :], var[:, :], ACT.Ln).then_inc(act_own, 1)
                act.wait_ge(act_own, n + 2)
                nc.scalar.activation(root[:, :], root[:, :], ACT.Exp, scale=-0.5).then_inc(root_ready, 1)

            def exps(b, u):
                act.wait_ge(mx_ready, b * 4 + (u + 1))
                nc.scalar.activation(es[:, u % 2, :], es[:, u % 2, :], ACT.Exp)
                for i in range(4):
                    row = lg[:, u % 2, i // 2, i % 2, :]
                    ins = nc.scalar.activation(row, row, ACT.Exp, bias=mx[:, u % 2, i:i + 1], accum_out=den[:, u % 2, i:i + 1])
                ins.then_inc(exp_done, 1)

            def p_turned(b, u):
                act.wait_ge(pt_ps, b * 4 + (u + 1))
                nc.scalar.activation(p_t[:, u % 2, :, :], wide(2, 8, P), ACT.Copy).then_inc(pt_ready, 1)

            with act.Fori(0, TB) as b:
                act.wait_ge(qt_ps, b + 1)
                nc.scalar.activation(q_t, wide(2, HEADS // 2, P), ACT.Copy).then_inc(q_ready, 1)
                act.wait_ge(xs_ps, b + 1)
                nc.scalar.activation(xs_row, wide(4, HEADS, HD), ACT.Copy).then_inc(xs_ready, 1)
                act.wait_ge(ssd_small, b + 1)
                nc.scalar.activation(ea, acum, ACT.Exp)
                nc.scalar.activation(cdec, alast, ACT.Exp)
                nc.scalar.activation(dte, dte, ACT.Exp).then_inc(ssd_exp, 1)
                exps(b, 0)
                exps(b, 1)
                p_turned(b, 0)
                exps(b, 2)
                p_turned(b, 1)
                exps(b, 3)
                p_turned(b, 2)
                p_turned(b, 3)
                for c in range(4):
                    act.wait_ge(seg_in, b * 4 + (c + 1))
                    nc.scalar.activation(decay[:, c % 2, :, :], decay[:, c % 2, :, :], ACT.Exp).then_inc(seg_exp, 1)
                act.wait_ge(yt_ps, b * 2 + 1)
                nc.scalar.activation(y_t[:, 0:8, bass.ts(b, P)], wide(0, 8, P), ACT.Copy).then_inc(yt_act, 1)
                act.wait_ge(y_gated, b + 1)
                for g in range(KV):
                    ins = nc.scalar.activation(decay[:, g, :, :], tmp[:, g * GH:(g + 1) * GH, :].rearrange("p a b -> p (a b)")
                                               .rearrange("p (a b) -> p a b", b=P), ACT.Square, accum_out=ss[:, g:g + 1])
                ins.then_inc(ss_ready, 1)
                roots(b)

            for i, row in enumerate((g1b, sc2b, sh2b)):
                act.wait_ge(row_ps, i + 1)
                nc.scalar.activation(row, wide(4 * (i % 2), D), ACT.Copy).then_inc(row_ready, 1)
            for m in range(TB + 1):
                if m < TB:
                    roots(TB + m)
                if m:
                    act.wait_ge(h2t_ps, m)
                    nc.scalar.activation(h2_t[:, :, (m - 1) * P:m * P], wide(4 * ((m - 1) % 2), KT, P), ACT.Copy).then_inc(h2t_ready, 1)
            act.wait_ge(h2t_ready, TB)
            nc.scalar.activation(h2_parts[:, 0, :, :], h2_t_dense, ACT.Copy).then_inc(h2_high, 1)
            for h in range(PH):
                act.wait_ge(q_ps, h + 1)
                nc.scalar.activation(q8[:, h, :], bank(h), ACT.Copy).then_inc(q8_ready, 1)
            act.wait_ge(h2_split, 1)
            act.sem_inc(g_stored[0], 16)
            act.sem_inc(g_stored[1], 16)
            act.wait_ge(x1_stored, 16)

            def scores(m):
                act.wait_ge(sc_ps, m + 1)
                if m:
                    act.wait_ge(sc_used, m)
                nc.scalar.activation(sc, wide(0, 2, PH, NKEY), ACT.Copy).then_inc(sc_ready, 1)

            def gates_by_expert(m):
                with act.Fori(0, P // (2 * TG)) as i:
                    for st in range(2):
                        act.wait_ge(g_stored[st], i * 16 + 16 * (m * (P // TG // 2) + 1))
                        for q in range(TG // 4):
                            act.wait_ge(g_ps, i * (2 * TG // 4) + (m * P + st * TG) // 4 + (2 * OH // 4 + q + 1))
                            nc.scalar.activation(stage[:, st, :, 4 * q:4 * q + 4], wide(4 + q % 2, 4, NKEY).rearrange("p t i -> p i t"), ACT.Copy)\
                                .then_inc(g_staged, 1)

            def ahead(m):
                def gelu(i, b):
                    tiles = i * 2 + (m * 2 * WIN_PAIRS + b + 1)
                    act.wait_ge(pre_used, i * 4 + (m * WIN_UNITS + 2 * b + 2 + 2))
                    act.wait_ge(acts_stored[b], i * 16 + 16 * (m * WIN_PAIRS + 1))
                    nc.scalar.activation(pre_gel[:, b, :], ps[:, 6 + b, 0:DT], ACT.Gelu).then_inc(pre_gelu, 1)
                    act.wait_ge(pre_gelu, tiles + 2)
                    act.dma_start(acts_out[bass.ds(tiles - 1, 1), :, :].rearrange("a p n -> (a p) n"), pre_gel[:, b, :])\
                        .then_inc(acts_stored[b], 16)

                def pair(i, first):
                    for j in range(4):
                        act.wait_ge(pre_full[j], i * 16 + 16 * (m * WIN_PAIRS + 1))
                        act.wait_ge(pre_used, i * 4 + (m * WIN_UNITS + j + 1))
                        nc.scalar.activation(split[:, j % 2, 0, :], pre_raw[:, j, :], ACT.Copy).then_inc(pre_high, 1)
                        if j == 1 and not first:
                            gelu(i - 1, 1)
                        if j == 3:
                            gelu(i, 0)

                pair(0, True)
                with act.Fori(1, WIN_PAIRS) as i:
                    pair(i, False)
                gelu(WIN_PAIRS - 1, 1)

            act.sem_inc(pre_used, 2)
            for i in range(2):
                act.sem_inc(acts_stored[i], 16)
            scores(0)
            for m in range(TB):
                ahead(m)
                act.wait_ge(pair_sub, m + 1)
                nc.scalar.activation(pair_v, pair_v, ACT.Exp).then_inc(pair_exp, 1)
                if m + 1 < TB:
                    scores(m + 1)
                    act.wait_ge(cols_ps, m + 1)
                    nc.scalar.activation(pick_cols[:, :, m * P:(m + 1) * P], ps[:, 6, 0:3 * P].rearrange("p (a b) -> p a b", a=3), ACT.Copy)\
                        .then_inc(cols_ready, 1)
                if m:
                    gates_by_expert(m - 1)

            def group(g):
                buf = g.c % 2
                for j in g.steps():
                    if g.units:
                        act.wait_ge(raw_full[j % RAWS], g.unit(0) * 4 + (16 * (j // RAWS + 1)))
                        if not (g.second and j < 2):
                            act.wait_ge(unit_used, g.unit(j - 1))
                        nc.scalar.activation(split[:, j % 2, 0, :], raw[:, j % RAWS, :], ACT.Copy).then_inc(high_done, 1)
                    if j == 1:
                        act.wait_ge(dots_done, g.val(1))
                        nc.scalar.activation(act4, act4, ACT.Gelu).then_inc(gelu_done, 1)
                    for i, due in g.tiles_at(j):
                        if due == "gelu":
                            act.wait_ge(unit_used, g.unit(g.units.index(("u", i, 1)) + 1))
                            act.wait_ge(w_ready, g.val(GT, i - 1))
                            nc.scalar.activation(gel[:, i % 2, :], ps[:, 6 + i % 2, 0:DT], ACT.Gelu).then_inc(tile_gelu, 1)
                        if due == "high":
                            act.wait_ge(w_made, g.val(GT, i + 1))
                            nc.scalar.activation(w_parts[:, buf, 0, i, :], gel[:, i % 2, :], ACT.Copy).then_inc(w_high, 1)

            stream(act, group)
            for half in range(2):
                act.wait_ge(tail_row, half + 1)
                nc.scalar.activation(g2b[:, half * 1024:(half + 1) * 1024], wide(6, 1024), ACT.Copy).then_inc(tail_row_ready, 1)
            with act.Fori(0, TB) as m:
                roots(m + 2 * TB)

        @block.vector
        def _(dve):
            own = Steps(dve, dve_own)
            dve.wait_ge(c_exp, 1)
            own(nc.vector.tensor_scalar(c_act[:, :], c_act[:, :], 1.0, None, ALU.add))
            own(nc.vector.reciprocal(c_act[:, :], c_act[:, :]))
            own(nc.vector.tensor_tensor(c_act[:, :], c_act[:, :], c_tmp[:, :], ALU.mult))

            dve.wait_ge(small_loaded, 9 * 16)
            dve.wait_ge(consts, 13)
            ang0 = ang[:, 0, :, :].rearrange("p a b -> p (a b)")
            ang1 = ang[:, 1, :, :].rearrange("p a b -> p (a b)")
            tn = turns[:, 0, :, :].rearrange("p a b -> p (a b)")
            tn1 = turns[:, 1, :, :].rearrange("p a b -> p (a b)")
            pos_f = turns[:, 1, :, 0]
            own(nc.vector.tensor_copy(pos_f, pos_i[:, :]))
            own(nc.vector.tensor_tensor(ang[:, 0, :, :], over(pos_f, 2, NF), over(inv[:, :], 1, TB), ALU.mult))
            own(nc.vector.tensor_scalar(tn, ang0, 1.0 / (2 * math.pi), None, ALU.mult))
            own(nc.vector.tensor_scalar(tn, tn, 12582912.0, None, ALU.add))
            own(nc.vector.tensor_scalar(tn, tn, -12582912.0, None, ALU.add))
            two_pi, part = 2 * math.pi, 6.28125
            part2 = round((two_pi - part) * 2 ** 19) / 2 ** 19
            for piece in (part, part2, two_pi - part - part2):
                own(nc.vector.scalar_tensor_tensor(ang0, tn, -piece, ang0, ALU.mult, ALU.add))
            own(nc.vector.tensor_scalar(ang1, ang0, math.pi / 2, None, ALU.add))
            own(nc.vector.tensor_scalar(tn1, ang1, math.pi, -two_pi, ALU.is_gt, ALU.mult))
            own(nc.vector.tensor_tensor(ang1, ang1, tn1, ALU.add))
            both = ang[:, :, :, :].rearrange("p a b c -> p (a b c)")
            nc.vector.tensor_scalar(both, both, 3.1415925, -3.1415925, ALU.min, ALU.max).then_inc(ang_ready, 1)
            for m in (1, 4):
                part = b_cols[:, m * KT:(m + 2) * KT]
                own(nc.vector.tensor_scalar(part, part, 1.0, None, ALU.add))

            def modulation(m):
                for k in range(KT):
                    dve.wait_ge(ada_full[k % 4], m * (16 * KT // 4) + 16 * (k // 4 + 1))
                    if k == 0:
                        nc.vector.tensor_scalar(acc, ada[:, 0, :], c_act[:, 0:1], None, ALU.mult).then_inc(ada_used, 1)
                    else:
                        dve.wait_ge(ada_used, m * KT + k)
                        nc.vector.scalar_tensor_tensor(acc, ada[:, k % 4, :], c_act[:, k:k + 1], acc, ALU.mult, ALU.add)\
                            .then_inc(ada_used, 1)
                dve.wait_ge(mod_sum, m + 1)
                nc.vector.tensor_tensor(mod_cols[:, bass.ts(m, KT)], ps[:, 4, 0:KT], b_cols[:, bass.ts(m, KT)], ALU.add)\
                    .then_inc(mod_ready, 1)

            with dve.Fori(0, 2) as m:
                modulation(m)
            dve.wait_ge(mod_ready, 2)
            dve.wait_ge(x_loaded, 16)
            for k in range(KT):
                nc.vector.tensor_scalar(h_t[:, k, :], h_t[:, k, :], mod_cols[:, KT + k:KT + k + 1], mod_cols[:, k:k + 1],
                                        ALU.mult, ALU.add).then_inc(h_ready, 1)

            with dve.Fori(0, 3) as n:
                modulation(n + 2)
                dve.wait_ge(proj_bank_free, n * 4 + 8)
                for m in range(4):
                    tile = n * 4 + m
                    src = x_raw[:, bass.ds(tile, 1), :].rearrange("p a s -> p (a s)")
                    dst = x_conv[:, bass.ds(tile, 1), :].rearrange("p a s -> p (a s)")
                    base = own.base + own.n + n * 15 + m * 4
                    for j in range(CONV):
                        w = convw[:, bass.ds(tile * CONV + j, 1)]
                        if j == 0:
                            ins = nc.vector.tensor_scalar(dst, src[:, 0:S], w, convb[:, bass.ds(tile, 1)], ALU.mult, ALU.add)
                        else:
                            dve.wait_ge(dve_own, base + j)
                            ins = nc.vector.scalar_tensor_tensor(dst, src[:, j:j + S], w, dst, ALU.mult, ALU.add)
                        ins.then_inc(conv_ready if m == 3 and j == 3 else dve_own, 1)
            own.n += 3 * 15
            modulation(5)


            dve.wait_ge(proj_done, 32)
            nc.vector.memset(k_t, 0.0)
            nc.vector.memset(vv, 0.0)
            nc.vector.memset(state, 0.0)
            dve.wait_ge(proj_bank_free, 20)
            own(nc.vector.tensor_tensor(dt_all[:, :, :], kvdt[:, :, KVW:], over(dtb[:, :], 1, TB), ALU.add))
            nc.vector.scalar_tensor_tensor(dt_abs[:, :, :], dt_all[:, :, :], -1.0, dt_all[:, :, :], ALU.mult, ALU.max).then_inc(dt_in, 1)
            dve.wait_ge(dt_log, 1)
            own(nc.vector.scalar_tensor_tensor(dt_all[:, :, :], dt_all[:, :, :], 0.0, dt_abs[:, :, :], ALU.max, ALU.add))
            dve.wait_ge(a_exp, 1)
            own(nc.vector.scalar_tensor_tensor(da_all[:, :, :], over(a_neg[:, :], 1, TB), -1.0, dt_all[:, :, :],
                                               ALU.mult, ALU.mult))
            dve.wait_ge(silu_done, 3)
            dve.wait_ge(z_done, 1)
            dve.wait_ge(trig_ready, 1)
            dve.wait_ge(consts2, 6)

            def logits(b, u, step):
                i = u % 2
                dve.wait_ge(lg_done, b * 4 + (u + 1))
                rows = lg[:, i, :, :, :].rearrange("p a b k -> p (a b) k")
                nc.vector.scalar_tensor_tensor(rows, wide(0, 4, 2 * P), HD ** -0.5, over(mask_now[:, :], 1, 4), ALU.mult, ALU.add)\
                    .then_inc(lg_read, 1)
                dve.wait_ge(lg_read, b * 4 + (u + 1))
                step(nc.vector.tensor_reduce(mx[:, i, :], rows, AX, ALU.max))
                s4 = sink[:, 4 * u:4 * u + 4].rearrange("p (a b) -> p b a", b=2)
                m4 = mx[:, i, :].rearrange("p (b a) -> p b a", b=2)
                e4 = es[:, i, :].rearrange("p (b a) -> p b a", b=2)
                step(nc.vector.tensor_tensor(m4, m4, s4, ALU.max))
                nc.vector.tensor_tensor(e4, s4, m4, ALU.subtract)
                nc.vector.tensor_scalar(mx[:, i, :], mx[:, i, :], -1.0, None, ALU.mult).then_inc(mx_ready, 1)

            def attended(b, u, step):
                i = u % 2
                dve.wait_ge(pv_done, b * 4 + (u + 1))
                step(nc.vector.tensor_tensor(den[:, i, :], den[:, i, :], es[:, i, :], ALU.add))
                step(nc.vector.reciprocal(den[:, i, :], den[:, i, :]))
                src = ps[:, 4 + u // 2, (u % 2) * 256:(u % 2) * 256 + 256].rearrange("p (a b d) -> p a b d", a=2, b=2)
                dst = y_row[:, u * 256:u * 256 + 256].rearrange("p (a b d) -> p a b d", a=2, b=2)
                r = over(den[:, i, :].rearrange("p (b a) -> p a b", b=2), 3, HD)
                nc.vector.tensor_tensor(dst, src, r, ALU.mult).then_inc(att_out, 1)

            def segment(b, c, step):
                dve.wait_ge(seg_ps, b * 4 + (c + 1))
                d = decay[:, c % 2, :, :]
                nc.vector.tensor_tensor(d, wide(c % 2, 4, P), over(acum[:, 4 * c:4 * c + 4], 2, P), ALU.subtract)\
                    .then_inc(seg_read, 1)
                dve.wait_ge(seg_read, b * 4 + (c + 1))
                nc.vector.tensor_scalar(d, d, 0.0, None, ALU.min).then_inc(seg_in, 1)

            def mixing(b, c):
                dve.wait_ge(seg_exp, b * 4 + (c + 1))
                nc.vector.tensor_tensor(m_t[:, 4 * c:4 * c + 4, :], decay[:, c % 2, :, :], over(cbm[:, c // 2, :], 1, 4), ALU.mult)\
                    .then_inc(m_ready, 1)

            def one_over_root(n, step):
                dve.wait_ge(root_ready, n + 1)
                step(nc.vector.tensor_tensor(root_t[:, :], root[:, :], root[:, :], ALU.mult))
                step(nc.vector.tensor_tensor(root_t[:, :], root_t[:, :], var[:, :], ALU.mult))
                step(nc.vector.tensor_scalar(root_t[:, :], root_t[:, :], -0.5, 1.5, ALU.mult, ALU.add))
                step(nc.vector.tensor_tensor(root[:, :], root[:, :], root_t[:, :], ALU.mult))

            start = own.n
            MIX_STEPS = 30
            with dve.Fori(0, TB) as b:
                step = Steps(dve, dve_own, b * MIX_STEPS + start)
                nc.vector.tensor_copy(cur, x_conv[:, :, bass.ts(b, P)])
                nc.vector.tensor_copy(qk[:, 0:HEADS, :].rearrange("p a b -> p (a b)"), qz[:, bass.ds(b, 1), 0:AW].rearrange("p a b -> p (a b)"))
                nc.vector.tensor_copy(qk[:, HEADS:, :].rearrange("p a b -> p (a b)"), kvdt[:, bass.ds(b, 1), 0:KV * HD].rearrange("p a b -> p (a b)"))
                nc.vector.tensor_copy(da_now, da_all[:, bass.ds(b, 1), :].rearrange("p a b -> p (a b)"))
                step(nc.vector.tensor_copy(trig_now, trig[:, :, bass.ds(b, 1), :].rearrange("p a b c -> p a (b c)")))
                t1, t2 = qk[:, :, 0:NF], qk[:, :, NF:ROT]
                sn, cs = over(trig_now[:, 0, :], 1, HEADS + KV), over(trig_now[:, 1, :], 1, HEADS + KV)
                for i, (t, f) in enumerate(((t1, cs), (t2, sn), (t2, cs), (t1, sn))):
                    ins = nc.vector.tensor_tensor(rope_tmp[:, i, :, :], t, f, ALU.mult)
                step(ins)
                nc.vector.tensor_tensor(t1, rope_tmp[:, 0, :, :], rope_tmp[:, 1, :, :], ALU.subtract)
                step(nc.vector.tensor_tensor(t2, rope_tmp[:, 2, :, :], rope_tmp[:, 3, :, :], ALU.add))
                nc.vector.tensor_copy(k_t[:, :, 0:P], k_t[:, :, P:2 * P])
                step(nc.vector.tensor_copy(vv[:, 0, :], vv[:, 1, :]))
                nc.vector.tensor_copy(vv[:, 1, :], kvdt[:, bass.ds(b, 1), KV * HD:KVW].rearrange("p a b -> p (a b)"))
                nc.vector.tensor_copy(kdup, over(qk[:, HEADS:, :], 2, 2)).then_inc(block_in, 1)
                dve.wait_ge(kb_ps, b + 1)
                nc.vector.tensor_copy(k_t[:, :, P:2 * P], ps[:, 6, 0:256].rearrange("p (a b) -> p a b", a=2))
                nc.vector.tensor_copy(b_row, ps[:, 6, 256:512].rearrange("p (a b) -> p a b", a=2))
                dve.wait_ge(cb_ps, b + 1)
                nc.vector.tensor_copy(acum, ps[:, 7, 0:HEADS])
                step(nc.vector.tensor_copy(alast, ps[:, 7, HEADS:2 * HEADS]))
                nc.vector.tensor_tensor(dte, alast, acum, ALU.subtract).then_inc(ssd_small, 1)
                nc.vector.tensor_tensor(cbm, ps[:, 7, 128:384].rearrange("p (a b) -> p a b", a=2), over(tri[:, :], 1, 2), ALU.mult)\
                    .then_inc(kv_ready, 1)
                logits(b, 0, step)
                logits(b, 1, step)
                attended(b, 0, step)
                logits(b, 2, step)
                attended(b, 1, step)
                logits(b, 3, step)
                attended(b, 2, step)
                nc.vector.tensor_copy(mask_now[:, 0:P], band[:, 0:P])
                dve.wait_ge(xs_ready, b + 1)
                dt_b = dt_all[:, bass.ds(b, 1), :].rearrange("p a b -> p (a b)")
                step(nc.vector.tensor_tensor(xdt, xs_row, over(dt_b, 2, HD), ALU.mult))
                dve.wait_ge(ssd_exp, b + 1)
                nc.vector.tensor_tensor(xw, xdt, over(dte, 2, HD), ALU.mult).then_inc(xw_ready, 1)
                segment(b, 0, step)
                segment(b, 1, step)
                attended(b, 3, step)
                mixing(b, 0)
                segment(b, 2, step)
                mixing(b, 1)
                segment(b, 3, step)
                mixing(b, 2)
                mixing(b, 3)
                dve.wait_ge(st_ps, b + 1)
                step(nc.vector.tensor_tensor(tmp, state, over(cdec, 2, HD), ALU.mult))
                nc.vector.tensor_tensor(state, tmp, wide(2, HEADS, HD), ALU.add).then_inc(state_new, 1)
                dve.wait_ge(state_new, b + 1)
                dve.wait_ge(y_ps, b + 1)
                nc.vector.tensor_tensor(xw, xs_row, over(dskip[:, :], 2, HD), ALU.mult)
                step(nc.vector.tensor_tensor(tmp, wide(4, HEADS, HD), over(ea, 2, HD), ALU.mult))
                step(nc.vector.tensor_tensor(tmp, tmp, wide(6, HEADS, HD), ALU.add))
                step(nc.vector.tensor_tensor(tmp, tmp, xw, ALU.add))
                z_b = qz[:, bass.ds(b, 1), AW:].rearrange("p a (h d) -> p (a h) d", d=HD)
                nc.vector.tensor_tensor(tmp, tmp, z_b, ALU.mult).then_inc(y_gated, 1)
                dve.wait_ge(ss_ready, b + 1)
                nc.vector.tensor_scalar(var[:, :], ss, 1.0 / (GH * HD), EPS, ALU.mult, ALU.add).then_inc(var_ready, 1)
                one_over_root(b, step)
                for g in range(KV):
                    ins = nc.vector.tensor_scalar(y_row[:, AW + g * 512:AW + (g + 1) * 512],
                                                  tmp[:, g * GH:(g + 1) * GH, :].rearrange("p a b -> p (a b)"), root[:, g:g + 1], None, ALU.mult)
                ins.then_inc(y_rows, 1)
                dve.wait_ge(yt_ps, b * 2 + 2)
                nc.vector.tensor_tensor(y_t[:, 8:16, bass.ts(b, P)], wide(2, 8, P), over(normw[:, :], 2, P), ALU.mult).then_inc(yt_dve, 1)
                assert step.n == MIX_STEPS, step.n
            own.n += TB * MIX_STEPS

            dve.sem_inc(mix_read, 4)
            dve.wait_ge(x1_loaded, 16)
            dve.wait_ge(row_ready, 3)
            for n in range(2):
                for m in range(TB):
                    cols = slice(n * 1024, (n + 1) * 1024)
                    dve.wait_ge(mix_ps, n * 4 + m + 1)
                    nc.vector.tensor_tensor(tmp2[:, 0:1024], wide(2 * m, 1024), g1b[:, cols], ALU.mult).then_inc(mix_read, 1)
                    dve.wait_ge(mix_read, 4 + n * 4 + m + 1)
                    own(nc.vector.scalar_tensor_tensor(x1[:, m, cols], x1[:, m, cols], ALPHA, tmp2[:, 0:1024], ALU.mult, ALU.add))

            def layer_norm(n, row, gain, step):
                for j in range(4):
                    ins = nc.vector.bn_stats(stats[:, j, :], row[:, j * 512:(j + 1) * 512])
                step(ins)
                step(nc.vector.bn_aggr(mv, stats.rearrange("p a b -> p (a b)")))
                nc.vector.tensor_scalar(var[:, 0:1], mv[:, 1:2], EPS, None, ALU.add).then_inc(var_ready, 1)
                one_over_root(n, step)
                step(nc.vector.tensor_scalar(row, row, mv[:, 0:1], root[:, 0:1], ALU.subtract, ALU.mult))
                step(nc.vector.tensor_tensor(row, row, gain, ALU.mult))

            dve.wait_ge(ln1_loaded, 2 * 16)
            start1 = own.n
            with dve.Fori(0, TB) as m:
                step = Steps(dve, dve_own, m * 10 + start1, held)
                row = x1[:, bass.ds(m, 1), :].rearrange("p a b -> p (a b)")
                h_row = h2[:, bass.ds(m, 1), :].rearrange("p a b -> p (a b)")
                layer_norm(m + TB, row, ln1gb, step)
                step(nc.vector.tensor_tensor(row, row, ln1bb, ALU.add))
                step(nc.vector.tensor_tensor(h_row, row, sc2b, ALU.mult))
                nc.vector.tensor_tensor(h_row, h_row, sh2b, ALU.add).then_inc(h2_ready, 1)
                assert step.n == 10, step.n
            own.n += TB * 10

            def best16(values, indices, source, scratch, step):
                step(nc.vector.max(values[:, 0:8], source))
                nc.vector.max_index(indices[:, 0:8], values[:, 0:8], source)
                step(nc.vector.match_replace(scratch, values[:, 0:8], source, NEG))
                step(nc.vector.max(values[:, 8:16], scratch))
                return nc.vector.max_index(indices[:, 8:16], values[:, 8:16], scratch)

            dve.wait_ge(h2_high, 1)
            nc.vector.tensor_tensor(h2_parts[:, 1, :, :], h2_t_dense, h2_parts[:, 0, :, :].bitcast(F32), ALU.subtract)\
                .then_inc(h2_split, 1)
            dve.sem_inc(parts_read, 1)
            start2 = own.n
            TOP_STEPS = 88
            dve.sem_inc(g_ps, 2 * OH // 4)

            def select(m):
                step = Steps(dve, dve_own, m * TOP_STEPS + start2, held)
                dve.wait_ge(sc_ready, m + 1)
                dve.sem_inc(held, 1)
                for side in range(2):
                    for h in range(PH):
                        ins = best16(top_v[:, side, h, :], top_i[:, side, h, :], sc[:, side, h, :], rest, step)
                step(ins)
                step(nc.vector.tensor_copy(top_f, top_i))
                step(nc.vector.tensor_tensor(cand, over(top_v[:, 0, :, :], 3, PK), over(top_v[:, 1, :, :], 2, PK), ALU.add))
                for h in range(PH):
                    flat = cand[:, h, :, :].rearrange("p a b -> p (a b)")
                    ins = best16(pair_v[:, h, :], pair_i[:, h, :], flat, flat, step)
                step(ins)
                step(nc.vector.tensor_copy(pick_sum, pair_v[:, :, 0]))
                nc.vector.tensor_tensor(pair_v, pair_v, over(pick_sum, 2, PK), ALU.subtract).then_inc(pair_sub, 1)
                nc.vector.tensor_scalar(part_u[:, 0, :, :], pair_i, 4, None, ALU.logical_shift_right)
                step(nc.vector.tensor_scalar(part_u[:, 1, :, :], pair_i, 15, None, ALU.bitwise_and))
                step(nc.vector.tensor_copy(part_f, part_u))
                dve.wait_ge(parts_read, m + 1)
                dve.sem_inc(held, 1)
                for side in range(2):
                    flat = hits.rearrange("p a b c -> p (a b) c")
                    places = part_f[:, side, :, :].rearrange("p a b -> p (a b)")
                    step(nc.vector.tensor_tensor(flat, over(iota[:, 0:PK], 1, PICKS), over(places, 2, PK), ALU.is_equal))
                    step(nc.vector.tensor_tensor(hits, hits, over(top_f[:, side, :, :], 2, PK), ALU.mult))
                    step(nc.vector.tensor_reduce(part_id[:, side, :, :].rearrange("p a b -> p (a b)"), flat, AX, ALU.add))
                step(nc.vector.scalar_tensor_tensor(part_f[:, 0, :, :], part_id[:, 0, :, :], float(NKEY), part_id[:, 1, :, :],
                                                    ALU.mult, ALU.add))
                nc.vector.tensor_copy(ids[:, bass.ds(m, 1), :].rearrange("p a (b c) -> p (a b) c", c=PK), part_f[:, 0, :, :])
                dve.wait_ge(pair_exp, m + 1)
                step(nc.vector.tensor_reduce(pick_sum, pair_v, AX, ALU.add))
                step(nc.vector.reciprocal(pick_sum, pick_sum))
                nc.vector.tensor_tensor(gates[:, bass.ds(m, 1), :].rearrange("p a (b c) -> p (a b) c", c=PK), pair_v,
                                        over(pick_sum, 2, PK), ALU.mult).then_inc(topk_done, 1)
                dve.wait_ge(topk_done, m + 1)
                dve.sem_inc(sc_used, 1)
                assert step.n == TOP_STEPS, step.n

            def one_hots(m):
                dve.wait_ge(cols_ready, m + 1)
                dve.sem_inc(held, 1)
                with dve.Fori(0, P // (2 * OH)) as i:
                    for buf in range(2):
                        dve.wait_ge(g_ps, m * (P // 4) + i * (2 * OH // 4) + (buf * OH // 4 + OH // 4))
                        dve.sem_inc(held, 1)
                        now = bass.ds(m * P + i * (2 * OH) + buf * OH, OH)
                        nc.vector.tensor_tensor(one_hot[:, buf, :, :, :], over(over(iota[:, :], 1, OH), 1, 2),
                                                over(pick_cols[:, 0:2, now], 3, NKEY), ALU.is_equal).then_inc(hot_ready, 1)

            select(0)
            with dve.Fori(1, TB) as m:
                select(m)
                one_hots(m - 1)
            own.n += TB * TOP_STEPS

            dve.sem_inc(row_used, SLOTS)
            dve.wait_ge(g_ps, DT // 4 + 2 * OH // 4)
            own(nc.vector.memset(out4, 0.0))

            def add_values(g, half, m, units_used):
                dve.wait_ge(unit_used, units_used)
                row = out4[:, m, half * UNIT:(half + 1) * UNIT]
                nc.vector.tensor_tensor(row, row, wide(2 * m, UNIT), ALU.add).then_inc(v_read, 1)

            def dot(g, q):
                dve.wait_ge(ring_full[q], g.val(32, 16))
                nc.vector.tensor_tensor_reduce(out=ring[q], in0=ring[q], in1=h2_now, scale=1.0, scalar=0.0,
                                               op0=ALU.mult, op1=ALU.add, accum_out=act4[:, q:q + 1]).then_inc(row_used, 1)
                if q == SLOTS - 1:
                    dve.wait_ge(row_used, g.val(2 * SLOTS, 2 * SLOTS))
                    dve.sem_inc(dots_done, 1)

            def weigh(g):
                dve.wait_ge(gelu_done, g.val(1))
                dve.wait_ge(row_used, g.val(2 * SLOTS, 0))
                nc.vector.tensor_tensor(w4, act4, gates[:, DB, bass.ds(g.val(SLOTS, -SLOTS), SLOTS)], ALU.mult).then_inc(picks_w, 1)
                dve.wait_ge(picks_w, g.val(1))

            def add_row(g, q):
                dve.wait_ge(ring_full[q], g.val(32))
                dve.wait_ge(row_used, g.val(2 * SLOTS, q))
                nc.vector.scalar_tensor_tensor(acc_v, ring[q], w4[:, q:q + 1], acc_v, ALU.mult, ALU.add).then_inc(row_used, 1)

            PICK_STEPS = {"start": ((), (0, 0, 0, 0)), "ahead": ((1, 2, 3, 5), (5, 6, 7, 7)),
                          "full": ((4, 5, 6, 7), (8, 12, 14, 15)), "last": ((1, 2, 3, 5), ())}

            def group(g):
                buf = g.c % 2
                for j in g.steps():
                    if g.units:
                        dve.wait_ge(high_done, g.unit(j + 1))
                        nc.vector.tensor_tensor(split[:, j % 2, 1, :], raw[:, j % RAWS, :], split[:, j % 2, 0, :].bitcast(F32), ALU.subtract)\
                            .then_inc(unit_split, 1)
                    for i, due in g.tiles_at(j):
                        if due == "made":
                            if g.kind == "full":
                                dve.wait_ge(tile_gelu, g.val(GT, i + 1 + 2 - AHEAD * GT))
                            else:
                                dve.wait_ge(gel_full[i % 2], g.val(16 * GT // 2, 16 * (i // 2 + 1)))
                            dve.wait_ge(gm_full[buf], g.round(16, 16))
                            act_t = gel[:, i % 2, :].rearrange("p (a b) -> p a b", b=TG)
                            nc.vector.tensor_tensor(act_t, act_t, gm[:, buf, :, i * TG:(i + 1) * TG], ALU.mult).then_inc(w_made, 1)
                        if due == "low":
                            dve.wait_ge(w_high, g.val(GT, i + 1))
                            nc.vector.tensor_tensor(w_parts[:, buf, 1, i, :], gel[:, i % 2, :], w_parts[:, buf, 0, i, :].bitcast(F32), ALU.subtract)\
                                .then_inc(w_ready, 1)
                    if g.kind == "full":
                        if j in (1, 2, 3):
                            add_values(g, 1, j - 1, g.unit(0))
                        if j in (9, 10, 11):
                            add_values(g, 0, j - 9, g.unit(8))
                    elif g.kind != "start":
                        for m in range(DB):
                            if j == 0 and not g.second:
                                add_values(g, 1, m, g.unit(0))
                            if j == 4:
                                add_values(g, 0, m, g.unit(4))
                    sums, dots = PICK_STEPS[g.kind]
                    if sums and j == min(2, sums[0]):
                        weigh(g)
                    for q in range(SLOTS):
                        if sums and sums[q] == j:
                            add_row(g, q)
                    for q in range(SLOTS):
                        if dots and dots[q] == j:
                            dot(g, q)
                if g.kind == "last":
                    for m in range(DB):
                        add_values(g, 1, m, g.unit(8))

            stream(dve, group)

            dve.wait_ge(row_used, (2 * GROUPS + 1) * SLOTS)
            dve.wait_ge(v_read, 2 * GROUPS * DB)
            dve.wait_ge(tail_loaded, 3 * 16)
            dve.wait_ge(tail_row_ready, 2)
            start3 = own.n
            with dve.Fori(0, TB) as m:
                step = Steps(dve, dve_own, m * 10 + start3, held)
                row = out4[:, bass.ds(m, 1), :].rearrange("p a b -> p (a b)")
                step(nc.vector.tensor_tensor(row, row, g2b, ALU.mult))
                step(nc.vector.scalar_tensor_tensor(row, x1_back[:, bass.ds(m, 1), :].rearrange("p a b -> p (a b)"), ALPHA, row,
                                                    ALU.mult, ALU.add))
                layer_norm(m + 2 * TB, row, ln2gb, step)
                nc.vector.tensor_tensor(row, row, ln2bb, ALU.add).then_inc(y_ready, 1)
                assert step.n == 10, step.n

        @block.tensor
        def _(pe):
            def mod_sums(m):
                pe.wait_ge(ada_used, (m + 1) * KT)
                for k in range(KT):
                    ins = nc.tensor.matmul(ps[:, 4, k:k + 1], acc[:, k * P:(k + 1) * P], ones[:, 0:1], start=True, stop=True)
                ins.then_inc(mod_sum, 1)

            def slice_of(first, n, cols, channels):
                for half in range(2):
                    pe.wait_ge(win_full[half], n * 16 + 16 * (first + 1))
                    for m in range(4):
                        if half == 0:
                            pe.wait_ge(proj_bank_free, n * 4 + (4 * first + m + 1))
                        for j in range(8):
                            k = half * 8 + j
                            if channels:
                                lhs, rhs = win[:, half, j, m * P:(m + 1) * P], h_t[:, k, :]
                            else:
                                lhs, rhs = h_t[:, k, m * P:(m + 1) * P], win[:, half, j, 0:cols]
                            ins = nc.tensor.matmul(ps[:, m, 0:cols], lhs, rhs, start=k == 0, stop=k == KT - 1)
                        if half == 1:
                            ins.then_inc(proj_done, 1)
                        elif m == 3:
                            ins.then_inc(win_used, 1)

            pe.wait_ge(consts2, 6)
            for m in range(2):
                mod_sums(m)
            pe.wait_ge(h_ready, KT)
            with pe.Fori(0, 3) as n:
                slice_of(0, n, 512, True)
                mod_sums(n + 2)
            slice_of(3, 0, KVW + HEADS, False)
            with pe.Fori(0, 3) as n:
                slice_of(4, n, 512, False)
            mod_sums(5)
            slice_of(4, 3, 512, False)

            def turn(dst, src):
                return nc.tensor.transpose(dst, src, ident[:, :])

            def logits(b, u):
                if u:
                    pe.wait_ge(lg_read, b * 4 + u)
                for pair in range(2):
                    for par in range(2):
                        rows = slice(64 * par, 64 * par + 64)
                        ins = nc.tensor.matmul(ps[:, par, pair * 256:pair * 256 + 256], q_t[rows, 2 * u + pair, :],
                                               k_t[rows, u // 2, :], start=True, stop=True)
                ins.then_inc(lg_done, 1)

            def turn_p(b, u):
                pe.wait_ge(exp_done, b * 4 + (u + 1))
                if u:
                    pe.wait_ge(pt_ready, b * 4 + u)
                for j in range(8):
                    ins = turn(wide(2, 8, P)[:, j, :], lg[:, u % 2, j // 4, j // 2 % 2, (j % 2) * P:(j % 2 + 1) * P])
                ins.then_inc(pt_ps, 1)

            def values(b, u):
                pe.wait_ge(pt_ready, b * 4 + (u + 1))
                if u % 2:
                    pe.wait_ge(att_out, b * 4 + u)
                for pair in range(2):
                    for par in range(2):
                        h = 4 * u + 2 * pair + par
                        for half in range(2):
                            ins = nc.tensor.matmul(ps[:, 4 + h // GH, (h % GH) * HD:(h % GH + 1) * HD],
                                                   p_t[:, u % 2, (par * 2 + pair) * 2 + half, :],
                                                   vv[:, half, (h // GH) * HD:(h // GH + 1) * HD], start=half == 0, stop=half == 1)
                ins.then_inc(pv_done, 1)

            def segments(b, c):
                if c >= 2:
                    pe.wait_ge(seg_read, b * 4 + (c - 1))
                for i in range(4):
                    h = 4 * c + i
                    ins = nc.tensor.matmul(ps[:, c % 2, i * P:(i + 1) * P], da_now[:, h:h + 1].to_broadcast([P, P]), tri[:, :],
                                           start=True, stop=True)
                ins.then_inc(seg_ps, 1)

            def within(b, c):
                pe.wait_ge(m_ready, b * 4 + (c + 1))
                for i in range(4):
                    h = 4 * c + i
                    ins = nc.tensor.matmul(ps[:, 6 + h // GH, (h % GH) * HD:(h % GH + 1) * HD], m_t[:, h, :], xdt[:, h, :],
                                           start=True, stop=True)
                return ins

            with pe.Fori(0, TB) as b:
                pe.wait_ge(block_in, b + 1)
                for i in range(HEADS // 2):
                    ins = turn(wide(2, 8, P)[:, i, :], qk[:, 2 * i:2 * i + 2, :].rearrange("p a b -> p (a b)"))
                ins.then_inc(qt_ps, 1)
                for g in range(KV):
                    turn(ps[:, 6, g * P:(g + 1) * P], kdup[:, g, :, :].rearrange("p a b -> p (a b)"))
                for g in range(KV):
                    ins = turn(ps[:, 6, (2 + g) * P:(3 + g) * P], cur[:, 8 + g, :])
                ins.then_inc(kb_ps, 1)
                nc.tensor.matmul(ps[:, 7, 0:HEADS], tri[:, :], da_now, start=True, stop=True)
                nc.tensor.matmul(ps[:, 7, HEADS:2 * HEADS], ones[:, :], da_now, start=True, stop=True)
                for g in range(KV):
                    ins = nc.tensor.matmul(ps[:, 7, (1 + g) * P:(2 + g) * P], cur[:, 8 + g, :], cur[:, 10 + g, :], start=True, stop=True)
                ins.then_inc(cb_ps, 1)
                for i in range(8):
                    ins = turn(wide(4, 8, P)[:, i, :], cur[:, i, :])
                ins.then_inc(xs_ps, 1)
                pe.wait_ge(q_ready, b + 1)
                pe.wait_ge(kv_ready, b + 1)
                logits(b, 0)
                logits(b, 1)
                turn_p(b, 0)
                logits(b, 2)
                pe.wait_ge(xs_ready, b + 1)
                values(b, 0)
                turn_p(b, 1)
                logits(b, 3)
                values(b, 1)
                turn_p(b, 2)
                pe.wait_ge(lg_read, b * 4 + 4)
                segments(b, 0)
                segments(b, 1)
                values(b, 2)
                turn_p(b, 3)
                values(b, 3)
                within(b, 0)
                segments(b, 2)
                within(b, 1)
                segments(b, 3)
                pe.wait_ge(xw_ready, b + 1)
                pe.wait_ge(att_out, b * 4 + 4)
                for g in range(KV):
                    nc.tensor.matmul(ps[:, 4 + g, :], cur[:, 10 + g, :], state[:, g * GH:(g + 1) * GH, :].rearrange("p a b -> p (a b)"),
                                     start=True, stop=True)
                for g in range(KV):
                    ins = nc.tensor.matmul(ps[:, 2 + g, :], b_row[:, g, :], xw[:, g * GH:(g + 1) * GH, :].rearrange("p a b -> p (a b)"),
                                           start=True, stop=True)
                ins.then_inc(st_ps, 1)
                within(b, 2)
                within(b, 3).then_inc(y_ps, 1)
                pe.wait_ge(seg_read, b * 4 + 4)
                for i in range(8):
                    ins = turn(wide(0, 8, P)[:, i, :], y_row[:, i * P:(i + 1) * P])
                ins.then_inc(yt_ps, 1)
                pe.wait_ge(y_rows, b + 1)
                for i in range(8):
                    ins = turn(wide(2, 8, P)[:, i, :], y_row[:, (8 + i) * P:(9 + i) * P])
                ins.then_inc(yt_ps, 1)
                pe.wait_ge(yt_act, b + 1)

            pe.wait_ge(yt_dve, TB)
            pe.wait_ge(mod_ready, MODS)
            for i, m in enumerate((2, 4, 3)):
                if i >= 2:
                    pe.wait_ge(row_ready, i - 1)
                for k in range(KT):
                    ins = nc.tensor.matmul(ps[:, 4 * (i % 2) + k // 4, (k % 4) * P:(k % 4 + 1) * P],
                                           mod_cols[:, m * KT + k:m * KT + k + 1].to_broadcast([P, P]), ident[:, :], start=True, stop=True)
                ins.then_inc(row_ps, 1)

            pe.wait_ge(row_ready, 3)
            with pe.Fori(0, 2) as n:
                for k in range(KT):
                    pe.wait_ge(wt_full[k % 4], n * 64 + 16 * (k // 4 + 1))
                    for m in range(TB):
                        if k == 0:
                            pe.wait_ge(mix_read, n * 4 + (m + 1))
                        for j in range(2):
                            ins = nc.tensor.matmul(ps[:, 2 * m + j, :], y_t[:, k, m * P:(m + 1) * P], wt[:, k % 4, j * 512:(j + 1) * 512],
                                                   start=k == 0, stop=k == KT - 1)
                        if k == KT - 1:
                            ins.then_inc(mix_ps, 1)
                        elif m == TB - 1:
                            ins.then_inc(wt_used, 1)
                pe.wait_ge(mix_ps, n * 4 + 4)
                pe.sem_inc(wt_used, 1)

            for m in range(TB):
                pe.wait_ge(h2_ready, m + 1)
                if m >= 2:
                    pe.wait_ge(h2t_ready, m - 1)
                for k in range(KT):
                    ins = turn(wide(4 * (m % 2), KT, P)[:, k, :], h2[:, m, k * P:(k + 1) * P])
                ins.then_inc(h2t_ps, 1)
            pe.wait_ge(h2t_ready, TB)
            for k in range(KT):
                pe.wait_ge(wt_full[k % 4], 128 + 16 * (k // 4 + 1))
                for h in range(PH):
                    ins = nc.tensor.matmul(bank(h), wt_q[:, k % 4, h * P:(h + 1) * P], h2_t[:, k, :], start=k == 0, stop=k == KT - 1)
                    if k == KT - 1:
                        ins.then_inc(q_ps, 1)
                if k < KT - 1:
                    ins.then_inc(wt_used, 1)
            pe.wait_ge(key_loaded, 16)
            pe.wait_ge(q8_ready, PH)

            def scores(m):
                if m:
                    pe.wait_ge(sc_ready, m)
                for h in range(PH):
                    for side in range(2):
                        rows = slice(64 * side, 64 * side + 64)
                        ins = nc.tensor.matmul(wide(0, 2, PH, NKEY)[:, side, h, :], q8[rows, h, m * P:(m + 1) * P],
                                               key_t[rows, :], start=True, stop=True)
                ins.then_inc(sc_ps, 1)

            def ahead(m):
                with pe.Fori(0, WIN_PAIRS) as n:
                    for j in range(4):
                        b, half = j // 2, j % 2
                        pe.wait_ge(pre_split, n * 4 + (m * WIN_UNITS + j + 1 + RAWS))
                        if half == 0:
                            pe.wait_ge(pre_gelu, n * 2 + (m * 2 * WIN_PAIRS + b + 1))
                        unit(j, b, half).then_inc(pre_used, 1)

            def unit(j, b, half):
                high, low = split[:, j % 2, 0, :], split[:, j % 2, 1, :]
                for kk in range(8):
                    k = half * 8 + kk
                    cols = slice(kk * P, (kk + 1) * P)
                    for n, (lhs, rhs) in enumerate(((high, 0), (high, 1), (low, 0))):
                        ins = nc.tensor.matmul(ps[:, 6 + b, 0:DT], lhs[:, cols], h2_parts[:, rhs, k, :],
                                               start=k == 0 and n == 0, stop=k == KT - 1 and n == 2)
                return ins

            def turned(m):
                pe.wait_ge(topk_done, m + 1)
                pe.wait_ge(pre_gelu, (m + 1) * 2 * WIN_PAIRS + 2)
                for i, what in enumerate((part_id[:, 0, :, :], part_id[:, 1, :, :], gates[:, m, :].rearrange("p (a b) -> p a b", b=PK))):
                    ins = turn(ps[:, 6, i * P:(i + 1) * P], what.rearrange("p a b -> p (a b)"))
                ins.then_inc(cols_ps, 1)
                pe.wait_ge(cols_ps, m + 1)
                pe.sem_inc(parts_read, 1)

            def gates_by_expert(m):
                with pe.Fori(0, P // (2 * OH)) as i:
                    for buf in range(2):
                        pe.wait_ge(hot_gated, i * 2 + (m * (P // OH) + buf + 1))
                        for quad in range(OH // 4):
                            pe.wait_ge(g_staged, i * (2 * OH // 4) + ((m * P + buf * OH) // 4 + quad + 1))
                            for t in range(4 * quad, 4 * quad + 4):
                                ins = nc.tensor.matmul(ps[:, 4 + quad, (t % 4) * P:(t % 4 + 1) * P], one_hot[:, buf, 0, t, :], one_hot[:, buf, 1, t, :],
                                                       start=True, stop=True)
                            ins.then_inc(g_ps, 1)

            pe.sem_inc(g_staged, 2)
            pe.sem_inc(pre_gelu, 2)
            scores(0)
            scores(1)
            pe.wait_ge(h2_split, 1)
            for m in range(TB):
                if m:
                    pe.wait_ge(cols_ready, m)
                ahead(m)
                if m < DB:
                    turned(m)
                if m + 2 < TB:
                    scores(m + 2)
                if m:
                    gates_by_expert(m - 1)

            def second_gate(half):
                for k in range(8):
                    c = 5 * KT + half * 8 + k
                    ins = nc.tensor.matmul(wide(6, 8, P)[:, k, :], mod_cols[:, c:c + 1].to_broadcast([P, P]), ident[:, :], start=True, stop=True)
                ins.then_inc(tail_row, 1)

            def group(g):
                buf = (g.c - 1) % 2
                if g.kind == "last":
                    pe.wait_ge(tile_gelu, (GROUPS - AHEAD) * GT + 2)
                    second_gate(0)
                for j, (table, i, half) in enumerate(g.units):
                    pe.wait_ge(unit_split, g.unit(j + 1))
                    if table == "u":
                        if half == 0:
                            pe.wait_ge(tile_gelu, g.val(GT, i + 1 - AHEAD * GT))
                        ins = unit(j, i % 2, half)
                    else:
                        high, low = split[:, j % 2, 0, :], split[:, j % 2, 1, :]
                        pe.wait_ge(w_ready, g.val(GT, i + 1 - GT))
                        for m in range(DB):
                            if i == 0 and not (g.second and half == 0):
                                pe.wait_ge(v_read, g.val(2 * DB, (half - 2) * DB + m - DB + 1))
                            for n, (lhs, rhs) in enumerate(((0, high), (0, low), (1, high))):
                                for b in range(2):
                                    ins = nc.tensor.matmul(ps[:, 2 * m + b, :], w_parts[:, buf, lhs, i, m * P:(m + 1) * P], rhs[:, b * 512:(b + 1) * 512],
                                                           start=i == 0 and n == 0, stop=i == GT - 1 and n == 2)
                    ins.then_inc(unit_used, 1)

            pe.wait_ge(pre_gelu, AHEAD * GT + 2)
            pe.wait_ge(cols_ready, DB)
            pe.wait_ge(g_staged, DT // 4 + 2)
            pe.sem_inc(tile_gelu, 2)
            stream(pe, group)
            pe.wait_ge(tail_row_ready, 1)
            second_gate(1)


def kernel(**inputs):
    import numpy as np
    import concourse.bacc as bacc
    from concourse.bass_utils import run_bass_kernel_spmd as run

    a = {n: np.asarray(v) for n, v in inputs.items()}
    x = a["x"][0]
    w_in = a["w_in"][0].reshape(KT, P, -1).transpose(1, 0, 2)
    z0 = AW + KVW
    xbc0 = z0 + AW
    dt0 = xbc0 + XT * P
    laid = {
        "x_rows": x,
        "x_cols": x.T.reshape(KT, P, S).transpose(1, 0, 2),
        "c_cols": a["c"][0].reshape(KT, P).T,
        "pos_cols": a["positions"][0].reshape(TB, P).T,
        "w_ada": a["w_ada"][0],
        "b_ada_cols": a["b_ada"][0].reshape(MODS * KT, P).T,
        "w_xbc": np.stack([w_in[:, :, xbc0 + i * 512:xbc0 + (i + 1) * 512] for i in range(XT // 4)]),
        "w_kvdt": np.concatenate([w_in[:, :, AW:z0], w_in[:, :, dt0:]], axis=2),
        "w_qz": np.stack([w_in[:, :, c:c + 512] for c in (0, 512, z0, z0 + 512)]),
        "conv_w": a["conv_w"][0].reshape(CONV, XT, P).transpose(2, 1, 0).reshape(P, XT * CONV),
        "conv_b": a["conv_b"][0].reshape(XT, P).T,
        "dt_bias": a["dt_bias"],
        "a_log": a["a_log"],
        "d_skip": a["d_skip"],
        "norm_w": a["ssd_norm_w"][0].reshape(AW // P, P).T,
        "sinks": a["attn_sinks"],
        "w_out": a["w_out"][0].reshape(KT, P, 2, D // 2).transpose(2, 0, 1, 3).reshape(2 * KT, P, D // 2),
        "ln1_g": a["ln1_g"],
        "ln1_b": a["ln1_b"],
        "w_q": a["peer_wq"][0].reshape(KT, P, PH * P),
        "keys": np.concatenate([a["peer_k1"][0].T, a["peer_k2"][0].T]),
        "u_units": a["peer_u"][0].reshape(NKEY, NKEY, 2, 8, P).transpose(1, 2, 4, 3, 0).reshape(2 * NKEY, P, UNIT),
        "u_tab": a["peer_u"][0],
        "v_tab": a["peer_v"][0],
        "ln2_g": a["ln2_g"],
        "ln2_b": a["ln2_b"],
    }
    nc = bacc.Bacc("TRN2", target_bir_lowering=False, num_devices=1)
    arrays, args = {}, []
    for name, value in laid.items():
        value = np.ascontiguousarray(value)
        arrays[f"in_{name}"] = value
        args.append(nc.dram_tensor(f"in_{name}", value.shape, mybir.dt.from_np(value.dtype), kind="ExternalInput").ap())
    args.append(nc.dram_tensor("out_rows", (S, D), F32, kind="ExternalOutput").ap())
    decoder_layer(nc, *args)
    result = run(nc, [arrays], core_ids=[0])
    return result.results[0]["out_rows"].reshape(1, S, D)
```

```python
import math
from contextlib import ExitStack

import concourse.bass as bass
from concourse import mybir

P = 128
D = 2048
KT = D // P
S = 512
TB = S // P
HEADS, HD = 16, 64
KV = 2
GH = HEADS // KV
AW = HEADS * HD
ROT = HD // 4
NF = ROT // 2
THETA = 500000.0
CONV = 4
XT = (AW + 2 * KV * P) // P
KVW = 2 * KV * HD
SLICES = 8
MODS = 6
PH, PK = 8, 16
NKEY = 128
PICKS = PH * PK
ALPHA = 2.0 ** 0.25
EPS = 1e-5
NEG = -1.0e30
DB = TB - 1
DT = DB * P
GT = 4
GROUPS = NKEY // GT
UNIT = 1024
RAWS = 4
SLOTS = PICKS // GROUPS
TG = 16
OH = 8
AHEAD = 6
WIN_PAIRS = AHEAD * GT // TB // 2
WIN_UNITS = 4 * WIN_PAIRS

F32 = mybir.dt.float32
F32R = mybir.dt.float32r
I32 = mybir.dt.int32
U32 = mybir.dt.uint32
ALU = mybir.AluOpType
ACT = mybir.ActivationFunctionType
AX = mybir.AxisListType.X

K = 1024
HT = 0
WIN = 8 * K
WPARTS = 26 * K
ADA = 16 * K
ACC = 24 * K
WT = 22 * K
SPARE = 26 * K
QZ = 28 * K
KVDT = 36 * K
XRAW = KVDT + TB * (KVW + HEADS)
XCONV = XRAW + XT * (S + CONV - 1)
GM = 0
RAW = GM + 2 * GT * DT
GEL = RAW + RAWS * UNIT
OUT4 = GEL + 2 * DT
RING = OUT4 + TB * D
SPREAD = 14 * K
STAGE = QZ
PARTS = 26 * K
WP, UP, HP = 2 * 2 * GT * DT, 2 * 2 * UNIT, 2 * KT * DT
LATE = PARTS + WP + UP + HP
ARENA = LATE + 2048
HCOLS = LATE - KT * S
LN1 = 36 * K
YHIGH = 14 * K
YLOW = LN1 + 2 * D
assert YLOW + KT * S <= LATE
assert RING + 2 * D <= 20 * K and LATE >= PARTS


class Steps:

    def __init__(self, engine, semaphore, base=0, held=None):
        self.engine, self.semaphore, self.base, self.held, self.n = engine, semaphore, base, held, 0

    def __call__(self, instruction):
        self.n += 1
        instruction.then_inc(self.semaphore, 1)
        self.engine.wait_ge(self.semaphore, self.base + self.n)
        if self.held is not None:
            self.engine.sem_inc(self.held, 1)


def over(ap, axis, n):
    wide = ap.unsqueeze(axis)
    shape = list(wide.shape)
    shape[axis] = n
    return wide.to_broadcast(shape)


class Group:

    def __init__(self, kind, c, p=None):
        self.kind, self.c, self.p = kind, c, p
        u = [("u", i, half) for i in range(GT) for half in range(2)]
        v = [("v", i, half) for half in range(2) for i in range(GT)]
        self.units = {"start": [], "ahead": v, "full": u[:4] + v[:4] + u[4:] + v[4:], "last": v}[kind]
        self.second = p is None and c == 1

    def val(self, times, plus=0):
        at = times * self.c + plus
        return at if self.p is None else self.p * (2 * times) + at

    def unit(self, j):
        if self.kind == "ahead":
            return self.val(2 * GT, j - 2 * GT)
        return self.val(4 * GT, j - 2 * GT * (AHEAD + 1))

    def round(self, times, plus=0):
        at = times * (self.c // 2) + plus
        return at if self.p is None else self.p * times + at

    def tiles_at(self, j):
        if self.kind == "start":
            return [(i, due) for i in range(GT) for due in ("made", "high", "low")]
        if self.kind == "ahead":
            return [(j // 2, "made")] if j % 2 == 0 else [(j // 2, "high"), (j // 2, "low")]
        due = []
        if self.kind == "full":
            for i in range(GT):
                since = j - self.units.index(("u", i, 1))
                due += [(i, what) for what in {2: ("gelu", "made"), 3: ("high",), 4: ("low",)}.get(since, ())]
        return due

    def steps(self):
        return range(max(len(self.units), 1))


def stream(engine, group):
    group(Group("start", 0))
    group(Group("ahead", 1))
    with engine.Fori(1, AHEAD // 2) as p:
        for c in range(2):
            group(Group("ahead", c, p))
    with engine.Fori(AHEAD // 2, GROUPS // 2) as p:
        for c in range(2):
            group(Group("full", c, p))
    group(Group("last", GROUPS))


def decoder_layer(nc, x_rows, x_cols, c_cols, pos_cols, w_ada, b_ada_cols, w_slices, conv_w, conv_b,
                  dt_bias, a_log, d_skip, norm_w, sinks, w_out, ln1_g, ln1_b, w_q, keys, u_units, u_tab, v_tab,
                  ln2_g, ln2_b, out):
    with ExitStack() as ctx:
        def sb(name, shape, dt=F32):
            return ctx.enter_context(nc.sbuf_tensor(name, shape, dt))

        def sem(name):
            return ctx.enter_context(nc.semaphore(name))

        taken = {}

        def at(off, *dims, base=None):
            n = math.prod(dims)
            flat = (arena if base is None else base)[:, off:off + n]
            if len(dims) == 1:
                return flat
            names = "abcd"[:len(dims)]
            return flat.rearrange(f"p ({' '.join(names)}) -> p {' '.join(names)}", **dict(zip(names[1:], dims[1:])))

        def place(region, off, *dims):
            start = taken.get(region, off)
            taken[region] = start + math.prod(dims)
            return at(start, *dims)

        ident = sb("ident", [P, P])
        tri = sb("tri", [P, P])
        ones = sb("ones", [P, P])
        band = sb("band", [P, 2 * P])
        mask_now = sb("mask_now", [P, 2 * P])
        iota = sb("iota", [P, NKEY])
        c_act = sb("c_act", [P, KT])
        c_tmp = sb("c_tmp", [P, KT])
        mod_cols = sb("mod_cols", [P, MODS * KT])
        b_cols = sb("b_cols", [P, MODS * KT])
        convw = sb("convw", [P, XT * CONV])
        convb = sb("convb", [P, XT])
        normw = sb("normw", [P, AW // P])
        dtb = sb("dtb", [P, HEADS])
        a_neg = sb("a_neg", [P, HEADS])
        dskip = sb("dskip", [P, HEADS])
        sink = sb("sink", [P, HEADS])
        pos_i = sb("pos_i", [P, TB], I32)
        inv = sb("inv", [P, NF])
        ang = sb("ang", [P, 2, TB, NF])
        turns = sb("turns", [P, 2, TB, NF])
        trig = sb("trig", [P, 2, TB, NF])
        dt_all = sb("dt_all", [P, TB, HEADS])
        da_all = sb("da_all", [P, TB, HEADS])
        dt_abs = sb("dt_abs", [P, TB, HEADS])
        var = sb("var", [P, KV])
        root = sb("root", [P, KV])
        root_t = sb("root_t", [P, KV])

        with ExitStack() as first:
            def early(name, shape, dt=F32):
                return first.enter_context(nc.sbuf_tensor(name, shape, dt))

            h_parts = early("h_parts", [P, 2, KT, S], F32R)
            early("below_w_parts", [P, WPARTS - 2 * KT * S])
            win_parts = early("win_parts", [P, 2, 2, 512], F32R)
            early("above_w_parts", [P, HCOLS - WPARTS - 2048])
            h_cols = early("h_cols", [P, KT, S])
        with ExitStack() as first:
            wout_parts = early("wout_parts", [P, 2, 2, 1024], F32R)
            early("below_y_high", [P, YHIGH - 4096])
            y_high = early("y_high", [P, KT, S], F32R)
            early("above_y_high", [P, YLOW - YHIGH - KT * S])
            y_low = early("y_low", [P, KT, S], F32R)
        with nc.sbuf_tensor("arena", [P, ARENA], F32) as arena:
            pass
        below_parts = sb("below_parts", [P, PARTS])
        w_parts = sb("w_parts", [P, 2, 2, GT, DT], F32R)
        split = sb("split", [P, 2, 2, UNIT], F32R)
        h2_parts = sb("h2_parts", [P, 2, KT, DT], F32R)
        sb("above_parts", [P, ARENA - LATE])
        gates_out = nc.dram_tensor("gates_by_expert", (P, DT // TG, NKEY, TG), F32, kind="Internal").ap()
        acts_out = nc.dram_tensor("acts_ahead", (AHEAD * GT, P, DT), F32, kind="Internal").ap()
        x1_out = nc.dram_tensor("x1_rows", (P, TB, D), F32, kind="Internal").ap()

        ps = ctx.enter_context(nc.psum_tensor("ps", [P, 8, 512], F32))

        def bank(i, n=1):
            return ps[:, i, :] if n == 1 else ps[:, i:i + n, :]

        def wide(i, *dims):
            flat = ps[:, :, :].rearrange("p b n -> p (b n)")[:, 512 * i:512 * i + math.prod(dims)]
            names = "abcd"[:len(dims)]
            return flat.rearrange(f"p ({' '.join(names)}) -> p {' '.join(names)}", **dict(zip(names[1:], dims[1:])))

        ada = at(ADA, 4, D)
        acc = at(ACC, D)
        qz = at(QZ, TB, 2 * AW)
        win_raw = [qz[:, 2 * i:2 * i + 2, 2 * AW - 512:] for i in range(2)]
        kvdt = at(KVDT, TB, KVW + HEADS)
        x_raw = at(XRAW, XT, S + CONV - 1)
        x_conv = at(XCONV, XT, S)

        cur = place("a", WIN, XT, P)
        qk = place("a", WIN, HEADS + KV, HD)
        kdup = place("a", WIN, KV, 2, HD)
        q_t = place("a", WIN, HEADS // 2, P)
        k_t = place("a", WIN, KV, 2 * P)
        vv = place("a", WIN, 2, KV * HD)
        lg = place("a", WIN, 2, 2, 2, 2 * P)
        p_t = place("a", WIN, 2, 8, P)
        y_row = place("a", WIN, 2 * AW)
        xs_row = place("a", WIN, HEADS, HD)
        b_row = place("a", WIN, KV, P)
        cbm = place("a", WIN, KV, P)
        assert taken["a"] <= WT
        xdt = place("b", XRAW, HEADS, HD)
        xw = place("b", XRAW, HEADS, HD)
        m_t = place("b", XRAW, HEADS, P)
        state = place("b", XRAW, HEADS, HD)
        tmp = place("b", XRAW, HEADS, HD)
        assert taken["b"] <= XCONV
        decay = place("c", SPARE, 2, 4, P)
        rope_tmp = place("c", SPARE, 4, HEADS + KV, NF)
        trig_now = place("c", SPARE, 2, NF)
        mx = place("c", SPARE, 2, 4)
        es = place("c", SPARE, 2, 4)
        den = place("c", SPARE, 2, 4)
        da_now = place("c", SPARE, HEADS)
        acum = place("c", SPARE, HEADS)
        alast = place("c", SPARE, HEADS)
        dte = place("c", SPARE, HEADS)
        ea = place("c", SPARE, HEADS)
        cdec = place("c", SPARE, HEADS)
        ss = place("c", SPARE, KV)
        assert taken["c"] <= QZ
        y_t = at(HT, KT, S, base=below_parts)

        wt = at(WT, 4, 1024, base=below_parts)
        g1b, sc2b, sh2b = (at(WIN + i * D, D) for i in range(3))
        h2 = at(WIN + 3 * D, TB, D)
        tmp2 = at(SPARE, D)
        x1 = at(QZ, TB, D)
        ln1gb, ln1bb = (at(LN1 + i * D, D) for i in range(2))
        late = LATE
        ids = place("d", late, TB, PICKS).bitcast(U32)
        gates = place("d", late, TB, PICKS)
        key_t = place("d", late, NKEY)
        stats = place("d", late, 4, 6)
        mv = place("d", late, 2)
        act4 = place("d", late, SLOTS)
        w4 = place("d", late, SLOTS)
        idx = place("d", late, SLOTS).bitcast(U32)
        assert taken["d"] <= ARENA
        h2_t = at(HT, KT, S, base=below_parts)

        sc = at(HT, 2, PH, NKEY)
        cand = at(HT + 4 * K, PH, PK, PK)
        hits = at(HT + 6 * K, PH, PK, PK)
        q8 = at(WIN, PH, S)
        top_v = place("e", WIN + 4 * K, 2, PH, PK)
        top_i = place("e", WIN + 4 * K, 2, PH, PK).bitcast(U32)
        top_f = place("e", WIN + 4 * K, 2, PH, PK)
        rest = at(HT + 6 * K, 2, PH, NKEY)
        pair_v = place("e", WIN + 4 * K, PH, PK)
        pair_i = place("e", WIN + 4 * K, PH, PK).bitcast(U32)
        part_u = place("e", WIN + 4 * K, 2, PH, PK).bitcast(U32)
        part_f = place("e", WIN + 4 * K, 2, PH, PK)
        part_id = place("e", WIN + 4 * K, 2, PH, PK)
        pick_sum = place("e", WIN + 4 * K, PH)
        assert taken["e"] <= WIN + 6 * K

        one_hot = at(SPREAD, 2, 2, OH, NKEY)
        pick_cols = at(SPREAD + 4 * OH * NKEY, 3, DT)
        stage = at(STAGE, 2, NKEY, TG)
        gm = at(GM, 2, DT // TG, GT * TG, base=below_parts)
        pre_gel = at(SPREAD + 4 * OH * NKEY + 3 * DT, 2, DT)
        assert SPREAD + 4 * OH * NKEY + 5 * DT <= 20 * K and STAGE + 2 * NKEY * TG <= PARTS + WP
        pre_raw = wt
        raw = at(RAW, RAWS, UNIT, base=below_parts)
        gel = at(GEL, 2, DT, base=below_parts)
        h2_t_dense = h2_t[:, :, 0:DT]
        out4 = at(OUT4, TB, D)
        acc_v = out4[:, DB, :]
        h2_now = h2[:, DB, :]
        ring = [at(o, D) for o in (RING, RING + D, WT, WT + D)]
        assert RING + 2 * D <= WIN + 3 * D + DB * D
        g2b = at(GM, D)
        x1_back = at(PARTS + WP + UP, TB, D)
        ln2gb, ln2bb = (at(PARTS + WP + UP + (TB + i) * D, D) for i in range(2))

        small_loaded = sem("small_loaded")
        c_loaded = sem("c_loaded")
        x_loaded = sem("x_loaded")
        ada_full = [sem(f"ada_full{i}") for i in range(4)]
        ada_used = sem("ada_used")
        win_full = [sem(f"win_full{i}") for i in range(2)]
        win_used = sem("win_used")
        win_high = sem("win_high")
        win_split = sem("win_split")
        h_high = sem("h_high")
        h_split = sem("h_split")
        pads_zero = sem("pads_zero")
        win_held = sem("win_held")
        consts = sem("consts")
        consts2 = sem("consts2")
        c_exp = sem("c_exp")
        ang_ready = sem("ang_ready")
        trig_ready = sem("trig_ready")
        mod_sum = sem("mod_sum")
        mod_ready = sem("mod_ready")
        h_ready = sem("h_ready")
        proj_done = sem("proj_done")
        proj_bank_free = sem("proj_bank_free")
        proj_out = sem("proj_out")
        conv_ready = sem("conv_ready")
        silu_done = sem("silu_done")
        dve_own = sem("dve_own")
        act_own = sem("act_own")
        names = (
            "dt_in dt_log a_exp block_in qt_ps kb_ps cb_ps xs_ps q_ready xs_ready kv_ready lg_done lg_read mx_ready "
            "exp_done pt_ps pt_ready pv_done att_out ssd_small ssd_exp xw_ready seg_ps seg_read seg_in seg_exp m_ready "
            "y_ps st_ps state_new y_gated ss_ready y_rows yt_ps yt_act yt_dve "
            "y_normed y_gained y_high_done y_split wout_high wout_split wout_used row_ps row_ready wt_used mix_ps mix_read x1_loaded ln1_loaded key_loaded h2_ready h2t_ps h2t_ready q_ps "
            "q8_ready sc_ps sc_ready sc_used pair_sub pair_exp topk_done row_used idx_copied dots_done gelu_done "
            "x1_stored h2_high h2_split parts_read cols_ps cols_ready spread hot_gated hot_ready g_ps g_staged "
            "pre_high pre_split pre_used pre_gelu high_done unit_split unit_used tile_gelu w_made w_high w_ready v_read picks_w tail_loaded tail_row tail_row_ready "
            "y_ready out_done z_done held idx_held var_ready root_ready"
        )
        (dt_in, dt_log, a_exp, block_in, qt_ps, kb_ps, cb_ps, xs_ps, q_ready, xs_ready, kv_ready, lg_done, lg_read, mx_ready,
         exp_done, pt_ps, pt_ready, pv_done, att_out, ssd_small, ssd_exp, xw_ready, seg_ps, seg_read, seg_in, seg_exp, m_ready,
         y_ps, st_ps, state_new, y_gated, ss_ready, y_rows, yt_ps, yt_act, yt_dve,
         y_normed, y_gained, y_high_done, y_split, wout_high, wout_split, wout_used, row_ps, row_ready, wt_used, mix_ps, mix_read, x1_loaded, ln1_loaded, key_loaded, h2_ready, h2t_ps, h2t_ready, q_ps,
         q8_ready, sc_ps, sc_ready, sc_used, pair_sub, pair_exp, topk_done, row_used, idx_copied, dots_done, gelu_done,
         x1_stored, h2_high, h2_split, parts_read, cols_ps, cols_ready, spread, hot_gated, hot_ready, g_ps, g_staged,
         pre_high, pre_split, pre_used, pre_gelu, high_done, unit_split, unit_used, tile_gelu, w_made, w_high, w_ready, v_read, picks_w, tail_loaded, tail_row, tail_row_ready,
         y_ready, out_done, z_done, held, idx_held, var_ready, root_ready) = map(sem, names.split())
        wt_full = [sem(f"wt_full{i}") for i in range(4)]
        ring_full = [sem(f"ring_full{i}") for i in range(SLOTS)]
        g_stored = [sem(f"g_stored{i}") for i in range(2)]
        pre_full = [sem(f"pre_full{i}") for i in range(RAWS)]
        acts_stored = [sem(f"acts_stored{i}") for i in range(2)]
        gel_full = [sem(f"gel_full{i}") for i in range(2)]
        raw_full = [sem(f"raw_full{i}") for i in range(RAWS)]
        gm_full = [sem(f"gm_full{i}") for i in range(2)]

        block = ctx.enter_context(nc.Block())

        @block.sync
        def _(sp):
            sp.dma_start(c_tmp[:, :], c_cols[:, :]).then_inc(c_loaded, 16)
            for to, what in ((b_cols, b_ada_cols), (convw, conv_w), (convb, conv_b), (normw, norm_w), (pos_i, pos_cols)):
                sp.dma_start(to[:, :], what[:, :]).then_inc(small_loaded, 16)
            for to, what in ((dtb, dt_bias), (a_neg, a_log), (dskip, d_skip), (sink, sinks)):
                sp.dma_start(to[:, :], what[0:1, :].to_broadcast([P, HEADS])).then_inc(small_loaded, 16)

            def ada_tiles(m):
                for k in range(KT):
                    if not (isinstance(m, int) and k < 4):
                        sp.wait_ge(ada_used, m * KT + k - 3)
                    sp.dma_start(ada[:, k % 4, :], w_ada[k * P:(k + 1) * P, bass.ts(m, D)]).then_inc(ada_full[k % 4], 16)

            ada_tiles(0)
            sp.dma_start(h_cols[:, :, :], x_cols[:, :, :]).then_inc(x_loaded, 16)
            with sp.Fori(1, MODS) as m:
                ada_tiles(m)

            def weights(slot, what):
                sp.dma_start(wt[:, slot, :], what).then_inc(wt_full[slot], 16)

            sp.wait_ge(mod_ready, MODS)
            for slot in range(4):
                weights(slot, w_out[slot, :, :])
            sp.wait_ge(yt_dve, TB)
            sp.wait_ge(yt_act, TB)
            sp.dma_start(x1, x_rows.rearrange("(b p) d -> p b d", p=P)).then_inc(x1_loaded, 16)
            for to, what in ((ln1gb, ln1_g), (ln1bb, ln1_b)):
                sp.dma_start(to, what[0:1, :].to_broadcast([P, D])).then_inc(ln1_loaded, 16)
            sp.dma_start(key_t, keys[:, :]).then_inc(key_loaded, 16)
            with sp.Fori(1, 8) as i:
                for slot in range(4):
                    sp.wait_ge(wout_split, i * 4 + (slot - 3))
                    weights(slot, w_out[bass.ds(i * 4 + slot, 1), :, :].rearrange("a p n -> (a p) n"))
            for slot in range(4):
                sp.wait_ge(wout_split, 29 + slot)
                weights(slot, w_q[slot, :, :])
            with sp.Fori(1, 4) as i:
                for slot in range(4):
                    sp.wait_ge(wt_used, i * 4 + (slot - 3))
                    weights(slot, w_q[bass.ds(i * 4 + slot, 1), :, :].rearrange("a p n -> (a p) n"))
            sp.wait_ge(h2_ready, TB)
            sp.dma_start(x1_out[:, :, :], x1).then_inc(x1_stored, 16)
            def store_gates(m):
                for n in range((m - 1) * P // TG, m * P // TG):
                    sp.wait_ge(g_staged, 2 + (n + 1) * TG // 4)
                    sp.dma_start(gates_out[:, n, :, :], stage[:, n % 2, :, :]).then_inc(g_stored[n % 2], 16)

            sp.wait_ge(q_ps, PH)
            sp.sem_inc(pre_split, RAWS)
            for m in range(TB):
                with sp.Fori(0, WIN_PAIRS) as i:
                    for j in range(4):
                        sp.wait_ge(pre_split, i * 4 + (m * WIN_UNITS + j + 1))
                        sp.dma_start(pre_raw[:, j, :], u_units[bass.ds(i * 4 + (m * WIN_UNITS + j), 1), :, :].rearrange("a p n -> (a p) n"))\
                            .then_inc(pre_full[j], 16)
                if 0 < m < DB:
                    store_gates(m)
                if m == DB:
                    sp.wait_ge(topk_done, TB)
                    v_tiles = v_tab.rearrange("(a b) d -> b a d", b=NKEY)
                    for j in range(RAWS):
                        sp.dma_start(raw[:, j, :], v_tiles[j, :, 0:UNIT]).then_inc(raw_full[j], 16)
                    store_gates(m)
            for i in range(2):
                sp.wait_ge(g_stored[i], 16 * (1 + DT // TG // 2))
                sp.wait_ge(acts_stored[i], 16 * (1 + AHEAD * GT // 2))
            sp.wait_ge(x1_stored, 16)

            def read_back(g, i):
                if not (g.kind == "start" and i < 2):
                    sp.wait_ge(w_ready, g.val(GT, i - 1))
                sp.dma_start(gel[:, i % 2, :], acts_out[bass.ds(g.val(GT, i), 1), :, :].rearrange("a p n -> (a p) n"))\
                    .then_inc(gel_full[i % 2], 16)

            def group(g):
                if g.kind != "last":
                    if not (g.kind == "start" or g.second):
                        sp.wait_ge(w_made, g.val(GT, -GT))
                    buf = g.c % 2
                    sp.dma_start(gm[:, buf, :, :], gates_out[:, :, bass.ds(g.val(GT), GT), :].rearrange("p a b c -> p a (b c)"))\
                        .then_inc(gm_full[buf], 16)
                if g.kind == "start":
                    for i in range(GT):
                        read_back(g, i)
                for j, (table, i, half) in enumerate(g.units):
                    if g.kind == "ahead" and j % 2 == 0:
                        read_back(g, j // 2)
                    slot = j % RAWS
                    if g.second and j < RAWS:
                        continue
                    sp.wait_ge(unit_split, g.unit(j - RAWS + 1))
                    if table == "u":
                        what = u_units[bass.ds(g.val(2 * GT, 2 * i + half), 1), :, :]
                    else:
                        what = v_tiles[bass.ds(g.val(GT, i - GT), 1), :, half * UNIT:(half + 1) * UNIT]
                    sp.dma_start(raw[:, slot, :], what.rearrange("a p n -> (a p) n")).then_inc(raw_full[slot], 16)

            stream(sp, group)
            sp.wait_ge(unit_used, Group("last", GROUPS).unit(0))
            sp.dma_start(x1_back, x1_out[:, :, :]).then_inc(tail_loaded, 16)
            for to, what in ((ln2gb, ln2_g), (ln2bb, ln2_b)):
                sp.dma_start(to, what[0:1, :].to_broadcast([P, D])).then_inc(tail_loaded, 16)
            for m in range(TB):
                sp.wait_ge(y_ready, m + 1)
                sp.dma_start(out[m * P:(m + 1) * P, :], out4[:, m, :]).then_inc(out_done, 16)
            sp.wait_ge(out_done, 16 * TB)

        @block.gpsimd
        def _(pool):
            for slot in range(2):
                pool.dma_start(win_raw[slot], w_slices[slot, :, :, :]).then_inc(win_full[slot], 16)
            nc.gpsimd.memset(ones[:, :], 1.0).then_inc(consts, 1)
            nc.gpsimd.memset(ident[:, :], 0.0).then_inc(consts, 1)
            nc.gpsimd.memset(band[:, :], 0.0).then_inc(consts, 1)
            for f in range(NF):
                nc.gpsimd.memset(inv[:, f:f + 1], float(THETA ** (-2.0 * f / ROT))).then_inc(consts, 1)
            nc.gpsimd.iota(iota[:, :], pattern=[[1, NKEY]], base=0, channel_multiplier=0,
                           allow_small_or_imprecise_dtypes=True).then_inc(consts, 1)
            pool.wait_ge(consts, 12)
            nc.gpsimd.affine_select(out=tri[:, :], in_=ones[:, :], compare_op=ALU.is_ge, fill=0.0, base=0,
                                    pattern=[[1, P]], channel_multiplier=-1).then_inc(consts2, 1)
            nc.gpsimd.affine_select(out=ident[:, :], in_=ident[:, :], compare_op=ALU.not_equal, fill=1.0, base=0,
                                    pattern=[[-1, P]], channel_multiplier=1).then_inc(consts2, 1)
            nc.gpsimd.affine_select(out=band[:, :], in_=band[:, :], compare_op=ALU.is_gt, fill=NEG, base=0,
                                    pattern=[[1, 2 * P]], channel_multiplier=-1).then_inc(consts2, 1)
            pool.wait_ge(consts2, 3)
            nc.gpsimd.affine_select(out=band[:, :], in_=band[:, :], compare_op=ALU.is_ge, fill=NEG, base=P,
                                    pattern=[[-1, 2 * P]], channel_multiplier=1).then_inc(consts2, 1)
            pool.wait_ge(consts2, 4)
            nc.gpsimd.memset(mask_now[:, 0:P], NEG).then_inc(consts2, 1)
            nc.gpsimd.tensor_copy(mask_now[:, P:2 * P], band[:, P:2 * P]).then_inc(consts2, 1)

            def win_low(i, more):
                for slot in range(2):
                    for j in range(2):
                        pool.wait_ge(win_high, i * 4 + (2 * slot + j + 1))
                        nc.gpsimd.tensor_tensor(win_parts[:, j, 1, :], win_raw[slot][:, j, :], win_parts[:, j, 0, :].bitcast(F32), ALU.subtract)\
                            .then_inc(win_split, 1)
                    if more:
                        pool.wait_ge(win_split, i * 4 + (2 * slot + 2))
                        pool.sem_inc(win_held, 1)
                        pool.dma_start(win_raw[slot], w_slices[bass.ds(i * 2 + (slot + 2), 1), :, :, :].rearrange("a p k n -> (a p) k n"))\
                            .then_inc(win_full[slot], 16)

            with pool.Fori(0, KT // 4) as i:
                win_low(i, True)
            pool.wait_ge(h_split, KT)
            nc.gpsimd.memset(x_raw[:, :, 0:CONV - 1], 0.0).then_inc(pads_zero, 1)
            with pool.Fori(KT // 4, SLICES * KT // 4 - 1) as i:
                win_low(i, True)
            win_low(SLICES * KT // 4 - 1, False)

            with pool.Fori(0, 2 * KT // 4) as i:
                for j in range(4):
                    pool.wait_ge(wout_high, i * 4 + (j + 1))
                    nc.gpsimd.tensor_tensor(wout_parts[:, j % 2, 1, :], wt[:, j, :], wout_parts[:, j % 2, 0, :].bitcast(F32), ALU.subtract)\
                        .then_inc(wout_split, 1)

            for m in range(TB):
                with pool.Fori(0, WIN_PAIRS) as i:
                    for j in range(4):
                        pool.wait_ge(pre_high, i * 4 + (m * WIN_UNITS + j + 1))
                        nc.gpsimd.tensor_tensor(split[:, j % 2, 1, :], pre_raw[:, j, :], split[:, j % 2, 0, :].bitcast(F32), ALU.subtract)\
                            .then_inc(pre_split, 1)
                if m:
                    with pool.Fori((m - 1) * P // (2 * OH), m * P // (2 * OH)) as i:
                        for buf in range(2):
                            pool.wait_ge(hot_ready, i * 2 + (buf + 1))
                            pool.sem_inc(spread, 1)
                            rows = one_hot[:, buf, 1, :, :]
                            nc.gpsimd.tensor_tensor(rows, rows, over(pick_cols[:, 2, bass.ds(i * (2 * OH) + buf * OH, OH)], 2, NKEY), ALU.mult)\
                                .then_inc(hot_gated, 1)

            pool.wait_ge(topk_done, TB)
            pool.wait_ge(g_ps, DT // 4 + 2 * OH // 4)
            pool.wait_ge(pre_split, AHEAD * GT * 2 + RAWS)
            for i in range(2):
                pool.wait_ge(acts_stored[i], 16 * (1 + AHEAD * GT // 2))
            with pool.Fori(0, GROUPS) as i:
                for t, table in enumerate((u_tab, v_tab)):
                    for slot in range(SLOTS):
                        count = i * (2 * SLOTS) + (t * SLOTS + slot + 1)
                        pool.wait_ge(row_used, count)
                        pool.sem_inc(idx_held, 1)
                        nc.gpsimd.tensor_copy(idx[:, slot:slot + 1], ids[:, DB, bass.ds(i * SLOTS + slot, 1)]).then_inc(idx_copied, 1)
                        pool.wait_ge(idx_copied, count)
                        pool.sem_inc(idx_held, 1)
                        nc.gpsimd.indirect_dma_start(
                            out=ring[slot], out_offset=None, in_=table[:, :],
                            in_offset=bass.IndirectOffsetOnAxis(ap=idx[:, slot:slot + 1], axis=0),
                        ).then_inc(ring_full[slot], 16)

            pool.wait_ge(tail_loaded, 3 * 16)
            for m in range(TB):
                row = out4[:, m, :]
                pool.wait_ge(y_normed, m + 1)
                nc.gpsimd.tensor_tensor(row, row, ln2gb, ALU.mult).then_inc(y_gained, 1)
                pool.wait_ge(y_gained, m + 1)
                nc.gpsimd.tensor_tensor(row, row, ln2bb, ALU.add).then_inc(y_ready, 1)

        @block.scalar
        def _(act):
            own = Steps(act, act_own)
            act.wait_ge(c_loaded, 16)
            nc.scalar.activation(c_act[:, :], c_tmp[:, :], ACT.Exp, scale=-1.0).then_inc(c_exp, 1)
            act.wait_ge(ang_ready, 1)
            nc.scalar.activation(trig[:, :, :, :].rearrange("p a b c -> p (a b c)"),
                                 ang[:, :, :, :].rearrange("p a b c -> p (a b c)"), ACT.Sin).then_inc(trig_ready, 1)
            act.sem_inc(proj_bank_free, 4)

            def win_high_part(s, k):
                act.wait_ge(win_full[k // 2 % 2], s * (16 * KT // 4) + 16 * (k // 4 + 1))
                if k >= 2 or not isinstance(s, int) or (s and k == 0):
                    act.wait_ge(win_used, s * (KT - 1) + max(k - 1, 0))
                nc.scalar.activation(win_parts[:, k % 2, 0, :], win_raw[k // 2 % 2][:, k % 2, :], ACT.Copy).then_inc(win_high, 1)

            def slice_parts(s, copied):
                win_high_part(s, 0)
                for m in range(4):
                    act.wait_ge(proj_done, s * 4 + (m - 3))
                    cols, to = copied(m)
                    nc.scalar.activation(to, ps[:, m, 0:cols], ACT.Copy).then_inc(proj_bank_free, 1)
                for k in range(1, KT):
                    win_high_part(s, k)

            def conv_in(s):
                return lambda m: (512, x_raw[:, bass.ds(s * 4 + m, 1), CONV - 1:].rearrange("p a s -> p (a s)"))

            def rows_in(n):
                return lambda m: (512, qz[:, m, n * 512:(n + 1) * 512])

            win_high_part(0, 0)
            win_high_part(0, 1)
            for k in range(KT):
                act.wait_ge(h_ready, k + 1)
                nc.scalar.activation(h_parts[:, 0, k, :], h_cols[:, k, :], ACT.Copy).then_inc(h_high, 1)
            for k in range(2, KT):
                win_high_part(0, k)
            with act.Fori(1, 3) as s:
                slice_parts(s, conv_in(s - 1))
            slice_parts(3, conv_in(2))
            slice_parts(4, lambda m: (KVW + HEADS, kvdt[:, m, :]))
            slice_parts(5, rows_in(0))
            slice_parts(6, rows_in(1))
            for n in range(3):
                act.wait_ge(conv_ready, n + 1)
                part = x_conv[:, 4 * n:4 * n + 4, :]
                nc.scalar.activation(part, part, ACT.Silu).then_inc(silu_done, 1)
            slice_parts(7, rows_in(2))
            for m in range(4):
                act.wait_ge(proj_done, 28 + m + 1)
                nc.scalar.activation(qz[:, m, 3 * 512:], bank(m), ACT.Copy).then_inc(proj_bank_free, 1)
            act.wait_ge(proj_bank_free, 4 + 32)
            gate = qz[:, :, AW:]
            nc.scalar.activation(gate, gate, ACT.Silu).then_inc(z_done, 1)
            act.wait_ge(dt_in, 1)
            own(nc.scalar.activation(dt_abs[:, :, :], dt_abs[:, :, :], ACT.Exp, scale=-1.0))
            nc.scalar.activation(dt_abs[:, :, :], dt_abs[:, :, :], ACT.Ln, bias=1.0).then_inc(dt_log, 1)
            nc.scalar.activation(a_neg[:, :], a_neg[:, :], ACT.Exp).then_inc(a_exp, 1)

            def roots(n):
                act.wait_ge(var_ready, n + 1)
                nc.scalar.activation(root[:, :], var[:, :], ACT.Ln).then_inc(act_own, 1)
                act.wait_ge(act_own, n + 2)
                nc.scalar.activation(root[:, :], root[:, :], ACT.Exp, scale=-0.5).then_inc(root_ready, 1)

            def exps(b, u):
                act.wait_ge(mx_ready, b * 4 + (u + 1))
                nc.scalar.activation(es[:, u % 2, :], es[:, u % 2, :], ACT.Exp)
                for i in range(4):
                    row = lg[:, u % 2, i // 2, i % 2, :]
                    ins = nc.scalar.activation(row, row, ACT.Exp, bias=mx[:, u % 2, i:i + 1], accum_out=den[:, u % 2, i:i + 1])
                ins.then_inc(exp_done, 1)

            def p_turned(b, u):
                act.wait_ge(pt_ps, b * 4 + (u + 1))
                nc.scalar.activation(p_t[:, u % 2, :, :], wide(2, 8, P), ACT.Copy).then_inc(pt_ready, 1)

            with act.Fori(0, TB) as b:
                act.wait_ge(qt_ps, b + 1)
                nc.scalar.activation(q_t, wide(2, HEADS // 2, P), ACT.Copy).then_inc(q_ready, 1)
                act.wait_ge(xs_ps, b + 1)
                nc.scalar.activation(xs_row, wide(4, HEADS, HD), ACT.Copy).then_inc(xs_ready, 1)
                act.wait_ge(ssd_small, b + 1)
                nc.scalar.activation(ea, acum, ACT.Exp)
                nc.scalar.activation(cdec, alast, ACT.Exp)
                nc.scalar.activation(dte, dte, ACT.Exp).then_inc(ssd_exp, 1)
                exps(b, 0)
                exps(b, 1)
                p_turned(b, 0)
                exps(b, 2)
                p_turned(b, 1)
                exps(b, 3)
                p_turned(b, 2)
                p_turned(b, 3)
                for c in range(4):
                    act.wait_ge(seg_in, b * 4 + (c + 1))
                    nc.scalar.activation(decay[:, c % 2, :, :], decay[:, c % 2, :, :], ACT.Exp).then_inc(seg_exp, 1)
                act.wait_ge(yt_ps, b * 2 + 1)
                nc.scalar.activation(y_t[:, 0:8, bass.ts(b, P)], wide(0, 8, P), ACT.Copy).then_inc(yt_act, 1)
                act.wait_ge(y_gated, b + 1)
                for g in range(KV):
                    ins = nc.scalar.activation(decay[:, g, :, :], tmp[:, g * GH:(g + 1) * GH, :].rearrange("p a b -> p (a b)")
                                               .rearrange("p (a b) -> p a b", b=P), ACT.Square, accum_out=ss[:, g:g + 1])
                ins.then_inc(ss_ready, 1)
                roots(b)

            act.wait_ge(yt_act, TB)
            act.wait_ge(yt_dve, TB)
            for half in range(2):
                part = slice(half * 8, half * 8 + 8)
                nc.scalar.activation(y_high[:, part, :], y_t[:, part, :], ACT.Copy).then_inc(y_high_done, 1)
            for i, row in enumerate((g1b, sc2b, sh2b)):
                act.wait_ge(row_ps, i + 1)
                nc.scalar.activation(row, wide(4 * (i % 2), D), ACT.Copy).then_inc(row_ready, 1)
            act.wait_ge(y_split, 2)
            act.sem_inc(wout_used, 2)
            with act.Fori(0, 2 * KT // 4) as i:
                for j in range(4):
                    act.wait_ge(wt_full[j], i * 16 + 16)
                    act.wait_ge(wout_used, i * 4 + (j + 1))
                    nc.scalar.activation(wout_parts[:, j % 2, 0, :], wt[:, j, :], ACT.Copy).then_inc(wout_high, 1)
            for m in range(TB + 1):
                if m < TB:
                    roots(TB + m)
                if m:
                    act.wait_ge(h2t_ps, m)
                    nc.scalar.activation(h2_t[:, :, (m - 1) * P:m * P], wide(4 * ((m - 1) % 2), KT, P), ACT.Copy).then_inc(h2t_ready, 1)
            act.wait_ge(h2t_ready, TB)
            nc.scalar.activation(h2_parts[:, 0, :, :], h2_t_dense, ACT.Copy).then_inc(h2_high, 1)
            for h in range(PH):
                act.wait_ge(q_ps, h + 1)
                nc.scalar.activation(q8[:, h, :], bank(h), ACT.Copy).then_inc(q8_ready, 1)
            act.wait_ge(h2_split, 1)
            act.sem_inc(g_stored[0], 16)
            act.sem_inc(g_stored[1], 16)
            act.wait_ge(x1_stored, 16)

            def scores(m):
                act.wait_ge(sc_ps, m + 1)
                if m:
                    act.wait_ge(sc_used, m)
                nc.scalar.activation(sc, wide(0, 2, PH, NKEY), ACT.Copy).then_inc(sc_ready, 1)

            def gates_by_expert(m):
                with act.Fori(0, P // (2 * TG)) as i:
                    for st in range(2):
                        act.wait_ge(g_stored[st], i * 16 + 16 * (m * (P // TG // 2) + 1))
                        for q in range(TG // 4):
                            act.wait_ge(g_ps, i * (2 * TG // 4) + (m * P + st * TG) // 4 + (2 * OH // 4 + q + 1))
                            nc.scalar.activation(stage[:, st, :, 4 * q:4 * q + 4], wide(4 + q % 2, 4, NKEY).rearrange("p t i -> p i t"), ACT.Copy)\
                                .then_inc(g_staged, 1)

            def ahead(m):
                def gelu(i, b):
                    tiles = i * 2 + (m * 2 * WIN_PAIRS + b + 1)
                    act.wait_ge(pre_used, i * 4 + (m * WIN_UNITS + 2 * b + 2 + 2))
                    act.wait_ge(acts_stored[b], i * 16 + 16 * (m * WIN_PAIRS + 1))
                    nc.scalar.activation(pre_gel[:, b, :], ps[:, 6 + b, 0:DT], ACT.Gelu).then_inc(pre_gelu, 1)
                    act.wait_ge(pre_gelu, tiles + 2)
                    act.dma_start(acts_out[bass.ds(tiles - 1, 1), :, :].rearrange("a p n -> (a p) n"), pre_gel[:, b, :])\
                        .then_inc(acts_stored[b], 16)

                def pair(i, first):
                    for j in range(4):
                        act.wait_ge(pre_full[j], i * 16 + 16 * (m * WIN_PAIRS + 1))
                        act.wait_ge(pre_used, i * 4 + (m * WIN_UNITS + j + 1))
                        nc.scalar.activation(split[:, j % 2, 0, :], pre_raw[:, j, :], ACT.Copy).then_inc(pre_high, 1)
                        if j == 1 and not first:
                            gelu(i - 1, 1)
                        if j == 3:
                            gelu(i, 0)

                pair(0, True)
                with act.Fori(1, WIN_PAIRS) as i:
                    pair(i, False)
                gelu(WIN_PAIRS - 1, 1)

            act.sem_inc(pre_used, 2)
            for i in range(2):
                act.sem_inc(acts_stored[i], 16)
            scores(0)
            for m in range(TB):
                ahead(m)
                act.wait_ge(pair_sub, m + 1)
                nc.scalar.activation(pair_v, pair_v, ACT.Exp).then_inc(pair_exp, 1)
                if m + 1 < TB:
                    scores(m + 1)
                    act.wait_ge(cols_ps, m + 1)
                    nc.scalar.activation(pick_cols[:, :, m * P:(m + 1) * P], ps[:, 6, 0:3 * P].rearrange("p (a b) -> p a b", a=3), ACT.Copy)\
                        .then_inc(cols_ready, 1)
                if m:
                    gates_by_expert(m - 1)

            def group(g):
                buf = g.c % 2
                for j in g.steps():
                    if g.units:
                        act.wait_ge(raw_full[j % RAWS], g.unit(0) * 4 + (16 * (j // RAWS + 1)))
                        if not (g.second and j < 2):
                            act.wait_ge(unit_used, g.unit(j - 1))
                        nc.scalar.activation(split[:, j % 2, 0, :], raw[:, j % RAWS, :], ACT.Copy).then_inc(high_done, 1)
                    if j == 1:
                        act.wait_ge(dots_done, g.val(1))
                        nc.scalar.activation(act4, act4, ACT.Gelu).then_inc(gelu_done, 1)
                    for i, due in g.tiles_at(j):
                        if due == "gelu":
                            act.wait_ge(unit_used, g.unit(g.units.index(("u", i, 1)) + 1))
                            act.wait_ge(w_ready, g.val(GT, i - 1))
                            nc.scalar.activation(gel[:, i % 2, :], ps[:, 6 + i % 2, 0:DT], ACT.Gelu).then_inc(tile_gelu, 1)
                        if due == "high":
                            act.wait_ge(w_made, g.val(GT, i + 1))
                            nc.scalar.activation(w_parts[:, buf, 0, i, :], gel[:, i % 2, :], ACT.Copy).then_inc(w_high, 1)

            stream(act, group)
            for half in range(2):
                act.wait_ge(tail_row, half + 1)
                nc.scalar.activation(g2b[:, half * 1024:(half + 1) * 1024], wide(6, 1024), ACT.Copy).then_inc(tail_row_ready, 1)
            with act.Fori(0, TB) as m:
                roots(m + 2 * TB)

        @block.vector
        def _(dve):
            own = Steps(dve, dve_own)
            dve.wait_ge(c_exp, 1)
            own(nc.vector.tensor_scalar(c_act[:, :], c_act[:, :], 1.0, None, ALU.add))
            own(nc.vector.reciprocal(c_act[:, :], c_act[:, :]))
            own(nc.vector.tensor_tensor(c_act[:, :], c_act[:, :], c_tmp[:, :], ALU.mult))

            dve.wait_ge(small_loaded, 9 * 16)
            dve.wait_ge(consts, 12)
            ang0 = ang[:, 0, :, :].rearrange("p a b -> p (a b)")
            ang1 = ang[:, 1, :, :].rearrange("p a b -> p (a b)")
            tn = turns[:, 0, :, :].rearrange("p a b -> p (a b)")
            tn1 = turns[:, 1, :, :].rearrange("p a b -> p (a b)")
            pos_f = turns[:, 1, :, 0]
            own(nc.vector.tensor_copy(pos_f, pos_i[:, :]))
            own(nc.vector.tensor_tensor(ang[:, 0, :, :], over(pos_f, 2, NF), over(inv[:, :], 1, TB), ALU.mult))
            own(nc.vector.tensor_scalar(tn, ang0, 1.0 / (2 * math.pi), None, ALU.mult))
            own(nc.vector.tensor_scalar(tn, tn, 12582912.0, None, ALU.add))
            own(nc.vector.tensor_scalar(tn, tn, -12582912.0, None, ALU.add))
            two_pi, part = 2 * math.pi, 6.28125
            part2 = round((two_pi - part) * 2 ** 19) / 2 ** 19
            for piece in (part, part2, two_pi - part - part2):
                own(nc.vector.scalar_tensor_tensor(ang0, tn, -piece, ang0, ALU.mult, ALU.add))
            own(nc.vector.tensor_scalar(ang1, ang0, math.pi / 2, None, ALU.add))
            own(nc.vector.tensor_scalar(tn1, ang1, math.pi, -two_pi, ALU.is_gt, ALU.mult))
            own(nc.vector.tensor_tensor(ang1, ang1, tn1, ALU.add))
            both = ang[:, :, :, :].rearrange("p a b c -> p (a b c)")
            nc.vector.tensor_scalar(both, both, 3.1415925, -3.1415925, ALU.min, ALU.max).then_inc(ang_ready, 1)
            for m in (1, 4):
                part = b_cols[:, m * KT:(m + 2) * KT]
                own(nc.vector.tensor_scalar(part, part, 1.0, None, ALU.add))

            def modulation(m):
                for k in range(KT):
                    dve.wait_ge(ada_full[k % 4], m * (16 * KT // 4) + 16 * (k // 4 + 1))
                    if k == 0:
                        nc.vector.tensor_scalar(acc, ada[:, 0, :], c_act[:, 0:1], None, ALU.mult).then_inc(ada_used, 1)
                    else:
                        dve.wait_ge(ada_used, m * KT + k)
                        nc.vector.scalar_tensor_tensor(acc, ada[:, k % 4, :], c_act[:, k:k + 1], acc, ALU.mult, ALU.add)\
                            .then_inc(ada_used, 1)
                dve.wait_ge(mod_sum, m + 1)
                nc.vector.tensor_tensor(mod_cols[:, bass.ts(m, KT)], ps[:, 4, 0:KT], b_cols[:, bass.ts(m, KT)], ALU.add)\
                    .then_inc(mod_ready, 1)

            with dve.Fori(0, 2) as m:
                modulation(m)
            dve.wait_ge(mod_ready, 2)
            dve.wait_ge(x_loaded, 16)
            for k in range(KT + 1):
                if k < KT:
                    nc.vector.tensor_scalar(h_cols[:, k, :], h_cols[:, k, :], mod_cols[:, KT + k:KT + k + 1], mod_cols[:, k:k + 1],
                                            ALU.mult, ALU.add).then_inc(h_ready, 1)
                if k:
                    dve.wait_ge(h_high, k)
                    nc.vector.tensor_tensor(h_parts[:, 1, k - 1, :], h_cols[:, k - 1, :], h_parts[:, 0, k - 1, :].bitcast(F32), ALU.subtract)\
                        .then_inc(h_split, 1)

            dve.wait_ge(pads_zero, 1)
            with dve.Fori(0, 3) as n:
                modulation(n + 2)
                dve.wait_ge(proj_bank_free, n * 4 + 8)
                for m in range(4):
                    tile = n * 4 + m
                    src = x_raw[:, bass.ds(tile, 1), :].rearrange("p a s -> p (a s)")
                    dst = x_conv[:, bass.ds(tile, 1), :].rearrange("p a s -> p (a s)")
                    base = own.base + own.n + n * 15 + m * 4
                    for j in range(CONV):
                        w = convw[:, bass.ds(tile * CONV + j, 1)]
                        if j == 0:
                            ins = nc.vector.tensor_scalar(dst, src[:, 0:S], w, convb[:, bass.ds(tile, 1)], ALU.mult, ALU.add)
                        else:
                            dve.wait_ge(dve_own, base + j)
                            ins = nc.vector.scalar_tensor_tensor(dst, src[:, j:j + S], w, dst, ALU.mult, ALU.add)
                        ins.then_inc(conv_ready if m == 3 and j == 3 else dve_own, 1)
            own.n += 3 * 15
            modulation(5)

            dve.wait_ge(proj_done, 32)
            nc.vector.memset(k_t, 0.0)
            nc.vector.memset(vv, 0.0)
            nc.vector.memset(state, 0.0)
            dve.wait_ge(proj_bank_free, 20)
            own(nc.vector.tensor_tensor(dt_all[:, :, :], kvdt[:, :, KVW:], over(dtb[:, :], 1, TB), ALU.add))
            nc.vector.scalar_tensor_tensor(dt_abs[:, :, :], dt_all[:, :, :], -1.0, dt_all[:, :, :], ALU.mult, ALU.max).then_inc(dt_in, 1)
            dve.wait_ge(dt_log, 1)
            own(nc.vector.scalar_tensor_tensor(dt_all[:, :, :], dt_all[:, :, :], 0.0, dt_abs[:, :, :], ALU.max, ALU.add))
            dve.wait_ge(a_exp, 1)
            own(nc.vector.scalar_tensor_tensor(da_all[:, :, :], over(a_neg[:, :], 1, TB), -1.0, dt_all[:, :, :],
                                               ALU.mult, ALU.mult))
            dve.wait_ge(silu_done, 3)
            dve.wait_ge(z_done, 1)
            dve.wait_ge(trig_ready, 1)
            dve.wait_ge(consts2, 6)

            def logits(b, u, step):
                i = u % 2
                dve.wait_ge(lg_done, b * 4 + (u + 1))
                rows = lg[:, i, :, :, :].rearrange("p a b k -> p (a b) k")
                nc.vector.scalar_tensor_tensor(rows, wide(0, 4, 2 * P), HD ** -0.5, over(mask_now[:, :], 1, 4), ALU.mult, ALU.add)\
                    .then_inc(lg_read, 1)
                dve.wait_ge(lg_read, b * 4 + (u + 1))
                step(nc.vector.tensor_reduce(mx[:, i, :], rows, AX, ALU.max))
                s4 = sink[:, 4 * u:4 * u + 4].rearrange("p (a b) -> p b a", b=2)
                m4 = mx[:, i, :].rearrange("p (b a) -> p b a", b=2)
                e4 = es[:, i, :].rearrange("p (b a) -> p b a", b=2)
                step(nc.vector.tensor_tensor(m4, m4, s4, ALU.max))
                nc.vector.tensor_tensor(e4, s4, m4, ALU.subtract)
                nc.vector.tensor_scalar(mx[:, i, :], mx[:, i, :], -1.0, None, ALU.mult).then_inc(mx_ready, 1)

            def attended(b, u, step):
                i = u % 2
                dve.wait_ge(pv_done, b * 4 + (u + 1))
                step(nc.vector.tensor_tensor(den[:, i, :], den[:, i, :], es[:, i, :], ALU.add))
                step(nc.vector.reciprocal(den[:, i, :], den[:, i, :]))
                src = ps[:, 4 + u // 2, (u % 2) * 256:(u % 2) * 256 + 256].rearrange("p (a b d) -> p a b d", a=2, b=2)
                dst = y_row[:, u * 256:u * 256 + 256].rearrange("p (a b d) -> p a b d", a=2, b=2)
                r = over(den[:, i, :].rearrange("p (b a) -> p a b", b=2), 3, HD)
                nc.vector.tensor_tensor(dst, src, r, ALU.mult).then_inc(att_out, 1)

            def segment(b, c, step):
                dve.wait_ge(seg_ps, b * 4 + (c + 1))
                d = decay[:, c % 2, :, :]
                nc.vector.tensor_tensor(d, wide(c % 2, 4, P), over(acum[:, 4 * c:4 * c + 4], 2, P), ALU.subtract)\
                    .then_inc(seg_read, 1)
                dve.wait_ge(seg_read, b * 4 + (c + 1))
                nc.vector.tensor_scalar(d, d, 0.0, None, ALU.min).then_inc(seg_in, 1)

            def mixing(b, c):
                dve.wait_ge(seg_exp, b * 4 + (c + 1))
                nc.vector.tensor_tensor(m_t[:, 4 * c:4 * c + 4, :], decay[:, c % 2, :, :], over(cbm[:, c // 2, :], 1, 4), ALU.mult)\
                    .then_inc(m_ready, 1)

            def one_over_root(n, step):
                dve.wait_ge(root_ready, n + 1)
                step(nc.vector.tensor_tensor(root_t[:, :], root[:, :], root[:, :], ALU.mult))
                step(nc.vector.tensor_tensor(root_t[:, :], root_t[:, :], var[:, :], ALU.mult))
                step(nc.vector.tensor_scalar(root_t[:, :], root_t[:, :], -0.5, 1.5, ALU.mult, ALU.add))
                step(nc.vector.tensor_tensor(root[:, :], root[:, :], root_t[:, :], ALU.mult))

            start = own.n
            MIX_STEPS = 30
            with dve.Fori(0, TB) as b:
                step = Steps(dve, dve_own, b * MIX_STEPS + start)
                nc.vector.tensor_copy(cur, x_conv[:, :, bass.ts(b, P)])
                nc.vector.tensor_copy(qk[:, 0:HEADS, :].rearrange("p a b -> p (a b)"), qz[:, bass.ds(b, 1), 0:AW].rearrange("p a b -> p (a b)"))
                nc.vector.tensor_copy(qk[:, HEADS:, :].rearrange("p a b -> p (a b)"), kvdt[:, bass.ds(b, 1), 0:KV * HD].rearrange("p a b -> p (a b)"))
                nc.vector.tensor_copy(da_now, da_all[:, bass.ds(b, 1), :].rearrange("p a b -> p (a b)"))
                step(nc.vector.tensor_copy(trig_now, trig[:, :, bass.ds(b, 1), :].rearrange("p a b c -> p a (b c)")))
                t1, t2 = qk[:, :, 0:NF], qk[:, :, NF:ROT]
                sn, cs = over(trig_now[:, 0, :], 1, HEADS + KV), over(trig_now[:, 1, :], 1, HEADS + KV)
                for i, (t, f) in enumerate(((t1, cs), (t2, sn), (t2, cs), (t1, sn))):
                    ins = nc.vector.tensor_tensor(rope_tmp[:, i, :, :], t, f, ALU.mult)
                step(ins)
                nc.vector.tensor_tensor(t1, rope_tmp[:, 0, :, :], rope_tmp[:, 1, :, :], ALU.subtract)
                step(nc.vector.tensor_tensor(t2, rope_tmp[:, 2, :, :], rope_tmp[:, 3, :, :], ALU.add))
                nc.vector.tensor_copy(k_t[:, :, 0:P], k_t[:, :, P:2 * P])
                step(nc.vector.tensor_copy(vv[:, 0, :], vv[:, 1, :]))
                nc.vector.tensor_copy(vv[:, 1, :], kvdt[:, bass.ds(b, 1), KV * HD:KVW].rearrange("p a b -> p (a b)"))
                nc.vector.tensor_copy(kdup, over(qk[:, HEADS:, :], 2, 2)).then_inc(block_in, 1)
                dve.wait_ge(kb_ps, b + 1)
                nc.vector.tensor_copy(k_t[:, :, P:2 * P], ps[:, 6, 0:256].rearrange("p (a b) -> p a b", a=2))
                nc.vector.tensor_copy(b_row, ps[:, 6, 256:512].rearrange("p (a b) -> p a b", a=2))
                dve.wait_ge(cb_ps, b + 1)
                nc.vector.tensor_copy(acum, ps[:, 7, 0:HEADS])
                step(nc.vector.tensor_copy(alast, ps[:, 7, HEADS:2 * HEADS]))
                nc.vector.tensor_tensor(dte, alast, acum, ALU.subtract).then_inc(ssd_small, 1)
                nc.vector.tensor_tensor(cbm, ps[:, 7, 128:384].rearrange("p (a b) -> p a b", a=2), over(tri[:, :], 1, 2), ALU.mult)\
                    .then_inc(kv_ready, 1)
                logits(b, 0, step)
                logits(b, 1, step)
                attended(b, 0, step)
                logits(b, 2, step)
                attended(b, 1, step)
                logits(b, 3, step)
                attended(b, 2, step)
                nc.vector.tensor_copy(mask_now[:, 0:P], band[:, 0:P])
                dve.wait_ge(xs_ready, b + 1)
                dt_b = dt_all[:, bass.ds(b, 1), :].rearrange("p a b -> p (a b)")
                step(nc.vector.tensor_tensor(xdt, xs_row, over(dt_b, 2, HD), ALU.mult))
                dve.wait_ge(ssd_exp, b + 1)
                nc.vector.tensor_tensor(xw, xdt, over(dte, 2, HD), ALU.mult).then_inc(xw_ready, 1)
                segment(b, 0, step)
                segment(b, 1, step)
                attended(b, 3, step)
                mixing(b, 0)
                segment(b, 2, step)
                mixing(b, 1)
                segment(b, 3, step)
                mixing(b, 2)
                mixing(b, 3)
                dve.wait_ge(st_ps, b + 1)
                step(nc.vector.tensor_tensor(tmp, state, over(cdec, 2, HD), ALU.mult))
                nc.vector.tensor_tensor(state, tmp, wide(2, HEADS, HD), ALU.add).then_inc(state_new, 1)
                dve.wait_ge(state_new, b + 1)
                dve.wait_ge(y_ps, b + 1)
                nc.vector.tensor_tensor(xw, xs_row, over(dskip[:, :], 2, HD), ALU.mult)
                step(nc.vector.tensor_tensor(tmp, wide(4, HEADS, HD), over(ea, 2, HD), ALU.mult))
                step(nc.vector.tensor_tensor(tmp, tmp, wide(6, HEADS, HD), ALU.add))
                step(nc.vector.tensor_tensor(tmp, tmp, xw, ALU.add))
                z_b = qz[:, bass.ds(b, 1), AW:].rearrange("p a (h d) -> p (a h) d", d=HD)
                nc.vector.tensor_tensor(tmp, tmp, z_b, ALU.mult).then_inc(y_gated, 1)
                dve.wait_ge(ss_ready, b + 1)
                nc.vector.tensor_scalar(var[:, :], ss, 1.0 / (GH * HD), EPS, ALU.mult, ALU.add).then_inc(var_ready, 1)
                one_over_root(b, step)
                for g in range(KV):
                    ins = nc.vector.tensor_scalar(y_row[:, AW + g * 512:AW + (g + 1) * 512],
                                                  tmp[:, g * GH:(g + 1) * GH, :].rearrange("p a b -> p (a b)"), root[:, g:g + 1], None, ALU.mult)
                ins.then_inc(y_rows, 1)
                dve.wait_ge(yt_ps, b * 2 + 2)
                nc.vector.tensor_tensor(y_t[:, 8:16, bass.ts(b, P)], wide(2, 8, P), over(normw[:, :], 2, P), ALU.mult).then_inc(yt_dve, 1)
                assert step.n == MIX_STEPS, step.n
            own.n += TB * MIX_STEPS

            for half in range(2):
                part = slice(half * 8, half * 8 + 8)
                dve.wait_ge(y_high_done, half + 1)
                nc.vector.tensor_tensor(y_low[:, part, :], y_t[:, part, :], y_high[:, part, :].bitcast(F32), ALU.subtract).then_inc(y_split, 1)

            dve.sem_inc(mix_read, 4)
            dve.wait_ge(x1_loaded, 16)
            dve.wait_ge(row_ready, 3)
            for n in range(2):
                for m in range(TB):
                    cols = slice(n * 1024, (n + 1) * 1024)
                    dve.wait_ge(mix_ps, n * 4 + m + 1)
                    nc.vector.tensor_tensor(tmp2[:, 0:1024], wide(2 * m, 1024), g1b[:, cols], ALU.mult).then_inc(mix_read, 1)
                    dve.wait_ge(mix_read, 4 + n * 4 + m + 1)
                    own(nc.vector.scalar_tensor_tensor(x1[:, m, cols], x1[:, m, cols], ALPHA, tmp2[:, 0:1024], ALU.mult, ALU.add))

            def normalise(n, row, step):
                for j in range(4):
                    ins = nc.vector.bn_stats(stats[:, j, :], row[:, j * 512:(j + 1) * 512])
                step(ins)
                step(nc.vector.bn_aggr(mv, stats.rearrange("p a b -> p (a b)")))
                nc.vector.tensor_scalar(var[:, 0:1], mv[:, 1:2], EPS, None, ALU.add).then_inc(var_ready, 1)
                one_over_root(n, step)
                return nc.vector.tensor_scalar(row, row, mv[:, 0:1], root[:, 0:1], ALU.subtract, ALU.mult)

            dve.wait_ge(ln1_loaded, 2 * 16)
            start1 = own.n
            with dve.Fori(0, TB) as m:
                step = Steps(dve, dve_own, m * 10 + start1, held)
                row = x1[:, bass.ds(m, 1), :].rearrange("p a b -> p (a b)")
                h_row = h2[:, bass.ds(m, 1), :].rearrange("p a b -> p (a b)")
                step(normalise(m + TB, row, step))
                step(nc.vector.tensor_tensor(row, row, ln1gb, ALU.mult))
                step(nc.vector.tensor_tensor(row, row, ln1bb, ALU.add))
                step(nc.vector.tensor_tensor(h_row, row, sc2b, ALU.mult))
                nc.vector.tensor_tensor(h_row, h_row, sh2b, ALU.add).then_inc(h2_ready, 1)
                assert step.n == 10, step.n
            own.n += TB * 10

            def best16(rows, step):
                for values, _, source, _ in rows:
                    ins = nc.vector.max(values[:, 0:8], source)
                step(ins)
                for values, indices, source, scratch in rows:
                    nc.vector.max_index(indices[:, 0:8], values[:, 0:8], source)
                    ins = nc.vector.match_replace(scratch, values[:, 0:8], source, NEG)
                step(ins)
                for values, _, _, scratch in rows:
                    ins = nc.vector.max(values[:, 8:16], scratch)
                step(ins)
                for values, indices, _, scratch in rows:
                    ins = nc.vector.max_index(indices[:, 8:16], values[:, 8:16], scratch)
                step(ins)

            dve.wait_ge(h2_high, 1)
            nc.vector.tensor_tensor(h2_parts[:, 1, :, :], h2_t_dense, h2_parts[:, 0, :, :].bitcast(F32), ALU.subtract)\
                .then_inc(h2_split, 1)
            dve.sem_inc(parts_read, 1)
            start2 = own.n
            TOP_STEPS = 22
            dve.sem_inc(g_ps, 2 * OH // 4)

            def select(m):
                step = Steps(dve, dve_own, m * TOP_STEPS + start2, held)
                dve.wait_ge(sc_ready, m + 1)
                dve.sem_inc(held, 1)
                best16([(top_v[:, side, h, :], top_i[:, side, h, :], sc[:, side, h, :], rest[:, side, h, :])
                        for side in range(2) for h in range(PH)], step)
                step(nc.vector.tensor_copy(top_f, top_i))
                step(nc.vector.tensor_tensor(cand, over(top_v[:, 0, :, :], 3, PK), over(top_v[:, 1, :, :], 2, PK), ALU.add))
                flat = [cand[:, h, :, :].rearrange("p a b -> p (a b)") for h in range(PH)]
                best16([(pair_v[:, h, :], pair_i[:, h, :], flat[h], flat[h]) for h in range(PH)], step)
                step(nc.vector.tensor_copy(pick_sum, pair_v[:, :, 0]))
                nc.vector.tensor_tensor(pair_v, pair_v, over(pick_sum, 2, PK), ALU.subtract).then_inc(pair_sub, 1)
                nc.vector.tensor_scalar(part_u[:, 0, :, :], pair_i, 4, None, ALU.logical_shift_right)
                step(nc.vector.tensor_scalar(part_u[:, 1, :, :], pair_i, 15, None, ALU.bitwise_and))
                step(nc.vector.tensor_copy(part_f, part_u))
                dve.wait_ge(parts_read, m + 1)
                dve.sem_inc(held, 1)
                for side in range(2):
                    flat = hits.rearrange("p a b c -> p (a b) c")
                    places = part_f[:, side, :, :].rearrange("p a b -> p (a b)")
                    step(nc.vector.tensor_tensor(flat, over(iota[:, 0:PK], 1, PICKS), over(places, 2, PK), ALU.is_equal))
                    step(nc.vector.tensor_tensor(hits, hits, over(top_f[:, side, :, :], 2, PK), ALU.mult))
                    step(nc.vector.tensor_reduce(part_id[:, side, :, :].rearrange("p a b -> p (a b)"), flat, AX, ALU.add))
                step(nc.vector.scalar_tensor_tensor(part_f[:, 0, :, :], part_id[:, 0, :, :], float(NKEY), part_id[:, 1, :, :],
                                                    ALU.mult, ALU.add))
                nc.vector.tensor_copy(ids[:, bass.ds(m, 1), :].rearrange("p a (b c) -> p (a b) c", c=PK), part_f[:, 0, :, :])
                dve.wait_ge(pair_exp, m + 1)
                step(nc.vector.tensor_reduce(pick_sum, pair_v, AX, ALU.add))
                step(nc.vector.reciprocal(pick_sum, pick_sum))
                nc.vector.tensor_tensor(gates[:, bass.ds(m, 1), :].rearrange("p a (b c) -> p (a b) c", c=PK), pair_v,
                                        over(pick_sum, 2, PK), ALU.mult).then_inc(topk_done, 1)
                dve.wait_ge(topk_done, m + 1)
                dve.sem_inc(sc_used, 1)
                assert step.n == TOP_STEPS, step.n

            def one_hots(m):
                dve.wait_ge(cols_ready, m + 1)
                dve.sem_inc(held, 1)
                with dve.Fori(0, P // (2 * OH)) as i:
                    for buf in range(2):
                        dve.wait_ge(g_ps, m * (P // 4) + i * (2 * OH // 4) + (buf * OH // 4 + OH // 4))
                        dve.sem_inc(held, 1)
                        now = bass.ds(m * P + i * (2 * OH) + buf * OH, OH)
                        nc.vector.tensor_tensor(one_hot[:, buf, :, :, :], over(over(iota[:, :], 1, OH), 1, 2),
                                                over(pick_cols[:, 0:2, now], 3, NKEY), ALU.is_equal).then_inc(hot_ready, 1)

            select(0)
            with dve.Fori(1, TB) as m:
                select(m)
                one_hots(m - 1)
            own.n += TB * TOP_STEPS

            dve.sem_inc(row_used, SLOTS)
            dve.wait_ge(g_ps, DT // 4 + 2 * OH // 4)
            own(nc.vector.memset(out4, 0.0))

            def add_values(g, half, m, units_used):
                dve.wait_ge(unit_used, units_used)
                row = out4[:, m, half * UNIT:(half + 1) * UNIT]
                nc.vector.tensor_tensor(row, row, wide(2 * m, UNIT), ALU.add).then_inc(v_read, 1)

            def dot(g, q):
                dve.wait_ge(ring_full[q], g.val(32, 16))
                nc.vector.tensor_tensor_reduce(out=ring[q], in0=ring[q], in1=h2_now, scale=1.0, scalar=0.0,
                                               op0=ALU.mult, op1=ALU.add, accum_out=act4[:, q:q + 1]).then_inc(row_used, 1)
                if q == SLOTS - 1:
                    dve.wait_ge(row_used, g.val(2 * SLOTS, 2 * SLOTS))
                    dve.sem_inc(dots_done, 1)

            def weigh(g):
                dve.wait_ge(gelu_done, g.val(1))
                dve.wait_ge(row_used, g.val(2 * SLOTS, 0))
                nc.vector.tensor_tensor(w4, act4, gates[:, DB, bass.ds(g.val(SLOTS, -SLOTS), SLOTS)], ALU.mult).then_inc(picks_w, 1)
                dve.wait_ge(picks_w, g.val(1))

            def add_row(g, q):
                dve.wait_ge(ring_full[q], g.val(32))
                dve.wait_ge(row_used, g.val(2 * SLOTS, q))
                nc.vector.scalar_tensor_tensor(acc_v, ring[q], w4[:, q:q + 1], acc_v, ALU.mult, ALU.add).then_inc(row_used, 1)

            PICK_STEPS = {"start": ((), ()), "ahead": ((1, 2, 3, 5), (5, 6, 7, 7)),
                          "full": ((4, 5, 6, 7), (8, 12, 14, 15)), "last": ((1, 2, 3, 5), ())}

            def group(g):
                buf = g.c % 2
                if g.kind == "start":
                    for q in range(SLOTS):
                        dot(g, q)
                for j in g.steps():
                    if g.units:
                        dve.wait_ge(high_done, g.unit(j + 1))
                        nc.vector.tensor_tensor(split[:, j % 2, 1, :], raw[:, j % RAWS, :], split[:, j % 2, 0, :].bitcast(F32), ALU.subtract)\
                            .then_inc(unit_split, 1)
                    for i, due in g.tiles_at(j):
                        if due == "made":
                            if g.kind == "full":
                                dve.wait_ge(tile_gelu, g.val(GT, i + 1 + 2 - AHEAD * GT))
                            else:
                                dve.wait_ge(gel_full[i % 2], g.val(16 * GT // 2, 16 * (i // 2 + 1)))
                            dve.wait_ge(gm_full[buf], g.round(16, 16))
                            act_t = gel[:, i % 2, :].rearrange("p (a b) -> p a b", b=TG)
                            nc.vector.tensor_tensor(act_t, act_t, gm[:, buf, :, i * TG:(i + 1) * TG], ALU.mult).then_inc(w_made, 1)
                        if due == "low":
                            dve.wait_ge(w_high, g.val(GT, i + 1))
                            nc.vector.tensor_tensor(w_parts[:, buf, 1, i, :], gel[:, i % 2, :], w_parts[:, buf, 0, i, :].bitcast(F32), ALU.subtract)\
                                .then_inc(w_ready, 1)
                    if g.kind == "full":
                        if j in (1, 2, 3):
                            add_values(g, 1, j - 1, g.unit(0))
                        if j in (9, 10, 11):
                            add_values(g, 0, j - 9, g.unit(8))
                    elif g.kind != "start":
                        for m in range(DB):
                            if j == 0 and not g.second:
                                add_values(g, 1, m, g.unit(0))
                            if j == 4:
                                add_values(g, 0, m, g.unit(4))
                    sums, dots = PICK_STEPS[g.kind]
                    if sums and j == min(2, sums[0]):
                        weigh(g)
                    for q in range(SLOTS):
                        if sums and sums[q] == j:
                            add_row(g, q)
                    for q in range(SLOTS):
                        if dots and dots[q] == j:
                            dot(g, q)
                if g.kind == "last":
                    for m in range(DB):
                        add_values(g, 1, m, g.unit(8))

            stream(dve, group)

            dve.wait_ge(row_used, (2 * GROUPS + 1) * SLOTS)
            dve.wait_ge(v_read, 2 * GROUPS * DB)
            dve.wait_ge(tail_loaded, 3 * 16)
            dve.wait_ge(tail_row_ready, 2)
            start3 = own.n
            with dve.Fori(0, TB) as m:
                step = Steps(dve, dve_own, m * 8 + start3, held)
                row = out4[:, bass.ds(m, 1), :].rearrange("p a b -> p (a b)")
                step(nc.vector.tensor_tensor(row, row, g2b, ALU.mult))
                step(nc.vector.scalar_tensor_tensor(row, x1_back[:, bass.ds(m, 1), :].rearrange("p a b -> p (a b)"), ALPHA, row,
                                                    ALU.mult, ALU.add))
                normalise(m + 2 * TB, row, step).then_inc(y_normed, 1)
                dve.wait_ge(y_normed, m + 1)
                dve.sem_inc(held, 1)
                assert step.n == 8, step.n

        @block.tensor
        def _(pe):
            def mod_sums(m):
                pe.wait_ge(ada_used, (m + 1) * KT)
                for k in range(KT):
                    ins = nc.tensor.matmul(ps[:, 4, k:k + 1], acc[:, k * P:(k + 1) * P], ones[:, 0:1], start=True, stop=True)
                ins.then_inc(mod_sum, 1)

            def slice_of(s, cols, channels):
                for k in range(KT):
                    pe.wait_ge(win_split, s * KT + (k + 1))
                    pe.wait_ge(h_split, k + 1)
                    for m in range(4):
                        if k == 0:
                            pe.wait_ge(proj_bank_free, s * 4 + (m + 1))
                        tile = slice(m * P, (m + 1) * P)
                        for n, (wp, hp) in enumerate(((0, 0), (0, 1), (1, 0))):
                            if channels:
                                lhs, rhs = win_parts[:, k % 2, wp, tile], h_parts[:, hp, k, :]
                            else:
                                lhs, rhs = h_parts[:, hp, k, tile], win_parts[:, k % 2, wp, 0:cols]
                            ins = nc.tensor.matmul(ps[:, m, 0:cols], lhs, rhs, start=k == 0 and n == 0, stop=k == KT - 1 and n == 2)
                        if k == KT - 1:
                            ins.then_inc(proj_done, 1)
                    if k < KT - 1:
                        ins.then_inc(win_used, 1)

            pe.wait_ge(consts2, 6)
            for m in range(2):
                mod_sums(m)
            with pe.Fori(0, 2) as s:
                slice_of(s, 512, True)
            mod_sums(2)
            slice_of(2, 512, True)
            slice_of(3, KVW + HEADS, False)
            mod_sums(3)
            slice_of(4, 512, False)
            slice_of(5, 512, False)
            mod_sums(4)
            slice_of(6, 512, False)
            slice_of(7, 512, False)
            mod_sums(5)

            def turn(dst, src):
                return nc.tensor.transpose(dst, src, ident[:, :])

            def logits(b, u):
                if u:
                    pe.wait_ge(lg_read, b * 4 + u)
                for pair in range(2):
                    for par in range(2):
                        rows = slice(64 * par, 64 * par + 64)
                        ins = nc.tensor.matmul(ps[:, par, pair * 256:pair * 256 + 256], q_t[rows, 2 * u + pair, :],
                                               k_t[rows, u // 2, :], start=True, stop=True)
                ins.then_inc(lg_done, 1)

            def turn_p(b, u):
                pe.wait_ge(exp_done, b * 4 + (u + 1))
                if u:
                    pe.wait_ge(pt_ready, b * 4 + u)
                for j in range(8):
                    ins = turn(wide(2, 8, P)[:, j, :], lg[:, u % 2, j // 4, j // 2 % 2, (j % 2) * P:(j % 2 + 1) * P])
                ins.then_inc(pt_ps, 1)

            def values(b, u):
                pe.wait_ge(pt_ready, b * 4 + (u + 1))
                if u % 2:
                    pe.wait_ge(att_out, b * 4 + u)
                for pair in range(2):
                    for par in range(2):
                        h = 4 * u + 2 * pair + par
                        for half in range(2):
                            ins = nc.tensor.matmul(ps[:, 4 + h // GH, (h % GH) * HD:(h % GH + 1) * HD],
                                                   p_t[:, u % 2, (par * 2 + pair) * 2 + half, :],
                                                   vv[:, half, (h // GH) * HD:(h // GH + 1) * HD], start=half == 0, stop=half == 1)
                ins.then_inc(pv_done, 1)

            def segments(b, c):
                if c >= 2:
                    pe.wait_ge(seg_read, b * 4 + (c - 1))
                for i in range(4):
                    h = 4 * c + i
                    ins = nc.tensor.matmul(ps[:, c % 2, i * P:(i + 1) * P], da_now[:, h:h + 1].to_broadcast([P, P]), tri[:, :],
                                           start=True, stop=True)
                ins.then_inc(seg_ps, 1)

            def within(b, c):
                pe.wait_ge(m_ready, b * 4 + (c + 1))
                for i in range(4):
                    h = 4 * c + i
                    ins = nc.tensor.matmul(ps[:, 6 + h // GH, (h % GH) * HD:(h % GH + 1) * HD], m_t[:, h, :], xdt[:, h, :],
                                           start=True, stop=True)
                return ins

            with pe.Fori(0, TB) as b:
                pe.wait_ge(block_in, b + 1)
                for i in range(HEADS // 2):
                    ins = turn(wide(2, 8, P)[:, i, :], qk[:, 2 * i:2 * i + 2, :].rearrange("p a b -> p (a b)"))
                ins.then_inc(qt_ps, 1)
                for g in range(KV):
                    turn(ps[:, 6, g * P:(g + 1) * P], kdup[:, g, :, :].rearrange("p a b -> p (a b)"))
                for g in range(KV):
                    ins = turn(ps[:, 6, (2 + g) * P:(3 + g) * P], cur[:, 8 + g, :])
                ins.then_inc(kb_ps, 1)
                nc.tensor.matmul(ps[:, 7, 0:HEADS], tri[:, :], da_now, start=True, stop=True)
                nc.tensor.matmul(ps[:, 7, HEADS:2 * HEADS], ones[:, :], da_now, start=True, stop=True)
                for g in range(KV):
                    ins = nc.tensor.matmul(ps[:, 7, (1 + g) * P:(2 + g) * P], cur[:, 8 + g, :], cur[:, 10 + g, :], start=True, stop=True)
                ins.then_inc(cb_ps, 1)
                for i in range(8):
                    ins = turn(wide(4, 8, P)[:, i, :], cur[:, i, :])
                ins.then_inc(xs_ps, 1)
                pe.wait_ge(q_ready, b + 1)
                pe.wait_ge(kv_ready, b + 1)
                logits(b, 0)
                logits(b, 1)
                turn_p(b, 0)
                logits(b, 2)
                pe.wait_ge(xs_ready, b + 1)
                values(b, 0)
                turn_p(b, 1)
                logits(b, 3)
                values(b, 1)
                turn_p(b, 2)
                pe.wait_ge(lg_read, b * 4 + 4)
                segments(b, 0)
                segments(b, 1)
                values(b, 2)
                turn_p(b, 3)
                values(b, 3)
                within(b, 0)
                segments(b, 2)
                within(b, 1)
                segments(b, 3)
                pe.wait_ge(xw_ready, b + 1)
                pe.wait_ge(att_out, b * 4 + 4)
                for g in range(KV):
                    nc.tensor.matmul(ps[:, 4 + g, :], cur[:, 10 + g, :], state[:, g * GH:(g + 1) * GH, :].rearrange("p a b -> p (a b)"),
                                     start=True, stop=True)
                for g in range(KV):
                    ins = nc.tensor.matmul(ps[:, 2 + g, :], b_row[:, g, :], xw[:, g * GH:(g + 1) * GH, :].rearrange("p a b -> p (a b)"),
                                           start=True, stop=True)
                ins.then_inc(st_ps, 1)
                within(b, 2)
                within(b, 3).then_inc(y_ps, 1)
                pe.wait_ge(seg_read, b * 4 + 4)
                for i in range(8):
                    ins = turn(wide(0, 8, P)[:, i, :], y_row[:, i * P:(i + 1) * P])
                ins.then_inc(yt_ps, 1)
                pe.wait_ge(y_rows, b + 1)
                for i in range(8):
                    ins = turn(wide(2, 8, P)[:, i, :], y_row[:, (8 + i) * P:(9 + i) * P])
                ins.then_inc(yt_ps, 1)
                pe.wait_ge(yt_act, b + 1)

            pe.wait_ge(yt_dve, TB)
            pe.wait_ge(mod_ready, MODS)
            for i, m in enumerate((2, 4, 3)):
                if i >= 2:
                    pe.wait_ge(row_ready, i - 1)
                for k in range(KT):
                    ins = nc.tensor.matmul(ps[:, 4 * (i % 2) + k // 4, (k % 4) * P:(k % 4 + 1) * P],
                                           mod_cols[:, m * KT + k:m * KT + k + 1].to_broadcast([P, P]), ident[:, :], start=True, stop=True)
                ins.then_inc(row_ps, 1)

            pe.wait_ge(row_ready, 3)
            pe.wait_ge(y_split, 2)
            with pe.Fori(0, 2) as n:
                for k in range(KT):
                    pe.wait_ge(wout_split, n * KT + (k + 1))
                    for m in range(TB):
                        if k == 0:
                            pe.wait_ge(mix_read, n * 4 + (m + 1))
                        for q, (y_part, wp) in enumerate(((y_high, 0), (y_high, 1), (y_low, 0))):
                            for j in range(2):
                                ins = nc.tensor.matmul(ps[:, 2 * m + j, :], y_part[:, k, m * P:(m + 1) * P], wout_parts[:, k % 2, wp, j * 512:(j + 1) * 512],
                                                       start=k == 0 and q == 0, stop=k == KT - 1 and q == 2)
                        if k == KT - 1:
                            ins.then_inc(mix_ps, 1)
                        elif m == TB - 1:
                            ins.then_inc(wout_used, 1)
                pe.wait_ge(mix_ps, n * 4 + 4)
                pe.sem_inc(wout_used, 1)

            for m in range(TB):
                pe.wait_ge(h2_ready, m + 1)
                if m >= 2:
                    pe.wait_ge(h2t_ready, m - 1)
                for k in range(KT):
                    ins = turn(wide(4 * (m % 2), KT, P)[:, k, :], h2[:, m, k * P:(k + 1) * P])
                ins.then_inc(h2t_ps, 1)
            pe.wait_ge(h2t_ready, TB)
            for k in range(KT):
                pe.wait_ge(wt_full[k % 4], 128 + 16 * (k // 4 + 1))
                for h in range(PH):
                    ins = nc.tensor.matmul(bank(h), wt[:, k % 4, h * P:(h + 1) * P], h2_t[:, k, :], start=k == 0, stop=k == KT - 1)
                    if k == KT - 1:
                        ins.then_inc(q_ps, 1)
                if k < KT - 1:
                    ins.then_inc(wt_used, 1)
            pe.wait_ge(key_loaded, 16)
            pe.wait_ge(q8_ready, PH)

            def scores(m):
                if m:
                    pe.wait_ge(sc_ready, m)
                for h in range(PH):
                    for side in range(2):
                        rows = slice(64 * side, 64 * side + 64)
                        ins = nc.tensor.matmul(wide(0, 2, PH, NKEY)[:, side, h, :], q8[rows, h, m * P:(m + 1) * P],
                                               key_t[rows, :], start=True, stop=True)
                ins.then_inc(sc_ps, 1)

            def ahead(m):
                with pe.Fori(0, WIN_PAIRS) as n:
                    for j in range(4):
                        b, half = j // 2, j % 2
                        pe.wait_ge(pre_split, n * 4 + (m * WIN_UNITS + j + 1 + RAWS))
                        if half == 0:
                            pe.wait_ge(pre_gelu, n * 2 + (m * 2 * WIN_PAIRS + b + 1))
                        unit(j, b, half).then_inc(pre_used, 1)

            def unit(j, b, half):
                high, low = split[:, j % 2, 0, :], split[:, j % 2, 1, :]
                for kk in range(8):
                    k = half * 8 + kk
                    cols = slice(kk * P, (kk + 1) * P)
                    for n, (lhs, rhs) in enumerate(((high, 0), (high, 1), (low, 0))):
                        ins = nc.tensor.matmul(ps[:, 6 + b, 0:DT], lhs[:, cols], h2_parts[:, rhs, k, :],
                                               start=k == 0 and n == 0, stop=k == KT - 1 and n == 2)
                return ins

            def turned(m):
                pe.wait_ge(topk_done, m + 1)
                pe.wait_ge(pre_gelu, (m + 1) * 2 * WIN_PAIRS + 2)
                for i, what in enumerate((part_id[:, 0, :, :], part_id[:, 1, :, :], gates[:, m, :].rearrange("p (a b) -> p a b", b=PK))):
                    ins = turn(ps[:, 6, i * P:(i + 1) * P], what.rearrange("p a b -> p (a b)"))
                ins.then_inc(cols_ps, 1)
                pe.wait_ge(cols_ps, m + 1)
                pe.sem_inc(parts_read, 1)

            def gates_by_expert(m):
                with pe.Fori(0, P // (2 * OH)) as i:
                    for buf in range(2):
                        pe.wait_ge(hot_gated, i * 2 + (m * (P // OH) + buf + 1))
                        for quad in range(OH // 4):
                            pe.wait_ge(g_staged, i * (2 * OH // 4) + ((m * P + buf * OH) // 4 + quad + 1))
                            for t in range(4 * quad, 4 * quad + 4):
                                ins = nc.tensor.matmul(ps[:, 4 + quad, (t % 4) * P:(t % 4 + 1) * P], one_hot[:, buf, 0, t, :], one_hot[:, buf, 1, t, :],
                                                       start=True, stop=True)
                            ins.then_inc(g_ps, 1)

            pe.sem_inc(g_staged, 2)
            pe.sem_inc(pre_gelu, 2)
            scores(0)
            scores(1)
            pe.wait_ge(h2_split, 1)
            for m in range(TB):
                if m:
                    pe.wait_ge(cols_ready, m)
                ahead(m)
                if m < DB:
                    turned(m)
                if m + 2 < TB:
                    scores(m + 2)
                if m:
                    gates_by_expert(m - 1)

            def second_gate(half):
                for k in range(8):
                    c = 5 * KT + half * 8 + k
                    ins = nc.tensor.matmul(wide(6, 8, P)[:, k, :], mod_cols[:, c:c + 1].to_broadcast([P, P]), ident[:, :], start=True, stop=True)
                ins.then_inc(tail_row, 1)

            def group(g):
                buf = (g.c - 1) % 2
                if g.kind == "last":
                    pe.wait_ge(tile_gelu, (GROUPS - AHEAD) * GT + 2)
                    second_gate(0)
                for j, (table, i, half) in enumerate(g.units):
                    pe.wait_ge(unit_split, g.unit(j + 1))
                    if table == "u":
                        if half == 0:
                            pe.wait_ge(tile_gelu, g.val(GT, i + 1 - AHEAD * GT))
                        ins = unit(j, i % 2, half)
                    else:
                        high, low = split[:, j % 2, 0, :], split[:, j % 2, 1, :]
                        pe.wait_ge(w_ready, g.val(GT, i + 1 - GT))
                        for m in range(DB):
                            if i == 0 and not (g.second and half == 0):
                                pe.wait_ge(v_read, g.val(2 * DB, (half - 2) * DB + m - DB + 1))
                            for n, (lhs, rhs) in enumerate(((0, high), (0, low), (1, high))):
                                for b in range(2):
                                    ins = nc.tensor.matmul(ps[:, 2 * m + b, :], w_parts[:, buf, lhs, i, m * P:(m + 1) * P], rhs[:, b * 512:(b + 1) * 512],
                                                           start=i == 0 and n == 0, stop=i == GT - 1 and n == 2)
                    ins.then_inc(unit_used, 1)

            pe.wait_ge(pre_gelu, AHEAD * GT + 2)
            pe.wait_ge(cols_ready, DB)
            pe.wait_ge(g_staged, DT // 4 + 2)
            pe.sem_inc(tile_gelu, 2)
            stream(pe, group)
            pe.wait_ge(tail_row_ready, 1)
            second_gate(1)


def kernel(**inputs):
    import numpy as np
    import concourse.bacc as bacc
    from concourse.bass_utils import run_bass_kernel_spmd as run

    a = {n: np.asarray(v) for n, v in inputs.items()}
    x = a["x"][0]
    w_in = a["w_in"][0].reshape(KT, P, -1).transpose(1, 0, 2)
    z0 = AW + KVW
    xbc0 = z0 + AW
    dt0 = xbc0 + XT * P
    kvdt = np.concatenate([w_in[:, :, AW:z0], w_in[:, :, dt0:]], axis=2)
    slices = [w_in[:, :, xbc0 + i * 512:xbc0 + (i + 1) * 512] for i in range(XT // 4)]
    slices.append(np.pad(kvdt, ((0, 0), (0, 0), (0, 512 - KVW - HEADS))))
    slices += [w_in[:, :, c:c + 512] for c in (0, 512, z0, z0 + 512)]
    laid = {
        "x_rows": x,
        "x_cols": x.T.reshape(KT, P, S).transpose(1, 0, 2),
        "c_cols": a["c"][0].reshape(KT, P).T,
        "pos_cols": a["positions"][0].reshape(TB, P).T,
        "w_ada": a["w_ada"][0],
        "b_ada_cols": a["b_ada"][0].reshape(MODS * KT, P).T,
        "w_slices": np.stack(slices, axis=2).reshape(P, KT // 2, 2, SLICES, 512).transpose(3, 1, 0, 2, 4).reshape(-1, P, 2, 512),
        "conv_w": a["conv_w"][0].reshape(CONV, XT, P).transpose(2, 1, 0).reshape(P, XT * CONV),
        "conv_b": a["conv_b"][0].reshape(XT, P).T,
        "dt_bias": a["dt_bias"],
        "a_log": a["a_log"],
        "d_skip": a["d_skip"],
        "norm_w": a["ssd_norm_w"][0].reshape(AW // P, P).T,
        "sinks": a["attn_sinks"],
        "w_out": a["w_out"][0].reshape(KT, P, 2, D // 2).transpose(2, 0, 1, 3).reshape(2 * KT, P, D // 2),
        "ln1_g": a["ln1_g"],
        "ln1_b": a["ln1_b"],
        "w_q": a["peer_wq"][0].reshape(KT, P, PH * P),
        "keys": np.concatenate([a["peer_k1"][0].T, a["peer_k2"][0].T]),
        "u_units": a["peer_u"][0].reshape(NKEY, NKEY, 2, 8, P).transpose(1, 2, 4, 3, 0).reshape(2 * NKEY, P, UNIT),
        "u_tab": a["peer_u"][0],
        "v_tab": a["peer_v"][0],
        "ln2_g": a["ln2_g"],
        "ln2_b": a["ln2_b"],
    }
    nc = bacc.Bacc("TRN2", target_bir_lowering=False, num_devices=1)
    arrays, args = {}, []
    for name, value in laid.items():
        value = np.ascontiguousarray(value)
        arrays[f"in_{name}"] = value
        args.append(nc.dram_tensor(f"in_{name}", value.shape, mybir.dt.from_np(value.dtype), kind="ExternalInput").ap())
    args.append(nc.dram_tensor("out_rows", (S, D), F32, kind="ExternalOutput").ap())
    decoder_layer(nc, *args)
    result = run(nc, [arrays], core_ids=[0])
    return result.results[0]["out_rows"].reshape(1, S, D)
```
